# Optimizing a Trainium2 kernel written in Bass

```python
import math
import jax, jax.numpy as jnp
from jax import lax
import numpy as np
import jax
import jax.numpy as jnp

D_MODEL = 1024
BATCH = 1
SEQ = 512
DEPTH = 2

ROPE_THETA = 10000.0
QBLOCK = 128
NORM_EPS = 1e-6
NEG_INF = -1e30

MLA_HEADS = 8
MLA_Q_LORA = 384
MLA_KV_LORA = 256
MLA_NOPE = 64
MLA_ROPE = 32
MLA_V = 64
SWA_HEADS = 8
SWA_KV_HEADS = 2
SWA_HD = 64
SWA_WINDOW = 128
DIFF_HEADS = 4
DIFF_HD = 64
FOX_HEADS = 8
FOX_HD = 64
FORGET_BIAS_MEAN = 3.0

EVEN_WIDTH = MLA_HEADS * MLA_V + SWA_HEADS * SWA_HD
ODD_WIDTH = DIFF_HEADS * 2 * DIFF_HD + FOX_HEADS * FOX_HD
EVEN_SPLITS = [MLA_Q_LORA, MLA_KV_LORA, MLA_ROPE, SWA_HEADS * SWA_HD,
               SWA_KV_HEADS * SWA_HD, SWA_KV_HEADS * SWA_HD, EVEN_WIDTH]
ODD_SPLITS = [DIFF_HEADS * 2 * DIFF_HD, DIFF_HEADS * 2 * DIFF_HD, DIFF_HEADS * 2 * DIFF_HD,
              FOX_HEADS * FOX_HD, FOX_HEADS * FOX_HD, FOX_HEADS * FOX_HD, FOX_HEADS, ODD_WIDTH]
EVEN_IN = sum(EVEN_SPLITS)
ODD_IN = sum(ODD_SPLITS)


def rmsnorm(x, g):
    xf = x.astype(jnp.float32)
    y = xf * lax.rsqrt(jnp.mean(xf * xf, axis=-1, keepdims=True) + NORM_EPS)
    return (y * g.astype(jnp.float32)).astype(x.dtype)

def split_cols(z, sizes):
    offs = [int(o) for o in np.cumsum(sizes)[:-1]]
    return jnp.split(z, offs, axis=-1)

def rope_tables(seq, dim):
    inv = 1.0 / (ROPE_THETA ** (jnp.arange(0, dim, 2, dtype=jnp.float32) / dim))
    ang = jnp.arange(seq, dtype=jnp.float32)[:, None] * inv[None, :]
    return jnp.cos(ang), jnp.sin(ang)

def apply_rope(x, cos, sin):
    half = x.shape[-1] // 2
    x1, x2 = x[..., :half], x[..., half:]
    c = cos[None, :, None, :].astype(x.dtype)
    s = sin[None, :, None, :].astype(x.dtype)
    return jnp.concatenate([x1 * c - x2 * s, x2 * c + x1 * s], axis=-1)

def causal_block_mask(blk, seq):
    t = blk * QBLOCK + jnp.arange(QBLOCK)
    return jnp.arange(seq)[None, :] <= t[:, None]

def sweep_query_blocks(block_fn, q_arrays):
    b, s = q_arrays[0].shape[0], q_arrays[0].shape[1]
    nblk = s // QBLOCK

    def to_blocks(a):
        return jnp.moveaxis(a.reshape(b, nblk, QBLOCK, *a.shape[2:]), 1, 0)

    xs = (jnp.arange(nblk), tuple(to_blocks(a) for a in q_arrays))
    out = lax.map(lambda args: block_fn(args[0], *args[1]), xs)
    out = jnp.moveaxis(out, 0, 1)
    return out.reshape(b, s, *out.shape[3:])

def mla_attention(q_nope, q_rope, k_nope, k_rope, v):
    seq = k_nope.shape[1]
    scale = (MLA_NOPE + MLA_ROPE) ** -0.5

    def block(blk, qn, qr):
        s = jnp.einsum('bqhd,bkhd->bhqk', qn, k_nope) + jnp.einsum('bqhr,bkr->bhqk', qr, k_rope)
        s = jnp.where(causal_block_mask(blk, seq), s.astype(jnp.float32) * scale, NEG_INF)
        p = jax.nn.softmax(s, axis=-1).astype(v.dtype)
        return jnp.einsum('bhqk,bkhd->bqhd', p, v)

    return sweep_query_blocks(block, (q_nope, q_rope))

def swa_sink_attention(q, k, v, sinks):
    b, s, h, d = q.shape
    kvh = k.shape[2]
    g = h // kvh
    w = SWA_WINDOW
    n = s // w
    qb = q.reshape(b, n, w, kvh, g, d)

    def band(a):
        ap = jnp.pad(a, ((0, 0), (w, 0), (0, 0), (0, 0))).reshape(b, n + 1, w, kvh, d)
        return jnp.concatenate([ap[:, :-1], ap[:, 1:]], axis=2)

    kb, vb = band(k), band(v)
    sc = jnp.einsum('bnqkgd,bnjkd->bnkgqj', qb, kb).astype(jnp.float32) * (d ** -0.5)
    qpos = (jnp.arange(n) * w)[:, None, None] + jnp.arange(w)[None, :, None]
    kpos = (jnp.arange(n) * w - w)[:, None, None] + jnp.arange(2 * w)[None, None, :]
    mask = (kpos <= qpos) & (qpos - kpos < w) & (kpos >= 0)
    sc = jnp.where(mask[None, :, None, None], sc, NEG_INF)
    sink = jnp.broadcast_to(sinks.astype(jnp.float32).reshape(1, 1, kvh, g, 1, 1), sc.shape[:-1] + (1,))
    p = jax.nn.softmax(jnp.concatenate([sc, sink], axis=-1), axis=-1)[..., :-1].astype(v.dtype)
    o = jnp.einsum('bnkgqj,bnjkd->bnqkgd', p, vb)
    return o.reshape(b, s, h, d)

def diff_attention(q1, q2, k1, k2, v, lam):
    seq = k1.shape[1]
    scale = DIFF_HD ** -0.5

    def block(blk, a, c):
        mask = causal_block_mask(blk, seq)
        s1 = jnp.where(mask, jnp.einsum('bqhd,bkhd->bhqk', a, k1).astype(jnp.float32) * scale, NEG_INF)
        s2 = jnp.where(mask, jnp.einsum('bqhd,bkhd->bhqk', c, k2).astype(jnp.float32) * scale, NEG_INF)
        p = (jax.nn.softmax(s1, axis=-1) - lam * jax.nn.softmax(s2, axis=-1)).astype(v.dtype)
        return jnp.einsum('bhqk,bkhe->bqhe', p, v)

    return sweep_query_blocks(block, (q1, q2))

def forgetting_attention(q, k, v, fcum):
    seq = k.shape[1]
    scale = FOX_HD ** -0.5
    f_key = jnp.transpose(fcum, (0, 2, 1))

    def block(blk, qb, fq):
        s = jnp.einsum('bqhd,bkhd->bhqk', qb, k).astype(jnp.float32) * scale
        s = s + jnp.transpose(fq, (0, 2, 1))[..., None] - f_key[:, :, None, :]
        s = jnp.where(causal_block_mask(blk, seq), s, NEG_INF)
        p = jax.nn.softmax(s, axis=-1).astype(v.dtype)
        return jnp.einsum('bhqk,bkhd->bqhd', p, v)

    return sweep_query_blocks(block, (q, fcum))

def even_mixer(h, w_in, q_norm, kv_norm, w_uq, w_ukv, sinks, w_out, rope_lat, rope_head):
    b, s, _ = h.shape
    z = h @ w_in
    z_cq, z_ckv, z_kr, z_sq, z_sk, z_sv, z_gate = split_cols(z, EVEN_SPLITS)
    cos_r, sin_r = rope_lat
    cos_h, sin_h = rope_head
    q = (rmsnorm(z_cq, q_norm) @ w_uq).reshape(b, s, MLA_HEADS, MLA_NOPE + MLA_ROPE)
    q_nope = q[..., :MLA_NOPE]
    q_rope = apply_rope(q[..., MLA_NOPE:], cos_r, sin_r)
    kv = (rmsnorm(z_ckv, kv_norm) @ w_ukv).reshape(b, s, MLA_HEADS, MLA_NOPE + MLA_V)
    k_nope = kv[..., :MLA_NOPE]
    v_mla = kv[..., MLA_NOPE:]
    k_rope = apply_rope(z_kr[:, :, None, :], cos_r, sin_r)[:, :, 0, :]
    o_mla = mla_attention(q_nope, q_rope, k_nope, k_rope, v_mla).reshape(b, s, MLA_HEADS * MLA_V)
    q_s = apply_rope(z_sq.reshape(b, s, SWA_HEADS, SWA_HD), cos_h, sin_h)
    k_s = apply_rope(z_sk.reshape(b, s, SWA_KV_HEADS, SWA_HD), cos_h, sin_h)
    v_s = z_sv.reshape(b, s, SWA_KV_HEADS, SWA_HD)
    o_swa = swa_sink_attention(q_s, k_s, v_s, sinks).reshape(b, s, SWA_HEADS * SWA_HD)
    o = jnp.concatenate([o_mla, o_swa], axis=-1) * jax.nn.silu(z_gate)
    return o @ w_out

def odd_mixer(h, w_in, forget_bias, lam_p, subln, w_out, rope_head, layer):
    b, s, _ = h.shape
    z = h @ w_in
    z_dq, z_dk, z_dv, z_fq, z_fk, z_fv, z_ff, z_gate = split_cols(z, ODD_SPLITS)
    cos_h, sin_h = rope_head
    q = apply_rope(z_dq.reshape(b, s, 2 * DIFF_HEADS, DIFF_HD), cos_h, sin_h).reshape(b, s, DIFF_HEADS, 2, DIFF_HD)
    k = apply_rope(z_dk.reshape(b, s, 2 * DIFF_HEADS, DIFF_HD), cos_h, sin_h).reshape(b, s, DIFF_HEADS, 2, DIFF_HD)
    v_d = z_dv.reshape(b, s, DIFF_HEADS, 2 * DIFF_HD)
    lam_init = 0.8 - 0.6 * math.exp(-0.3 * layer)
    lp = lam_p.astype(jnp.float32)
    lam = jnp.exp(jnp.sum(lp[0] * lp[1])) - jnp.exp(jnp.sum(lp[2] * lp[3])) + lam_init
    o_d = diff_attention(q[:, :, :, 0], q[:, :, :, 1], k[:, :, :, 0], k[:, :, :, 1], v_d, lam)
    o_d = (rmsnorm(o_d, subln) * (1.0 - lam_init)).reshape(b, s, DIFF_HEADS * 2 * DIFF_HD)
    fq = z_fq.reshape(b, s, FOX_HEADS, FOX_HD)
    fk = z_fk.reshape(b, s, FOX_HEADS, FOX_HD)
    fv = z_fv.reshape(b, s, FOX_HEADS, FOX_HD)
    logf = jax.nn.log_sigmoid(z_ff.astype(jnp.float32) + forget_bias.astype(jnp.float32))
    fcum = jnp.cumsum(logf, axis=1)
    o_f = forgetting_attention(fq, fk, fv, fcum).reshape(b, s, FOX_HEADS * FOX_HD)
    o = jnp.concatenate([o_d, o_f], axis=-1) * jax.nn.silu(z_gate)
    return o @ w_out

def first_inputs(seed: int = 0) -> dict:
    key = jax.random.key(seed)
    ks = jax.random.split(key, 20)
    n_even = (DEPTH + 1) // 2
    n_odd = DEPTH // 2

    def nrm(k, shape, std):
        return std * jax.random.normal(k, shape, jnp.float32)

    return {
        'x': nrm(ks[0], (BATCH, SEQ, D_MODEL), 1.0),
        'c': nrm(ks[1], (BATCH, D_MODEL), 1.0),
        'w_ada': nrm(ks[2], (DEPTH, D_MODEL, 3 * D_MODEL), 0.5 * D_MODEL ** -0.5),
        'b_ada': nrm(ks[3], (DEPTH, 3 * D_MODEL), 0.01),
        'g_pre': 1.0 + nrm(ks[4], (DEPTH, D_MODEL), 0.02),
        'g_post': 1.0 + nrm(ks[5], (DEPTH, D_MODEL), 0.02),
        'ev_w_in': nrm(ks[6], (n_even, D_MODEL, EVEN_IN), D_MODEL ** -0.5),
        'ev_q_norm': 1.0 + nrm(ks[7], (n_even, MLA_Q_LORA), 0.02),
        'ev_kv_norm': 1.0 + nrm(ks[8], (n_even, MLA_KV_LORA), 0.02),
        'ev_w_uq': nrm(ks[9], (n_even, MLA_Q_LORA, MLA_HEADS * (MLA_NOPE + MLA_ROPE)), MLA_Q_LORA ** -0.5),
        'ev_w_ukv': nrm(ks[10], (n_even, MLA_KV_LORA, MLA_HEADS * (MLA_NOPE + MLA_V)), MLA_KV_LORA ** -0.5),
        'ev_sinks': nrm(ks[11], (n_even, SWA_HEADS), 0.5),
        'ev_w_out': nrm(ks[12], (n_even, EVEN_WIDTH, D_MODEL), EVEN_WIDTH ** -0.5),
        'od_w_in': nrm(ks[13], (n_odd, D_MODEL, ODD_IN), D_MODEL ** -0.5),
        'od_forget_bias': FORGET_BIAS_MEAN + nrm(ks[14], (n_odd, FOX_HEADS), 0.5),
        'od_lambda': nrm(ks[15], (n_odd, 4, DIFF_HD), 0.1),
        'od_subln': 1.0 + nrm(ks[16], (n_odd, 2 * DIFF_HD), 0.02),
        'od_w_out': nrm(ks[17], (n_odd, ODD_WIDTH, D_MODEL), ODD_WIDTH ** -0.5),
    }

def first_block(x, c, w_ada, b_ada, g_pre, g_post, ev_w_in, ev_q_norm, ev_kv_norm, ev_w_uq, ev_w_ukv,
              ev_sinks, ev_w_out, od_w_in, od_forget_bias, od_lambda, od_subln, od_w_out):
    seq = x.shape[1]
    rope_head = rope_tables(seq, SWA_HD)
    rope_lat = rope_tables(seq, MLA_ROPE)
    cond = jax.nn.silu(c)
    for layer in range(DEPTH):
        mod = cond @ w_ada[layer] + b_ada[layer]
        shift, scale, gate = jnp.split(mod, 3, axis=-1)
        h = rmsnorm(x, g_pre[layer]) * (1.0 + scale[:, None, :]) + shift[:, None, :]
        i = layer // 2
        if layer % 2 == 0:
            y = even_mixer(h, ev_w_in[i], ev_q_norm[i], ev_kv_norm[i], ev_w_uq[i], ev_w_ukv[i],
                           ev_sinks[i], ev_w_out[i], rope_lat, rope_head)
        else:
            y = odd_mixer(h, od_w_in[i], od_forget_bias[i], od_lambda[i], od_subln[i], od_w_out[i],
                          rope_head, layer)
        x = x + gate[:, None, :] * rmsnorm(y, g_post[layer])
    return x


DEPTH_2 = 1

HEAD_DIM = D_MODEL // 16
NSA_HEADS = 6
NSA_KV_GROUPS = 2
NSA_HPG = NSA_HEADS // NSA_KV_GROUPS
CMP_BLOCK = 32
CMP_STRIDE = 16
CMP_HIDDEN = 2 * HEAD_DIM
SLC_BLOCK = 64
SLC_TOPN = 16
WINDOW = 512
NSA_QBLOCK = 64
FORCE_BONUS = 1000.0
NEG_BIG = -1e30
LB_FLOOR = 1e-30
SB_HEADS = 4
SB_QBLOCK = 128
HG_HEADS = 6
HG_KDIM = HEAD_DIM
HG_VDIM = HEAD_DIM
HG_CHUNK = 64
NUM_BUCKETS = 32
MAX_DISTANCE = 128
D_NSA = NSA_HEADS * HEAD_DIM
D_KV = NSA_KV_GROUPS * HEAD_DIM
D_SB = SB_HEADS * HEAD_DIM
D_HG = HG_HEADS * HG_VDIM
D_MIX = D_NSA + D_SB + D_HG
N_GATES = NSA_HEADS * 3
SPLIT_SIZES = (D_NSA, D_KV, D_KV, D_KV, D_KV, D_KV, D_KV, N_GATES, D_NSA,
               D_SB, D_SB, D_SB, D_SB,
               HG_HEADS * HG_KDIM, HG_HEADS * HG_KDIM, D_HG, D_HG)
D_IN = sum(SPLIT_SIZES)
ALPHA = (2 * DEPTH_2) ** 0.25
OUT_INIT_SCALE = (8 * DEPTH_2) ** -0.25
LN_EPS = 1e-5
RMS_EPS = 1e-6


def t5_bucket(rel):
    n = jnp.maximum(rel, 0)
    max_exact = NUM_BUCKETS // 2
    large = max_exact + (jnp.log(jnp.maximum(n, 1).astype(jnp.float32) / max_exact)
                         / math.log(MAX_DISTANCE / max_exact)
                         * (NUM_BUCKETS - max_exact)).astype(jnp.int32)
    large = jnp.clip(large, 0, NUM_BUCKETS - 1)
    return jnp.where(n < max_exact, n, large)

def masked_softmax(s, mask):
    s = jnp.where(mask, s.astype(jnp.float32), NEG_BIG)
    p = jax.nn.softmax(s, axis=-1)
    return jnp.where(mask, p, 0.0)

def layer_norm(v, g, b):
    v32 = v.astype(jnp.float32)
    mu = jnp.mean(v32, axis=-1, keepdims=True)
    var = jnp.mean(jnp.square(v32 - mu), axis=-1, keepdims=True)
    return ((v32 - mu) * lax.rsqrt(var + LN_EPS) * g + b).astype(v.dtype)

def nsa_mixer(q, kc_src, vc_src, ks_src, vs_src, kw_src, vw_src, gate_logits,
              cmp_pos, w_ck1, w_ck2, w_cv1, w_cv2, rel_bias):
    B, S = q.shape[:2]
    G, HPG, dk, QB = NSA_KV_GROUPS, NSA_HPG, HEAD_DIM, NSA_QBLOCK
    scale = 1.0 / math.sqrt(dk)
    q = q.reshape(B, S, G, HPG, dk).transpose(0, 2, 3, 1, 4)
    gates = jax.nn.sigmoid(gate_logits.reshape(B, S, G, HPG, 3).transpose(0, 2, 3, 1, 4))

    n_cmp = (S - CMP_BLOCK) // CMP_STRIDE + 1
    blk_idx = np.arange(n_cmp)[:, None] * CMP_STRIDE + np.arange(CMP_BLOCK)[None, :]

    def compress(src, w1, w2):
        blocks = src.reshape(B, S, G, dk)[:, blk_idx] + cmp_pos[None, None, :, None, :]
        blocks = blocks.transpose(0, 3, 1, 2, 4).reshape(B, G, n_cmp, CMP_BLOCK * dk)
        return jax.nn.gelu(blocks @ w1) @ w2

    kc = compress(kc_src, w_ck1, w_ck2)
    vc = compress(vc_src, w_cv1, w_cv2)
    cmp_start = np.arange(n_cmp) * CMP_STRIDE
    cmp_end = jnp.asarray(cmp_start + CMP_BLOCK - 1, dtype=jnp.int32)

    n_slc = S // SLC_BLOCK
    topn = min(SLC_TOPN, n_slc)
    slc_start = np.arange(n_slc) * SLC_BLOCK
    overlap = jnp.asarray(((cmp_start[:, None] < slc_start[None, :] + SLC_BLOCK)
                           & (cmp_start[:, None] + CMP_BLOCK > slc_start[None, :])).astype(np.float32))
    ks = ks_src.reshape(B, S, G, dk).transpose(0, 2, 1, 3).reshape(B, G, n_slc, SLC_BLOCK, dk)
    vs = vs_src.reshape(B, S, G, dk).transpose(0, 2, 1, 3).reshape(B, G, n_slc, SLC_BLOCK, dk)

    pad = ((0, 0), (0, 0), (WINDOW, 0), (0, 0))
    kw = jnp.pad(kw_src.reshape(B, S, G, dk).transpose(0, 2, 1, 3), pad)
    vw = jnp.pad(vw_src.reshape(B, S, G, dk).transpose(0, 2, 1, 3), pad)

    tbl = rel_bias.reshape(NUM_BUCKETS, G, HPG)
    tbl_g = tbl.transpose(1, 0, 2)
    b_ix = jnp.arange(B)[:, None, None, None]
    g_ix = jnp.arange(G)[None, :, None, None]
    blk = jnp.arange(n_slc)

    def block(i):
        t0 = i * QB
        t = t0 + jnp.arange(QB)
        qb = lax.dynamic_slice_in_dim(q, t0, QB, axis=3)
        gb = lax.dynamic_slice_in_dim(gates, t0, QB, axis=3)

        rel_c = t[:, None] - cmp_end[None, :]
        bias_c = tbl[t5_bucket(rel_c)].transpose(2, 3, 0, 1)
        s_c = jnp.einsum('bghtd,bgnd->bghtn', qb, kc) * scale + bias_c
        p_c = masked_softmax(s_c, rel_c >= 0)
        o_c = jnp.einsum('bghtn,bgnd->bghtd', p_c.astype(vc.dtype), vc)

        imp = jnp.einsum('bghtn,nj->bgtj', p_c, overlap)
        cur = t // SLC_BLOCK
        forced = (blk[None, :] == 0) | (blk[None, :] == cur[:, None]) | (blk[None, :] == cur[:, None] - 1)
        valid = blk[None, :] * SLC_BLOCK <= t[:, None]
        score = jnp.where(valid, imp + FORCE_BONUS * forced.astype(jnp.float32), NEG_BIG)
        _, idx = lax.top_k(score, topn)
        k_sel = ks[b_ix, g_ix, idx].reshape(B, G, QB, topn * SLC_BLOCK, dk)
        v_sel = vs[b_ix, g_ix, idx].reshape(B, G, QB, topn * SLC_BLOCK, dk)
        pos = (idx[..., None] * SLC_BLOCK + jnp.arange(SLC_BLOCK)).reshape(B, G, QB, topn * SLC_BLOCK)
        rel_s = t[:, None] - pos
        bias_s = jnp.moveaxis(tbl_g[g_ix, t5_bucket(rel_s)], -1, 2)
        s_s = jnp.einsum('bghtd,bgtkd->bghtk', qb, k_sel) * scale + bias_s
        p_s = masked_softmax(s_s, (rel_s >= 0)[:, :, None])
        o_s = jnp.einsum('bghtk,bgtkd->bghtd', p_s.astype(v_sel.dtype), v_sel)

        kwb = lax.dynamic_slice_in_dim(kw, t0, WINDOW + QB, axis=2)
        vwb = lax.dynamic_slice_in_dim(vw, t0, WINDOW + QB, axis=2)
        pos_w = t0 - WINDOW + jnp.arange(WINDOW + QB)
        rel_w = t[:, None] - pos_w[None, :]
        mask_w = (rel_w >= 0) & (rel_w < WINDOW) & (pos_w[None, :] >= 0)
        bias_w = tbl[t5_bucket(rel_w)].transpose(2, 3, 0, 1)
        s_w = jnp.einsum('bghtd,bgkd->bghtk', qb, kwb) * scale + bias_w
        p_w = masked_softmax(s_w, mask_w)
        o_w = jnp.einsum('bghtk,bgkd->bghtd', p_w.astype(vwb.dtype), vwb)

        return gb[..., 0:1] * o_c + gb[..., 1:2] * o_s + gb[..., 2:3] * o_w

    o = lax.map(block, jnp.arange(S // QB))
    return o.transpose(1, 0, 4, 2, 3, 5).reshape(B, S, D_NSA)

def stick_breaking_mixer(q, k, v):
    B, S = q.shape[:2]
    H, dk, QB = SB_HEADS, HEAD_DIM, SB_QBLOCK
    scale = 1.0 / math.sqrt(dk)
    q = q.reshape(B, S, H, dk).transpose(0, 2, 1, 3)
    k = k.reshape(B, S, H, dk).transpose(0, 2, 1, 3)
    v = v.reshape(B, S, H, dk).transpose(0, 2, 1, 3)
    s_idx = jnp.arange(S)

    def block(i):
        t0 = i * QB
        t = t0 + jnp.arange(QB)
        qb = lax.dynamic_slice_in_dim(q, t0, QB, axis=2)
        z = jnp.einsum('bhtd,bhsd->bhts', qb, k).astype(jnp.float32) * scale
        mask = s_idx[None, :] < t[:, None]
        log_rest = jnp.where(mask, jax.nn.log_sigmoid(-z), 0.0)
        rcs = lax.cumsum(log_rest, axis=3, reverse=True)
        between = jnp.pad(rcs[..., 1:], ((0, 0), (0, 0), (0, 0), (0, 1)))
        log_a = jnp.where(mask, jax.nn.log_sigmoid(z) + between, 0.0)
        a = jnp.where(mask, jnp.exp(log_a), 0.0)
        return jnp.einsum('bhts,bhsd->bhtd', a.astype(v.dtype), v)

    o = lax.map(block, jnp.arange(S // QB))
    return o.transpose(1, 0, 3, 2, 4).reshape(B, S, D_SB)

def hgrn2_mixer(q, f_logit, i_val, lb):
    B, S = q.shape[:2]
    H, dk, dv, C = HG_HEADS, HG_KDIM, HG_VDIM, HG_CHUNK
    n_c = S // C
    f32 = f_logit.astype(jnp.float32)
    log_f = jnp.logaddexp(jnp.log(jnp.maximum(lb, LB_FLOOR)), jnp.log1p(-lb) + jax.nn.log_sigmoid(f32))
    key = (1.0 - lb) * jax.nn.sigmoid(-f32)

    def heads(a, d):
        return a.astype(jnp.float32).reshape(B, n_c, C, H, d).transpose(1, 0, 3, 2, 4)

    qc, kc, lfc, vc = heads(q, dk), heads(key, dk), heads(log_f, dk), heads(i_val, dv)
    causal = jnp.asarray(np.tril(np.ones((C, C), dtype=bool)))[None, None, :, :, None]

    def step(state, inp):
        qx, kx, lf, vx = inp
        b = jnp.cumsum(lf, axis=2)
        diff = b[:, :, :, None, :] - b[:, :, None, :, :]
        decay = jnp.where(causal, jnp.exp(jnp.where(causal, diff, 0.0)), 0.0)
        att = jnp.einsum('bhtd,bhsd,bhtsd->bhts', qx, kx, decay)
        o = att @ vx + jnp.einsum('bhtd,bhde->bhte', qx * jnp.exp(b), state)
        b_last = b[:, :, -1:, :]
        state = (jnp.exp(b_last[:, :, 0, :])[..., None] * state
                 + jnp.einsum('bhsd,bhse->bhde', kx * jnp.exp(b_last - b), vx))
        return state, o

    s0 = jnp.zeros((B, H, dk, dv), jnp.float32)
    _, o = lax.scan(step, s0, (qc, kc, lfc, vc))
    return o.transpose(1, 0, 3, 2, 4).reshape(B, S, H, dv)

def second_inputs(seed: int = 0) -> dict:
    key = jax.random.key(seed)
    ks = jax.random.split(key, 13)

    def nrm(k, shape, scale):
        return jax.random.normal(k, shape, jnp.float32) * scale

    x = nrm(ks[0], (BATCH, SEQ, D_MODEL), 1.0)
    w_in = nrm(ks[1], (DEPTH_2, D_MODEL, D_IN), D_MODEL ** -0.5)
    cmp_pos = nrm(ks[2], (DEPTH_2, CMP_BLOCK, HEAD_DIM), 0.1)
    w_ck1 = nrm(ks[3], (DEPTH_2, CMP_BLOCK * HEAD_DIM, CMP_HIDDEN), (CMP_BLOCK * HEAD_DIM) ** -0.5)
    w_ck2 = nrm(ks[4], (DEPTH_2, CMP_HIDDEN, HEAD_DIM), CMP_HIDDEN ** -0.5)
    w_cv1 = nrm(ks[5], (DEPTH_2, CMP_BLOCK * HEAD_DIM, CMP_HIDDEN), (CMP_BLOCK * HEAD_DIM) ** -0.5)
    w_cv2 = nrm(ks[6], (DEPTH_2, CMP_HIDDEN, HEAD_DIM), CMP_HIDDEN ** -0.5)
    hg_lb = nrm(ks[7], (DEPTH_2, HG_HEADS * HG_KDIM), 0.5)
    hg_norm_w = 1.0 + nrm(ks[8], (DEPTH_2, D_HG), 0.05)
    w_out = nrm(ks[9], (DEPTH_2, D_MIX, D_MODEL), D_MIX ** -0.5 * OUT_INIT_SCALE)
    ln_g = 1.0 + nrm(ks[10], (DEPTH_2, D_MODEL), 0.05)
    ln_b = nrm(ks[11], (DEPTH_2, D_MODEL), 0.02)
    rel_bias = nrm(ks[12], (NUM_BUCKETS, NSA_HEADS), 0.5)
    return {'x': x, 'w_in': w_in, 'cmp_pos': cmp_pos, 'w_ck1': w_ck1, 'w_ck2': w_ck2,
            'w_cv1': w_cv1, 'w_cv2': w_cv2, 'hg_lb': hg_lb, 'hg_norm_w': hg_norm_w,
            'w_out': w_out, 'ln_g': ln_g, 'ln_b': ln_b, 'rel_bias': rel_bias}

def second_block(x, w_in, cmp_pos, w_ck1, w_ck2, w_cv1, w_cv2, hg_lb, hg_norm_w,
              w_out, ln_g, ln_b, rel_bias):
    lb_w = jax.nn.softmax(hg_lb.astype(jnp.float32), axis=0)
    lb_all = jnp.cumsum(lb_w, axis=0) - lb_w[0]
    offsets = np.cumsum(SPLIT_SIZES)[:-1].tolist()
    for l in range(DEPTH_2):
        h = x @ w_in[l]
        (nsa_q, nsa_kc, nsa_vc, nsa_ks, nsa_vs, nsa_kw, nsa_vw, nsa_g, nsa_z,
         sb_q, sb_k, sb_v, sb_z, hg_q, hg_f, hg_i, hg_z) = jnp.split(h, offsets, axis=-1)
        o_nsa = nsa_mixer(nsa_q, nsa_kc, nsa_vc, nsa_ks, nsa_vs, nsa_kw, nsa_vw, nsa_g,
                          cmp_pos[l], w_ck1[l], w_ck2[l], w_cv1[l], w_cv2[l], rel_bias)
        o_sb = stick_breaking_mixer(sb_q, sb_k, sb_v)
        o_hg = hgrn2_mixer(hg_q, hg_f, hg_i, lb_all[l])
        o_hg = o_hg * lax.rsqrt(jnp.mean(jnp.square(o_hg), axis=-1, keepdims=True) + RMS_EPS)
        o_hg = (o_hg * hg_norm_w[l].reshape(HG_HEADS, HG_VDIM)).reshape(o_hg.shape[0], o_hg.shape[1], D_HG)
        mixed = jnp.concatenate([o_nsa * jax.nn.silu(nsa_z),
                                 o_sb * jax.nn.silu(sb_z),
                                 o_hg.astype(x.dtype) * jax.nn.silu(hg_z)], axis=-1)
        x = layer_norm(ALPHA * x + (mixed @ w_out[l]).astype(x.dtype), ln_g[l], ln_b[l])
    return x


def setup_inputs(seed=0):
    out = dict(first_inputs(seed))
    for name, value in second_inputs(seed + 1).items():
        if name != "x":
            out[name + "_2"] = value
    return out


def reference(
    x, c, w_ada, b_ada, g_pre, g_post, ev_w_in, ev_q_norm, ev_kv_norm, ev_w_uq, ev_w_ukv,
    ev_sinks, ev_w_out, od_w_in, od_forget_bias, od_lambda, od_subln, od_w_out, w_in_2,
    cmp_pos_2, w_ck1_2, w_ck2_2, w_cv1_2, w_cv2_2, hg_lb_2, hg_norm_w_2, w_out_2, ln_g_2,
    ln_b_2, rel_bias_2,
):
    x = first_block(
        x, c, w_ada, b_ada, g_pre, g_post, ev_w_in, ev_q_norm, ev_kv_norm, ev_w_uq, ev_w_ukv,
        ev_sinks, ev_w_out, od_w_in, od_forget_bias, od_lambda, od_subln, od_w_out,
    )
    return second_block(
        x, w_in_2, cmp_pos_2, w_ck1_2, w_ck2_2, w_cv1_2, w_cv2_2, hg_lb_2, hg_norm_w_2, w_out_2,
        ln_g_2, ln_b_2, rel_bias_2,
    )


_drawn_inputs = setup_inputs


def setup_inputs(seed=0):
    import zlib

    import numpy as np

    out = dict(_drawn_inputs(seed))
    spreads = {}
    factors = {'b_ada': 2.783,
     'g_pre': 4.689,
     'g_post': 5.957,
     'ev_q_norm': 8.0,
     'ev_kv_norm': 8.0,
     'ev_sinks': 8.0,
     'od_subln': 8.0,
     'cmp_pos_2': 8.0,
     'w_ck1_2': 4.346,
     'w_ck2_2': 4.326,
     'hg_norm_w_2': 5.814,
     'rel_bias_2': 4.435}
    for name, (base, spread) in spreads.items():
        noise = np.random.default_rng([zlib.crc32(name.encode()), seed]).standard_normal(out[name].shape)
        drawn = base * np.exp(spread * noise) if base else spread * noise
        out[name] = jnp.asarray(drawn.astype(out[name].dtype))
    for name, factor in factors.items():
        out[name] = (out[name] * factor).astype(out[name].dtype)
    return out
```

```python
from contextlib import ExitStack
import math

import numpy as np
import concourse.bass as bass
from concourse import mybir

F32 = mybir.dt.float32
ALU = mybir.AluOpType
ACT = mybir.ActivationFunctionType
AX = mybir.AxisListType

P = 128
D = 1024
S = 512
T = S // P
KT = D // P
NEG = -1e30

QL, KVL, RD = 384, 256, 32
NH = 8
MN = 64
MQ = MN + RD
DH = 4
LAM_INIT = 0.8 - 0.6 * math.exp(-0.3 * 1)
EPS = 1e-6
NG, HPG, NSH = 2, 3, 6
CB, CS = 32, 16
NC = (S - CB) // CS + 1
SBH, HGH = 4, 6
ALPHA = 2 ** 0.25
LN_EPS = 1e-5
LOG_FLOOR = float(np.log(np.float32(1e-30)))
CLAMP = 80.0
NLEV = 7

ADA = 3 * D


def bucket_onehots():
    dist = np.arange(-511, 513)
    n = np.maximum(dist, 0)
    large = 16 + (np.log(np.maximum(n, 1).astype(np.float32) / np.float32(16))
                  / np.float32(math.log(128 / 16)) * np.float32(16)).astype(np.int32)
    b = np.where(n < 16, n, np.clip(large, 0, 31))
    b = np.where(dist < 0, 32, b)
    fwd = (np.arange(33)[:, None] == b[None, :]).astype(np.float32)
    return fwd, np.ascontiguousarray(fwd[:, 1022:382:-1])


def constants():
    c = {}
    for name, dim in (("head", 64), ("lat", RD)):
        inv = 1.0 / (np.float32(10000.0) ** (np.arange(0, dim, 2, dtype=np.float32) / np.float32(dim)))
        ang = np.arange(S, dtype=np.float32)[:, None] * inv[None, :].astype(np.float32)
        cos, sin = np.cos(ang).astype(np.float32), np.sin(ang).astype(np.float32)
        c[f"cos_{name}"] = np.concatenate([cos, cos], 1)
        c[f"sin_{name}"] = np.concatenate([-sin, sin], 1)
    q, k = np.arange(P)[:, None], np.arange(P)[None, :]
    zero = np.zeros((P, S - P), np.float32)
    c["causal"] = np.concatenate([zero, np.where(k <= q, 0, NEG).astype(np.float32)], 1)
    c["strict"] = np.concatenate([zero, np.where(k < q, 0, NEG).astype(np.float32)], 1)
    c["window"] = np.concatenate([np.where(k > q, 0, NEG), np.where(k <= q, 0, NEG)], 1).astype(np.float32)
    c["ident"] = np.eye(P, dtype=np.float32)
    lev = []
    s, t = np.arange(P)[:, None], np.arange(P)[None, :]
    for l in range(NLEV):
        h = 1 << l
        lev.append((s // (2 * h) == t // (2 * h)) & (s % (2 * h) < h) & (t % (2 * h) >= h))
    lev.append(s == t)
    c["levels"] = np.concatenate(lev, 1).astype(np.float32)
    end = np.arange(NC) * CS + CB - 1
    ok = (np.arange(S)[:, None] >= end[None, :]).astype(np.float32)
    c["cmp_ok"] = ok
    c["onehot_f"], c["onehot_r"] = bucket_onehots()
    return c


def pr_plan():
    jobs, chunks = [], []

    def chunk(name, names):
        chunks.append(name)
        jobs.extend(names)
        chunk_end[name] = len(jobs)

    chunk_end = {}

    def ada(L):
        for c in range(4):
            chunk(("ada", L, c), [("adac", L, c)])
        for c in range(2):
            chunk(("ada", L, 4 + c), [("adag", L, c)])

    def transposes(name):
        jobs.extend((name, i) for i in range(T))

    def out_proj(L):
        for k in range(T):
            jobs.extend([("mT", L, k, 0), ("mT", L, k, 1)])
        chunks.append(("wo", L, 0))
        chunks.append(("wo", L, 1))
        for i in range(T):
            for h in range(2):
                jobs.append(("y", L, i, h))
        chunk_end[("wo", L, 0)] = chunk_end[("wo", L, 1)] = len(jobs)

    ada(0)
    jobs.extend(("hT", 0, k) for k in range(KT))
    chunk(("w", "cq"), [("cq", i) for i in range(T)])
    chunk(("w", "ckv"), [("ckv", i) for i in range(T)])
    transposes("cqT")
    transposes("ckvT")
    u = []
    for i in range(T):
        u += [("uq", i, 0), ("uq", i, 1)]
        if i >= 1:
            u += [("mqT", i - 1, 0), ("mqT", i - 1, 1)]
    u += [("mqT", T - 1, 0), ("mqT", T - 1, 1)]
    chunk(("w", "uq"), u)
    u = []
    for i in range(T):
        u += [("ukv", i, 0), ("ukv", i, 1)]
        if i >= 1:
            u += [("mkT", i - 1, 0), ("mkT", i - 1, 1)]
    u += [("mkT", T - 1, 0), ("mkT", T - 1, 1)]
    chunk(("w", "ukv"), u)

    def with_transposes(a, b):
        u = []
        for i in range(T):
            u.append((a, i))
            if i >= 1:
                u.append((b, i - 1))
        return u + [(b, T - 1)]

    chunk(("w", "sq"), with_transposes("sq", "sqT"))
    chunk(("w", "skv"), with_transposes("skv", "skT"))
    for g in range(2):
        chunk(("w", "gate0", g), [("gate0", g, i) for i in range(T)])
    out_proj(0)
    ada(1)
    jobs.extend(("hT", 1, k) for k in range(KT))
    chunk(("w", "dq"), with_transposes("dq", "dqT"))
    chunk(("w", "dk"), with_transposes("dk", "dkT"))
    chunk(("w", "dv"), [("dv", i) for i in range(T)])
    chunk(("w", "ff"), [("ff",)])
    chunk(("w", "fq"), [("fq", m) for m in range(4)])
    chunk(("w", "fk"), [("fk", m) for m in range(4)])
    chunk(("w", "fv"), [("fv", i) for i in range(T)])
    for g in range(2):
        chunk(("w", "gate1", g), [("gate1", g, i) for i in range(T)])
    out_proj(1)
    jobs.extend(("hT", 2, k) for k in range(KT))
    jobs.append(("relrow", 0))
    jobs.append(("relrow", 1))
    jobs.append(("relcmp", 0))
    jobs.append(("relcmp", 1))
    chunk(("w", "kvc"), [("kc",), ("vc",), ("ks",)] + [("vs", i) for i in range(T)])
    chunk(("w", "kw"), [("kw",)] + [("vwg", i) for i in range(T)])
    chunk(("w", "nq"), [("nq", m) for m in range(3)])
    chunk(("w", "ck1"), [("ckh",)])
    chunk(("w", "cv1"), [("cvh",)])
    chunk(("w", "nz"), [("kcT",), ("vcT", 0), ("vcT", 1)] + [("nz", i) for i in range(T)])
    chunk(("w", "sbqk"), [("sbq", 0), ("sbq", 1), ("sbk", 0), ("sbk", 1)])
    chunk(("w", "sbvz"), [("sbvz", i) for i in range(T)])
    chunk(("w", "hf"), [("hf", m) for m in range(3)])
    chunk(("w", "hq"), [("hq", m) for m in range(3)])
    chunk(("w", "hi"), [("hi", i) for i in range(T)])
    chunk(("w", "hz"), [("hz", i) for i in range(T)])
    for c in range(T - 1):
        jobs.append(("kbT", c))
        jobs.append(("st", c))
    out_proj(2)
    return jobs, chunks, chunk_end


def attention_plan(L):
    groups = []
    for i in range(T):
        if L == 0:
            groups.append(("mla", i, [[("mla", h, i)] for h in range(NH)]))
            groups.append(("swa", i, [[("swa", h, i)] for h in range(NH)]))
        elif L == 1:
            groups.append(("dif", i, [[("dif", 2 * h, i), ("dif", 2 * h + 1, i)] for h in range(DH)]))
            groups.append(("fox", i, [[("fox", h, i)] for h in range(NH)]))
        else:
            groups.append(("cmp", i, [[("cmp", h, i)] for h in range(NSH)]))
            groups.append(("sel", i, [[("sel", h, i)] for h in range(NSH)]))
            groups.append(("win", i, [[("win", h, i)] for h in range(NSH)]))
            groups.append(("sb", i, [[("sb", h, i)] for h in range(SBH)]))
    return groups


RING = 3
WCOLS = KT * 512
NP = 4
LOOK = 2

_CONSTS = ["cos_head", "sin_head", "cos_lat", "sin_lat", "causal", "strict", "window", "ident",
           "levels", "cmp_ok", "onehot_f", "onehot_r"]


def two_block_kernel(nc, A, C, out):
    jobs, chunks, chunk_end = pr_plan()
    prn = {name: n for n, name in enumerate(jobs)}

    with ExitStack() as ctx:
        def sb(name, shape):
            return ctx.enter_context(nc.sbuf_tensor(name, shape, F32))

        def bank(name):
            return ctx.enter_context(nc.psum_tensor(name, [P, 512], F32))

        def sem(name):
            return ctx.enter_context(nc.semaphore(name))

        PR = [bank(f"PR{i}") for i in range(2)]
        SC = [bank(f"SC{i}") for i in range(2)]
        PT = [bank(f"PT{i}") for i in range(2)]
        OB = [bank(f"OB{i}") for i in range(2)]

        ring = sb("ring", [P, RING, WCOLS])
        x = sb("x", [P, T, D])
        hT = sb("hT", [P, KT, S])
        tok = sb("tok", [P, T, D])
        stage = sb("stage", [P, 3072])
        pts = sb("pts", [P, 2, 512])
        t1 = sb("t1", [P, 512])
        t2 = sb("t2", [P, 512])
        d1 = sb("d1", [P, 512])
        d2 = sb("d2", [P, 512])
        d3 = sb("d3", [P, 512])
        cosh_ = sb("cosh", [P, T, 64])
        sinh_ = sb("sinh", [P, T, 64])
        cosl = sb("cosl", [P, T, RD])
        sinl = sb("sinl", [P, T, RD])
        causal = sb("causal", [P, 512])
        window = sb("window", [P, 256])
        ident = sb("ident", [P, P])
        grow = sb("grow", [P, 1024])
        cT = sb("cT", [P, KT])
        cond = sb("cond", [P, KT])
        bcol = sb("bcol", [P, 2, 16])
        gpre = sb("gpre", [P, 2, KT])
        modc = sb("modc", [P, 16])
        acol = sb("acol", [P, KT])
        qn = sb("qn", [P, 3])
        kvn = sb("kvn", [P, 2])
        sink = sb("sink", [P, 2, NH])
        ss = sb("ss", [P, 8])
        rv = sb("rv", [P, 8])
        rr = sb("rr", [P, 8])
        rt = sb("rt", [P, 8])
        lamr = sb("lamr", [P, 4, 64])
        lam = sb("lam", [P, 8])
        subln = sb("subln", [P, 2 * MN])
        rsum = sb("rsum", [P, 16, NH])
        nmax = sb("nmax", [P, 16, NH])
        esink = sb("esink", [P, 16, NH])
        fbias = sb("fbias", [NH, 1])
        fr = sb("fr", [P, 16])
        lam_ss = sb("lam_ss", [P, T])

        arena = sb("arena", [P, 17984])

        def carve(sizes):
            at, got = 0, {}
            for name, shape, rows in sizes:
                n = int(np.prod(shape))
                v = arena[0:rows, at:at + n]
                if len(shape) == 2:
                    v = v.rearrange("p (a b) -> p a b", a=shape[0])
                if len(shape) == 3:
                    v = v.rearrange("p (a b c) -> p a b c", a=shape[0], b=shape[1])
                got[name] = v
                at += n
            assert at <= 17600, at
            return got

        a0 = carve([("mqT", (NH, S), MQ), ("mkT", (NH, S), MQ), ("mV", (T, NH * MN), P),
                    ("sqT", (4, S), P), ("skT", (S,), P), ("sV", (T, P), P), ("krr", (T, RD), P),
                    ("cqT", (3, S), P), ("ckvT", (2, S), P)])
        a1 = carve([("dqT", (DH, S), P), ("dkT", (DH, S), P), ("dV", (T, 512), P),
                    ("fqT", (NH, S), MN + 2), ("fkT", (NH, S), MN + 2), ("fV", (T, 512), P)])
        a2 = carve([("nqT", (3, S), P), ("ksT", (S,), P), ("kwT", (S,), P), ("vs", (T, P), P),
                    ("vw", (T, P), P), ("B", (NSH, S), P), ("sbq", (2, S), P), ("sbk", (2, S), P),
                    ("sbv", (T, 256), P), ("Bc", (T, NSH, NC), P), ("hq", (3, S), P),
                    ("key", (3, S), P), ("b", (3, S), P), ("hi", (T, 384), P),
                    ("gates", (T, 18), P), ("kcT", (NC,), P), ("vc", (NG, MN), NC),
                    ("cmpok", (T, NC), P), ("hk", (NG * NC,), P), ("hv", (NG * NC,), P),
                    ("ck2", (MN,), P), ("cv2", (MN,), P), ("pos2", (16,), P), ("tbl", (NSH,), 33)])
        kvC = {n: arena[:, o:o + 1024].rearrange("p (g t) -> p g t", g=NG)
               for n, o in (("k", 6656), ("v", 7680))}
        onehot_f = arena[0:33, 10472:10472 + 1024]
        onehot_r = arena[0:33, 10472 + 1024:10472 + 1664]
        relrow = arena[0:NSH, 10472 + 1664:10472 + 2304]
        blk = {"k": stage[:, 0:992].rearrange("p (c n) -> p c n", c=16),
               "v": stage[:, 1024:1024 + 992].rearrange("p (c n) -> p c n", c=16)}
        Y = [arena[:, o:o + NLEV * 384].rearrange("p (l m t) -> p l m t", l=NLEV, m=3)
             for o in (0, 2688)]
        qb = [v.rearrange("p (m t) -> p m t", m=3) for v in (arena[:, 5376:5760], stage[:, 2048:2432])]
        kb = [v.rearrange("p (m t) -> p m t", m=3) for v in (arena[:, 5760:6144], stage[:, 2432:2816])]
        kbT = arena[:, 6144:6528]
        dec = [arena[:, 6528 + 4 * r:6531 + 4 * r] for r in range(2)]
        state = arena[:, 6656:7040].rearrange("p (m e) -> p m e", m=3)
        hgnorm = arena[:, 17600:17984]
        gm = [stage[:, 1024 * r:1024 * r + 1024].rearrange("p (l t) -> p l t", l=8) for r in range(2)]
        levels = grow[:, :].rearrange("p (l t) -> p l t", l=8)
        lng = arena[:, 7680:8704]
        lnb = arena[:, 8704:9728]

        cqn = stage[:, 0:1536].rearrange("p (i n) -> p i n", i=T)
        ckvn = stage[:, 1536:2560].rearrange("p (i n) -> p i n", i=T)
        qtok = stage[:, 0:1536].rearrange("p (b n) -> p b n", b=2)
        ktok = stage[:, 1536:3072].rearrange("p (b n) -> p b n", b=2)
        rtok = stage[:, 0:1024].rearrange("p (b n) -> p b n", b=2)
        rktok = stage[:, 1024:1280].rearrange("p (b n) -> p b n", b=2)
        bgate = stage[:, 0:1024]
        gpost = stage[:, 1024:2048]
        zm = stage[:, 0:1024].rearrange("p (b n) -> p b n", b=2)
        pb = stage[:, 1024:3072].rearrange("p (b n) -> p b n", b=NP)
        ybuf = stage[:, 0:2048].rearrange("p (b n) -> p b n", b=2)
        frow = stage[0:NH, 0:512]
        nfrow = stage[0:NH, 512:1024]

        pr_done = sem("pr_done")
        pr_free = [sem(f"pr_free{i}") for i in range(2)]
        w_in = [sem(f"w_in{i}") for i in range(RING)]
        x_in = sem("x_in")
        c_in = sem("c_in")
        row_in = sem("row_in")
        l1_in = sem("l1_in")
        l2_in = sem("l2_in")
        hg_in = sem("hg_in")
        ln_in = sem("ln_in")
        frow_in = sem("frow_in")
        rel_out = sem("rel_out")
        rel_in = sem("rel_in")
        y_out = sem("y_out")
        act_seq = sem("act_seq")
        dve_seq = sem("dve_seq")
        pool_seq = sem("pool_seq")
        rs_v = sem("rs_v")
        rs_e = sem("rs_e")
        sq_s = sem("sq_s")
        exp_b = sem("exp_b")
        exp_c = sem("exp_c")
        cond_s = sem("cond_s")
        xn_s = sem("xn_s")
        x_s = sem("x_s")
        mod_s = sem("mod_s")
        sil_c = sem("sil_c")
        sil_s = sem("sil_s")
        lam_a = sem("lam_a")
        lam_b = sem("lam_b")
        ff_a = sem("ff_a")
        ff_b = sem("ff_b")
        frow_s = sem("frow_s")
        ybuf_s = sem("ybuf_s")
        mean_s = sem("mean_s")
        relr_s = sem("relr_s")
        blk_s = sem("blk_s")
        ge_a = sem("ge_a")
        ge_b = sem("ge_b")
        hg_a = sem("hg_a")
        hg_b = sem("hg_b")
        s_done = sem("s_done")
        masked = sem("masked")
        p_done = sem("p_done")
        post = sem("post")
        sb_l = sem("sb_l")
        sb_a = sem("sb_a")
        pt_done = sem("pt_done")
        pt_ev = [sem(f"pt_ev{i}") for i in range(2)]
        pv_done = sem("pv_done")
        ob_free = sem("ob_free")
        y_s = sem("y_s")
        ye_s = sem("ye_s")
        yr_s = sem("yr_s")
        g_done = sem("g_done")
        gm_s = sem("gm_s")
        ho_done = sem("ho_done")
        hof = sem("hof")
        st_s = sem("st_s")
        hs_a = sem("hs_a")

        plan = [attention_plan(L) for L in range(3)]
        s_no, v_no, g_no, last_v = {}, {}, {}, {}
        s_units, v_units = [], []
        for L in range(3):
            for g, (kind, i, vus) in enumerate(plan[L]):
                for j, sus in enumerate(vus):
                    v_no[L, g, j] = len(v_units)
                    for su in sus:
                        s_no[su] = len(s_units)
                        s_units.append((L, g, su, len(v_units)))
                    v_units.append((L, g, j, sus))
                g_no[L, g] = len(g_no)
                last_v[L, g] = len(v_units) - 1

        post_no = {}
        for v, e in enumerate(v_units):
            if e[3][0][0] in ("dif", "cmp"):
                post_no[v] = len(post_no)

        def steps(L):
            mine = [v for v, e in enumerate(v_units) if e[0] == L]
            s_all = [s for s, e in enumerate(s_units) if e[0] == L]
            nxt = s_all[0]
            for v in mine:
                need = s_no[v_units[v][3][-1]]
                upto = min(need + LOOK, s_all[-1])
                new = list(range(nxt, upto + 1))
                nxt = max(nxt, upto + 1)
                yield v, v_units[v], new

        def score_operands(su):
            kind, h, i = su
            q = slice(i * P, i * P + P)
            nk = (i + 1) * P
            tail = slice(S - nk, S)
            if kind == "mla":
                return a0["mqT"][:, h, q], a0["mkT"][:, h, 0:nk], causal[:, tail], MQ ** -0.5, nk
            if kind == "swa":
                r, j = 64 * (h // 4), h % 4
                k0 = max(i - 1, 0) * P
                return (a0["sqT"][r:r + 64, j, q], a0["skT"][r:r + 64, k0:nk],
                        window[:, 256 - (nk - k0):256], MN ** -0.5, nk - k0)
            if kind == "dif":
                r = 64 * (h % 2)
                return (a1["dqT"][r:r + 64, h // 2, q], a1["dkT"][r:r + 64, h // 2, 0:nk],
                        causal[:, tail], MN ** -0.5, nk)
            if kind == "fox":
                return a1["fqT"][:, h, q], a1["fkT"][:, h, 0:nk], causal[:, tail], 1.0, nk
            r, m = 64 * (h // HPG), h % HPG
            if kind == "cmp":
                return a2["nqT"][r:r + 64, m, q], a2["kcT"][r:r + 64, :], a2["Bc"][:, i, h, :], 1.0, NC
            if kind in ("sel", "win"):
                k = a2["ksT" if kind == "sel" else "kwT"]
                return a2["nqT"][r:r + 64, m, q], k[r:r + 64, 0:nk], a2["B"][:, h, tail], 1.0, nk
            r = 64 * (h % 2)
            return a2["sbq"][r:r + 64, h // 2, q], a2["sbk"][r:r + 64, h // 2, 0:nk], causal[:, tail], 1.0, nk

        def value_blocks(su):
            kind, h, i = su
            if kind == "mla":
                return [a0["mV"][:, k, h * 64:h * 64 + 64] for k in range(i + 1)]
            if kind == "swa":
                r = 64 * (h // 4)
                return [a0["sV"][:, k, r:r + 64] for k in range(max(i - 1, 0), i + 1)]
            if kind == "dif":
                return [a1["dV"][:, k, (h // 2) * P:(h // 2) * P + P] for k in range(i + 1)]
            if kind == "fox":
                return [a1["fV"][:, k, h * 64:h * 64 + 64] for k in range(i + 1)]
            if kind == "cmp":
                return [a2["vc"][:, h // HPG, :]]
            if kind in ("sel", "win"):
                v, r = a2["vs" if kind == "sel" else "vw"], 64 * (h // HPG)
                return [v[:, k, r:r + 64] for k in range(i + 1)]
            return [a2["sbv"][:, k, h * 64:h * 64 + 64] for k in range(i + 1)]

        def column(su):
            return su[1]

        def take(eng, name):
            p = prn[name]
            eng.wait_ge(pr_done, p + 1)
            return PR[p % 2]

        def drained(eng, name):
            p = prn[name]
            eng.wait_ge(pr_free[p % 2], p // 2 + 1)
            if p:
                eng.wait_ge(pr_free[(p - 1) % 2], (p - 1) // 2 + 1)

        def used(eng, name):
            eng.wait_ge(pr_done, prn[name] + 1)

        OFF1 = {n: o for n, o in zip(("dq", "dk", "dv", "fq", "fk", "fv", "ff", "gate"),
                                     (0, 512, 1024, 1536, 2048, 2560, 3072, 3080))}
        wcols = {}

        def wsrc(w, c0, n):
            return w[:, c0:c0 + n].rearrange("(k p) n -> p k n", p=P)

        def chunk_parts(name):
            kind = name[0]
            if kind == "ada":
                return KT, 512, [(slice(0, 512), wsrc(A["w_ada"][name[1]], 512 * name[2], 512))]
            if kind == "wo":
                w = {0: A["ev_w_out"][0], 1: A["od_w_out"][0], 2: A["w_out_2"][0]}[name[1]]
                return KT, 512, [(slice(0, 512), wsrc(w, 512 * name[2], 512))]
            n = name[1]
            ev, od, w2 = A["ev_w_in"][0], A["od_w_in"][0], A["w_in_2"][0]
            if n in ("uq", "ukv"):
                w = A["ev_w_uq"][0] if n == "uq" else A["ev_w_ukv"][0]
                return w.shape[0] // P, w.shape[1], [(slice(0, w.shape[1]), wsrc(w, 0, w.shape[1]))]
            if n in ("ck1", "cv1"):
                w = A["w_ck1_2" if n == "ck1" else "w_cv1_2"][0]
                return 16, P, [(slice(0, P), wsrc(w, 0, P))]
            if n == "nq":
                w = w2[:, 0:384].rearrange("(k p) (g m d) -> m p k g d", p=P, g=NG, m=3)
                return KT, 384, [((m, g), w[m][:, :, g, :]) for m in range(3) for g in range(NG)]
            at = {"cq": (ev, 0, 384), "ckv": (ev, 384, 288), "sq": (ev, 672, 512), "skv": (ev, 1184, 256),
                  "kvc": (w2, 384, 512), "kw": (w2, 896, 274), "nz": (w2, 1170, 384),
                  "sbqk": (w2, 1554, 512), "sbvz": (w2, 2066, 512), "hq": (w2, 2578, 384),
                  "hf": (w2, 2962, 384), "hi": (w2, 3346, 384), "hz": (w2, 3730, 384)}
            if n in at:
                w, c0, n_ = at[n]
            elif n == "gate0":
                w, c0, n_ = ev, 1440 + 512 * name[2], 512
            elif n == "gate1":
                w, c0, n_ = od, OFF1["gate"] + 512 * name[2], 512
            else:
                w, c0, n_ = od, OFF1[n], 8 if n == "ff" else 512
            return KT, n_, [(slice(0, n_), wsrc(w, c0, n_))]

        chunk_no = {c: n for n, c in enumerate(chunks)}
        w_val, w_view, filled = {}, {}, [0] * RING
        for n, c in enumerate(chunks):
            K, width, parts = chunk_parts(c)
            filled[n % RING] += 16 * len(parts)
            w_val[c] = filled[n % RING]
            w_view[c] = ring[:, n % RING, 0:K * width].rearrange("p (k n) -> p k n", k=K)

        def rows(ap, n, at=0):
            return bass.AP(ap.tensor, ap.offset + at, [[0, P], [1, n]])

        scr = nc.dram_tensor("rel_rows", [NSH, P, 640], F32, kind="Internal").ap()
        block = ctx.enter_context(nc.Block())

        @block.sync
        def _(sp):
            for n, c in enumerate(chunks):
                if n >= RING:
                    sp.wait_ge(pr_done, chunk_end[chunks[n - RING]])
                for where, src in chunk_parts(c)[2]:
                    if isinstance(where, tuple):
                        dst = w_view[c][:, :, where[0] * P + where[1] * MN:where[0] * P + where[1] * MN + MN]
                    else:
                        dst = w_view[c][:, :, where]
                    sp.dma_start(dst, src).then_inc(w_in[n % RING], 16)
                if c == ("w", "cv1"):
                    sp.wait_ge(relr_s, 1)
                    sp.dma_start(scr, spread(relrow, P)).then_inc(rel_out, 16)
                    sp.wait_ge(rel_out, 16)
                    sp.dma_start(a2["B"], bass.AP(scr.tensor, scr.offset + P - 1,
                                                  [[639, P], [640 * P, NSH], [1, S]])).then_inc(rel_in, 16)
            for i in range(T):
                sp.wait_ge(x_s, 2 * T + i + 1)
                sp.dma_start(out[0, i * P:i * P + P, :], x[:, i, :]).then_inc(y_out, 16)
            sp.wait_ge(y_out, 16 * T)

        @block.tensor
        def _(pe):
            count = [0]

            def begin(name):
                p = prn[name]
                assert p == count[0], (name, p, count[0])
                count[0] += 1
                if p >= 2:
                    pe.wait_ge(pr_free[p % 2], p // 2)
                return PR[p % 2]

            def weights(c):
                pe.wait_ge(w_in[chunk_no[c] % RING], w_val[c])
                return w_view[c]

            def contract(dst, lhs, rhs, K):
                for k in range(K):
                    mm = pe.matmul(dst, lhs(k), rhs(k), start=(k == 0), stop=(k == K - 1))
                return mm

            def token_major(name, W, i, c0, n, src=hT, K=KT):
                b = begin(name)
                contract(b[:, 0:n], lambda k: src[:, k, i * P:i * P + P], lambda k: W[:, k, c0:c0 + n],
                         K).then_inc(pr_done, 1)

            def feature_major(name, W, c0, m=P):
                b = begin(name)
                contract(b[0:m, :], lambda k: W[:, k, c0:c0 + m], lambda k: hT[:, k, :], KT).then_inc(pr_done, 1)

            def transposes(name, srcs, m=P):
                b = begin(name)
                for j, s in enumerate(srcs):
                    tr = pe.transpose(b[0:m, j * P:j * P + P], s, ident[:, :])
                tr.then_inc(pr_done, 1)

            def ada(L):
                if L == 0:
                    pe.wait_ge(cond_s, 1)
                for c in range(4):
                    W = weights(("ada", L, c))
                    b = begin(("adac", L, c))
                    for m in range(4):
                        mm = contract(b[:, m:m + 1], lambda k: W[:, k, m * P:m * P + P],
                                      lambda k: cond[:, k:k + 1], KT)
                    mm.then_inc(pr_done, 1)
                for c in range(2):
                    W = weights(("ada", L, 4 + c))
                    b = begin(("adag", L, c))
                    contract(b[:, :], lambda k: cond[:, k:k + 1].to_broadcast([P, P]),
                             lambda k: W[:, k, :], KT).then_inc(pr_done, 1)

            def make_hT(L):
                src = x if L == 2 else tok
                for k in range(KT):
                    if k == 0:
                        if L == 2:
                            pe.wait_ge(x_s, 2 * T)
                        else:
                            pe.wait_ge(xn_s, T * (L + 1))
                    transposes(("hT", L, k), [src[:, i, k * P:k * P + P] for i in range(T)])
                drained(pe, ("hT", L, KT - 1))

            def attention(L):
                def values(v):
                    L_, g, j, sus = v_units[v]
                    su = sus[-1]
                    ob = OB[g_no[L, g] % 2]
                    if j == 0 and g_no[L, g] >= 2:
                        pe.wait_ge(ob_free, g_no[L, g] - 1)
                    pe.wait_ge(pt_ev[v % 2], v // 2 + 1)
                    blocks = value_blocks(su)
                    w = 128 if su[0] == "dif" else 64
                    h = su[1] // 2 if su[0] == "dif" else su[1]
                    for n, vb in enumerate(blocks):
                        rows_ = NC if su[0] == "cmp" else P
                        mm = pe.matmul(ob[:, h * w:h * w + w], pts[0:rows_, v % 2, n * P:n * P + P], vb,
                                       start=(n == 0), stop=(n == len(blocks) - 1))
                    mm.then_inc(pv_done, 1)

                first = True
                for v, (_, g, j, sus), new in steps(L):
                    for s in new:
                        if s >= 2:
                            pe.wait_ge(masked, s - 1)
                        q, k, _, _, n = score_operands(s_units[s][2])
                        pe.matmul(SC[s % 2][:, 0:n], q, k, start=True, stop=True).then_inc(s_done, 1)
                    su = sus[-1]
                    s = s_no[su]
                    if su[0] in ("dif", "cmp"):
                        pe.wait_ge(post, post_no[v] + 1)
                    else:
                        pe.wait_ge(p_done, s + 1)
                    if v >= 2:
                        pe.wait_ge(pt_ev[v % 2], v // 2)
                    n = score_operands(su)[4]
                    nb = -(-n // P)
                    for b in range(nb):
                        w = min(P, n - b * P)
                        tr = pe.transpose(PT[v % 2][0:w, b * P:b * P + P], pb[:, s % NP, b * P:b * P + w],
                                          ident[:, :])
                    tr.then_inc(pt_done, 1)
                    if not first:
                        values(v - 1)
                    first = False
                values(v)

            def out_proj(L):
                pe.wait_ge(ob_free, g_no[L, len(plan[L]) - 1] + 1)
                if L == 2:
                    pe.wait_ge(hof, T)
                for i in range(T):
                    for g in range(2):
                        transposes(("mT", L, i, g), [tok[:, i, (4 * g + j) * P:(4 * g + j + 1) * P] for j in range(4)])
                drained(pe, ("mT", L, T - 1, 1))
                W = [weights(("wo", L, h)) for h in range(2)]
                for i in range(T):
                    for h in range(2):
                        token_major(("y", L, i, h), W[h], i, 0, 512)

            pe.wait_ge(c_in, 16 * N_C)
            ada(0)
            make_hT(0)
            W = weights(("w", "cq"))
            for i in range(T):
                token_major(("cq", i), W, i, 0, 384)
            W = weights(("w", "ckv"))
            for i in range(T):
                token_major(("ckv", i), W, i, 0, 288)
            for i in range(T):
                if i == 0:
                    drained(pe, ("ckv", T - 1))
                transposes(("cqT", i), [cqn[:, i, k * P:k * P + P] for k in range(3)])
            for i in range(T):
                transposes(("ckvT", i), [ckvn[:, i, k * P:k * P + P] for k in range(2)])
            drained(pe, ("ckvT", T - 1))
            for w, src, K, n, tr_name, tile in (("uq", a0["cqT"], 3, 384, "mqT", qtok),
                                                ("ukv", a0["ckvT"], 2, 512, "mkT", ktok)):
                W = weights(("w", w))
                for i in range(T + 1):
                    if i < T:
                        for g in range(2):
                            token_major((w, i, g), W, i, n * g, n, src, K)
                    if i >= 1:
                        drained(pe, (w, i - 1, 1))
                        for g in range(2):
                            transposes((tr_name, i - 1, g),
                                       [tile[:, (i - 1) % 2, (4 * g + j) * MQ:(4 * g + j + 1) * MQ] for j in range(4)], MQ)

            def roped(name, n, nt, tile):
                W = weights(("w", name[0]))
                for i in range(T + 1):
                    if i < T:
                        token_major((name[0], i), W, i, 0, n)
                    if i >= 1:
                        drained(pe, (name[0], i - 1))
                        transposes((name[1], i - 1), [tile[:, (i - 1) % 2, k * P:k * P + P] for k in range(nt)])

            roped(("sq", "sqT"), 512, 4, rtok)
            roped(("skv", "skT"), 256, 1, rktok)
            for g in range(2):
                W = weights(("w", "gate0", g))
                for i in range(T):
                    token_major(("gate0", g, i), W, i, 0, 512)
            drained(pe, ("gate0", 1, T - 1))
            attention(0)
            out_proj(0)
            ada(1)
            make_hT(1)
            roped(("dq", "dqT"), 512, 4, rtok)
            roped(("dk", "dkT"), 512, 4, rtok)
            W = weights(("w", "dv"))
            for i in range(T):
                token_major(("dv", i), W, i, 0, 512)
            feature_major(("ff",), weights(("w", "ff")), 0, NH)
            for n in ("fq", "fk"):
                W = weights(("w", n))
                for m in range(4):
                    feature_major((n, m), W, m * P)
            W = weights(("w", "fv"))
            for i in range(T):
                token_major(("fv", i), W, i, 0, 512)
            for g in range(2):
                W = weights(("w", "gate1", g))
                for i in range(T):
                    token_major(("gate1", g, i), W, i, 0, 512)
            drained(pe, ("gate1", 1, T - 1))
            pe.wait_ge(frow_in, 32 * NH)
            attention(1)
            out_proj(1)
            make_hT(2)
            pe.wait_ge(l2_in, 16 * N_L2)
            pe.wait_ge(pool_seq, 3)
            for r in range(2):
                b = begin(("relrow", r))
                pe.matmul(b[0:NSH, 0:320], a2["tbl"][:, 0:NSH], onehot_r[:, 320 * r:320 * r + 320],
                          start=True, stop=True).then_inc(pr_done, 1)
            for r in range(2):
                b = begin(("relcmp", r))
                for i in (2 * r, 2 * r + 1):
                    for n in range(NC):
                        at = 511 + P * i - CS * n - (CB - 1)
                        c = ((i % 2) * NC + n) * NSH
                        mm = pe.matmul(b[:, c:c + NSH], onehot_f[:, at:at + P], a2["tbl"][:, 0:NSH],
                                       start=True, stop=True)
                mm.then_inc(pr_done, 1)
            W = weights(("w", "kvc"))
            for n, name in enumerate((("kc",), ("vc",), ("ks",))):
                feature_major(name, W, n * P)
            for i in range(T):
                token_major(("vs", i), W, i, 384, P)
            W = weights(("w", "kw"))
            feature_major(("kw",), W, 0)
            for i in range(T):
                token_major(("vwg", i), W, i, P, 146)
            W = weights(("w", "nq"))
            for m in range(3):
                feature_major(("nq", m), W, m * P)
            for n, name in (("k", "ckh"), ("v", "cvh")):
                W = weights(("w", f"c{n}1"))
                pe.wait_ge(blk_s, 1 if n == "k" else 2)
                b = begin((name,))
                contract(b[:, 0:NG * NC], lambda k: W[:, k, :], lambda k: blk[n][:, k, :], 16).then_inc(pr_done, 1)
            drained(pe, ("cvh",))
            b = begin(("kcT",))
            pe.matmul(b[0:MN, 0:NG * NC], a2["ck2"], a2["hk"], start=True, stop=True).then_inc(pr_done, 1)
            for g in range(NG):
                b = begin(("vcT", g))
                pe.matmul(b[0:NC, 0:MN], a2["hv"][:, g * NC:g * NC + NC], a2["cv2"],
                          start=True, stop=True).then_inc(pr_done, 1)
            W = weights(("w", "nz"))
            for i in range(T):
                token_major(("nz", i), W, i, 0, 384)
            W = weights(("w", "sbqk"))
            for n, name in enumerate((("sbq", 0), ("sbq", 1), ("sbk", 0), ("sbk", 1))):
                feature_major(name, W, n * P)
            W = weights(("w", "sbvz"))
            for i in range(T):
                token_major(("sbvz", i), W, i, 0, 512)
            for n in ("hf", "hq"):
                W = weights(("w", n))
                for m in range(3):
                    feature_major((n, m), W, m * P)
            for n in ("hi", "hz"):
                W = weights(("w", n))
                for i in range(T):
                    token_major((n, i), W, i, 0, 384)
            drained(pe, ("hz", T - 1))
            pe.wait_ge(rel_in, 16)
            attention(2)

            pe.wait_ge(ob_free, len(g_no))
            pe.wait_ge(masked, len(s_units))
            for r in range(2):
                pe.wait_ge(pt_ev[r], (len(v_units) + 1 - r) // 2)
            GB = [SC, PT]
            for c in range(T):
                t = slice(c * P, c * P + P)
                pe.wait_ge(yr_s, c + 1)
                if c < T - 1:
                    transposes(("kbT", c), [kb[c % 2][:, m, :] for m in range(3)])

                def level_products(h):
                    n = c * HGH + h
                    m, r = h // 2, 64 * (h % 2)
                    if n >= 2:
                        pe.wait_ge(gm_s, n - 1)
                    for l in range(8):
                        dst = GB[n % 2][l // 4][:, (l % 4) * P:(l % 4 + 1) * P]
                        if l < NLEV:
                            a = b_ = Y[c % 2][r:r + 64, l, m, :]
                        else:
                            a, b_ = a2["key"][r:r + 64, m, t], a2["hq"][r:r + 64, m, t]
                        mm = pe.matmul(dst, a, b_, start=True, stop=True)
                    mm.then_inc(g_done, 1)

                def outputs(h):
                    n = c * HGH + h
                    m, r = h // 2, 64 * (h % 2)
                    ob = OB[c % 2][:, h * MN:h * MN + MN]
                    if c > 0 and h % 2 == 0:
                        pe.matmul(OB[c % 2][:, m * P:m * P + P], qb[c % 2][:, m, :], state[:, m, :],
                                  start=True, stop=False)
                    pe.wait_ge(gm_s, n + 1)
                    for l in range(8):
                        mm = pe.matmul(ob, gm[n % 2][:, l, :], a2["hi"][:, c, h * MN:h * MN + MN],
                                       start=(c == 0 and l == 0), stop=(l == 7 and (c == 0 or h % 2 == 1)))
                    mm.then_inc(ho_done, 1)

                if c >= 2:
                    pe.wait_ge(hof, c - 1)
                if c > 0:
                    drained(pe, ("st", c - 1))
                for h in range(HGH + 1):
                    if h < HGH:
                        level_products(h)
                    if h >= 1:
                        outputs(h - 1)
                if c < T - 1:
                    drained(pe, ("kbT", c))
                    b = begin(("st", c))
                    for m in range(3):
                        mm = pe.matmul(b[:, m * P:m * P + P], kbT[:, m * P:m * P + P],
                                       a2["hi"][:, c, m * P:m * P + P], start=True, stop=True)
                    mm.then_inc(pr_done, 1)
            out_proj(2)

        @block.scalar
        def _(act):
            seen = Ticks()

            def link(ins):
                n = seen.next("act_seq")
                ins.then_inc(act_seq, 1)
                act.wait_ge(act_seq, n)

            def give(ins, s, value):
                ins.then_inc(s, 1)
                act.wait_ge(s, value)

            def release(ins, name):
                p = prn[name]
                give(ins, pr_free[p % 2], p // 2 + 1)

            def hear(s, key):
                act.wait_ge(s, seen.next(key))

            def say(ins, s, key):
                give(ins, s, seen.next(key))

            def copy(dst, src, scale=1.0):
                return act.activation(dst, src, ACT.Copy, scale=scale)

            def rsqrt(n=1):
                hear(rs_v, "rs_v")
                link(act.activation(rr[:, 0:n], rv[:, 0:n], ACT.Ln))
                say(act.activation(rr[:, 0:n], rr[:, 0:n], ACT.Exp, scale=-0.5), rs_e, "rs_e")

            def token_square(name, n):
                b = take(act, name)
                say(act.activation(t1[:, 0:n], b[:, 0:n], ACT.Square, accum_out=ss[:, 0:1]), sq_s, "sq_s")
                rsqrt()

            gates_seen = []

            def exp_neg(name, n):
                t = (t1, t2)[len(gates_seen) % 2][:, 0:n]
                gates_seen.append(name)
                hear(sil_c, "sil_c")
                say(act.activation(t, t, ACT.Exp, scale=-1.0), sil_s, "sil_s")

            def heads(v, j=4):
                return v.rearrange("p (j t) -> p j t", j=j)

            def hT_even(L):
                if L < 2:
                    act.wait_ge(mod_s, L + 1)
                for k in range(0, KT, 2):
                    b = take(act, ("hT", L, k))
                    if L < 2:
                        ins = act.activation(hT[:, k, :], b[:, :], ACT.Identity, scale=acol[:, k:k + 1],
                                             bias=modc[:, k:k + 1])
                    else:
                        ins = copy(hT[:, k, :], b[:, :])
                    release(ins, ("hT", L, k))

            def attention(L):
                pending = []

                def stick_tail():
                    if pending:
                        s = pending.pop()
                        n = score_operands(s_units[s][2])[4]
                        hear(sb_a, "sb_a")
                        give(act.activation(pb[:, s % NP, 0:n], zm[:, s % 2, 0:n], ACT.Exp), p_done, s + 1)

                for v, (_, g, j, sus), new in steps(L):
                    for s in new:
                        _, sg, su, _ = s_units[s]
                        n = score_operands(su)[4]
                        c = su[1]
                        row = g_no[L, sg] % 16
                        if su[0] != "sb":
                            stick_tail()
                        act.wait_ge(masked, s + 1)
                        if s >= NP:
                            act.wait_ge(pt_done, s_units[s - NP][3] + 1)
                        if su[0] == "sb":
                            t = (t1, t2)[s % 2][:, 0:n]
                            link(act.activation(t, t, ACT.Exp))
                            say(act.activation(t, t, ACT.Ln, bias=1.0), sb_l, "sb_l")
                            stick_tail()
                            pending.append(s)
                            continue
                        give(act.activation(pb[:, s % NP, 0:n], zm[:, s % 2, 0:n], ACT.Exp,
                                            bias=nmax[:, row, c:c + 1], scale=-1.0,
                                            accum_out=rsum[:, row, c:c + 1]), p_done, s + 1)
                        if su[0] == "swa":
                            link(act.activation(esink[:, row, c:c + 1], sink[:, 0, c:c + 1], ACT.Exp,
                                                bias=nmax[:, row, c:c + 1]))
                    if s_units[-1][0] == L and s_no[sus[-1]] + LOOK >= len(s_units) - 1:
                        stick_tail()
                    if v % 2 == 0:
                        act.wait_ge(pt_done, v + 1)
                        if v >= 2:
                            act.wait_ge(pv_done, v - 1)
                        r, w = transposed_shape(sus[-1])
                        give(copy(pts[0:r, 0, 0:w], PT[0][0:r, 0:w]), pt_ev[0], v // 2 + 1)
                    if sus[0][0] == "dif" and v - 1 in last_v.values() and v_units[v - 1][3][0][0] == "dif":
                        pass
                    if v >= 1 and v_units[v - 1][0] == L and last_v[L, v_units[v - 1][1]] == v - 1 \
                            and v_units[v - 1][3][0][0] == "dif":
                        rsqrt(DH)

            def out_proj(L):
                for i in range(T):
                    b = take(act, ("mT", L, i, 0))
                    release(copy(hT[:, 0:4, i * P:i * P + P], heads(b[:, :])), ("mT", L, i, 0))
                for i in range(T):
                    drained(act, ("y", L, i, 1))
                    if L == 2:
                        say(act.activation(tok[:, i, :], ybuf[:, i % 2, :], ACT.Copy,
                                           accum_out=ss[:, 0:1]), sq_s, "sq_s")
                        hear(mean_s, "mean_s")
                        say(act.activation(tok[:, i, :], ybuf[:, i % 2, :], ACT.Square,
                                           bias=lam[:, 7:8], accum_out=ss[:, 0:1]), sq_s, "sq_s")
                    else:
                        say(act.activation(tok[:, i, :], ybuf[:, i % 2, :], ACT.Square,
                                           accum_out=ss[:, 0:1]), sq_s, "sq_s")
                    rsqrt()

            act.dma_start(cT[:, :], A["c"].rearrange("o (k p) -> p (o k)", p=P),
                          allow_slow_non_contiguous=True).then_inc(x_in, 16)
            act.dma_start(x[:, :, :], A["x"][0].rearrange("(i p) d -> p i d", p=P)).then_inc(x_in, 16)
            act.dma_start(ident[:, :], C["ident"]).then_inc(c_in, 16)
            for L in range(2):
                act.dma_start(bcol[:, L, :], A["b_ada"][L, 0:2 * D].rearrange("(k p) -> p k", p=P),
                          allow_slow_non_contiguous=True).then_inc(c_in, 16)
                act.dma_start(gpre[:, L, :], A["g_pre"][L].rearrange("(k p) -> p k", p=P),
                          allow_slow_non_contiguous=True).then_inc(c_in, 16)
            act.dma_start(bgate, rows(A["b_ada"], D, 2 * D)).then_inc(row_in, 16)
            act.dma_start(gpost, rows(A["g_post"], D)).then_inc(row_in, 16)
            for dst, name in ((cosh_, "cos_head"), (sinh_, "sin_head"), (cosl, "cos_lat"), (sinl, "sin_lat")):
                act.dma_start(dst[:, :, :], C[name].rearrange("(i p) d -> p i d", p=P)).then_inc(c_in, 16)
            act.dma_start(causal[:, :], C["causal"]).then_inc(c_in, 16)
            act.dma_start(window[:, :], C["window"]).then_inc(c_in, 16)
            act.dma_start(qn[:, :], A["ev_q_norm"][0].rearrange("(k p) -> p k", p=P),
                          allow_slow_non_contiguous=True).then_inc(c_in, 16)
            act.dma_start(kvn[:, :], A["ev_kv_norm"][0].rearrange("(k p) -> p k", p=P),
                          allow_slow_non_contiguous=True).then_inc(c_in, 16)
            act.dma_start(sink[:, 0, :], rows(A["ev_sinks"], NH)).then_inc(c_in, 16)
            act.dma_start(lamr[:, :, :], bass.AP(A["od_lambda"].tensor, 0, [[0, P], [64, 4], [1, 64]])).then_inc(c_in, 16)
            act.dma_start(subln[:, :], rows(A["od_subln"], 2 * MN)).then_inc(c_in, 16)
            act.dma_start(fbias[:, :], A["od_forget_bias"].rearrange("o h -> h o"),
                          allow_slow_non_contiguous=True).then_inc(c_in, 16)

            act.wait_ge(exp_b, 1)
            say(act.activation(cond[:, :], cond[:, :], ACT.Exp, scale=-1.0), exp_c, "exp_c")
            rsqrt(T)
            hT_even(0)
            for i in range(T):
                token_square(("cq", i), QL)
            for i in range(T):
                token_square(("ckv", i), KVL)
            for name, nk, dst, g in (("cqT", 3, a0["cqT"], qn), ("ckvT", 2, a0["ckvT"], kvn)):
                for i in range(T):
                    b = take(act, (name, i))
                    for k in range(nk):
                        ins = act.activation(dst[:, k, i * P:i * P + P], b[:, k * P:k * P + P], ACT.Copy,
                                             scale=g[:, k:k + 1])
                        if k < nk - 1:
                            link(ins)
                    release(ins, (name, i))
            for i in range(T):
                for g in range(2):
                    b = take(act, ("mqT", i, g))
                    release(copy(a0["mqT"][:, 4 * g:4 * g + 4, i * P:i * P + P], heads(b[0:MQ, :])), ("mqT", i, g))
            for i in range(T):
                if i >= 2:
                    used(act, ("mkT", i - 2, 1))
                for g in range(2):
                    b = take(act, ("ukv", i, g))[:, :].rearrange("p (h d) -> p h d", h=4)
                    kt = ktok[:, i % 2, 384 * g:384 * g + 384].rearrange("p (h d) -> p h d", h=4)
                    link(copy(kt[:, :, 0:MN], b[:, :, 0:MN]))
                    link(copy(kt[:, :, MN:MQ], spread(a0["krr"][:, i, :], 4)))
                    mv = a0["mV"][:, i, 256 * g:256 * g + 256].rearrange("p (h d) -> p h d", h=4)
                    release(copy(mv, b[:, :, MN:2 * MN]), ("ukv", i, g))
            for i in range(T):
                b = take(act, ("sqT", i))
                release(copy(a0["sqT"][:, :, i * P:i * P + P], heads(b[:, :])), ("sqT", i))
            for i in range(T):
                b = take(act, ("skT", i))
                release(copy(a0["skT"][:, i * P:i * P + P], b[:, 0:P]), ("skT", i))
            for g in range(2):
                for i in range(T):
                    exp_neg(("gate0", g, i), 512)
            attention(0)
            out_proj(0)

            act.wait_ge(x_s, T)
            act.dma_start(bgate, rows(A["b_ada"], D, ADA + 2 * D)).then_inc(row_in, 16)
            act.dma_start(gpost, rows(A["g_post"], D, D)).then_inc(row_in, 16)
            rsqrt(T)
            hT_even(1)
            for n in ("dq", "dk"):
                for i in range(T):
                    b = take(act, (n + "T", i))
                    release(copy(a1[n + "T"][:, :, i * P:i * P + P], heads(b[:, :])), (n + "T", i))
            for i in range(T):
                b = take(act, ("dv", i))
                release(copy(a1["dV"][:, i, :], b[:, :]), ("dv", i))
            act.wait_ge(lam_a, 1)
            say(act.activation(lam[:, 2:4], lam[:, 0:2], ACT.Exp), lam_b, "lam_b")
            act.wait_ge(ff_b, 1)
            link(act.activation(d2[0:NH, :], d2[0:NH, :], ACT.Exp))
            say(act.activation(d2[0:NH, :], d2[0:NH, :], ACT.Ln, bias=1.0), ff_a, "ff_a")
            for m in range(4):
                b = take(act, ("fq", m))
                link(copy(a1["fqT"][0:MN, 2 * m, :], b[0:MN, :], MN ** -0.5))
                release(copy(a1["fqT"][0:MN, 2 * m + 1, :], b[MN:P, :], MN ** -0.5), ("fq", m))
            act.wait_ge(frow_s, 1)
            act.wait_ge(pool_seq, 2)
            for h in range(NH):
                act.dma_start(a1["fqT"][MN + 1:MN + 2, h, :], frow[h:h + 1, :]).then_inc(frow_in, 16)
                act.dma_start(a1["fkT"][MN:MN + 1, h, :], nfrow[h:h + 1, :]).then_inc(frow_in, 16)
            for g in range(2):
                for i in range(T):
                    exp_neg(("gate1", g, i), 512)
            attention(1)
            act.wait_ge(ob_free, g_no[1, len(plan[1]) - 1] + 1)
            act.dma_start(onehot_r, C["onehot_r"]).then_inc(l2_in, 16)
            act.dma_start(onehot_f, C["onehot_f"]).then_inc(l2_in, 16)
            act.dma_start(a2["tbl"][0:32, :], A["rel_bias_2"]).then_inc(l2_in, 16)
            act.dma_start(a2["ck2"], A["w_ck2_2"][0]).then_inc(l2_in, 16)
            act.dma_start(a2["cv2"], A["w_cv2_2"][0]).then_inc(l2_in, 16)
            for s_ in range(2):
                act.dma_start(a2["pos2"][MN * s_:MN * s_ + MN, :],
                              A["cmp_pos_2"][0].rearrange("(c s) d -> s d c", s=2)[s_],
                          allow_slow_non_contiguous=True).then_inc(l2_in, 16)
            act.dma_start(a2["cmpok"], C["cmp_ok"].rearrange("(i p) n -> p i n", p=P)).then_inc(l2_in, 16)
            act.dma_start(causal[:, :], C["strict"]).then_inc(l2_in, 16)
            out_proj(1)

            act.wait_ge(x_s, 2 * T)
            act.dma_start(grow[:, :], C["levels"]).then_inc(hg_in, 16)
            act.dma_start(hgnorm, rows(A["hg_norm_w_2"], 384)).then_inc(hg_in, 16)
            hT_even(2)
            for n, dst in (("k", kvC["k"]), ("v", kvC["v"])):
                b = take(act, (n + "c",))
                for g in range(NG):
                    link(copy(dst[0:MN, g, :], b[MN * g:MN * g + MN, :]))
                    ins = copy(dst[MN:P, g, 0:S - 1], b[MN * g:MN * g + MN, 1:S])
                    if g == 0:
                        link(ins)
                release(ins, (n + "c",))
            b = take(act, ("ks",))
            release(copy(a2["ksT"], b[:, :]), ("ks",))
            for i in range(T):
                b = take(act, ("vs", i))
                release(copy(a2["vs"][:, i, :], b[:, 0:P]), ("vs", i))
            b = take(act, ("kw",))
            release(copy(a2["kwT"], b[:, :]), ("kw",))
            for i in range(T):
                exp_neg(("vwg", i), 18)
            for m in range(3):
                b = take(act, ("nq", m))
                release(copy(a2["nqT"][:, m, :], b[:, :], MN ** -0.5), ("nq", m))
            for _ in range(2):
                hear(ge_b, "ge_b")
                say(act.activation(d2[:, 0:NG * NC], d2[:, 0:NG * NC], ACT.Exp,
                                   scale=-2.0 * math.sqrt(2.0 / math.pi)), ge_a, "ge_a")
            for i in range(T):
                exp_neg(("nz", i), 384)
            for n in ("sbq", "sbk"):
                for m in range(2):
                    b = take(act, (n, m))
                    release(copy(a2[n][:, m, :], b[:, :], MN ** -0.5 if n == "sbq" else 1.0), (n, m))
            for i in range(T):
                exp_neg(("sbvz", i), 256)
            for m in range(3):
                b = take(act, ("hf", m))
                if m == 0:
                    drained(act, ("sbvz", T - 1))
                say(copy(t1[:, :], b[:, :]), hg_a, "hg_a")
                for n in range(2):
                    hear(hg_b, "hg_b")
                    if n == 0:
                        link(act.activation(t2[:, :], t2[:, :], ACT.Exp))
                    link(act.activation(d1[:, :], d1[:, :], ACT.Exp))
                    say(act.activation(d1[:, :], d1[:, :], ACT.Ln, bias=1.0), hg_a, "hg_a")
            for m in range(3):
                b = take(act, ("hq", m))
                release(copy(a2["hq"][:, m, :], b[:, :]), ("hq", m))
            drained(act, ("hf", 2))
            for i in range(T):
                exp_neg(("hz", i), 384)
            attention(2)
            act.wait_ge(ob_free, g_no[2, len(plan[2]) - 1] + 1)
            act.dma_start(lng, rows(A["ln_g_2"], D)).then_inc(ln_in, 16)
            act.dma_start(lnb, rows(A["ln_b_2"], D)).then_inc(ln_in, 16)

            def exponentials(c):
                t = slice(c * P, c * P + P)
                act.wait_ge(y_s, c + 1)
                link(act.activation(Y[c % 2], Y[c % 2], ACT.Exp))
                link(act.activation(kb[c % 2], kb[c % 2], ACT.Exp))
                link(act.activation(qb[c % 2], a2["b"][:, :, t], ACT.Exp))
                give(act.activation(dec[c % 2], a2["b"][:, :, c * P + P - 1:c * P + P], ACT.Exp), ye_s, c + 1)

            exponentials(0)
            for c in range(T):
                if c < T - 1:
                    b = take(act, ("kbT", c))
                    if c:
                        used(act, ("st", c - 1))
                    release(copy(kbT, b[:, 0:384]), ("kbT", c))
                    exponentials(c + 1)
                rsqrt(HGH)
            out_proj(2)

        @block.gpsimd
        def _(pool):
            pool.wait_ge(pv_done, last_v[0, len(plan[0]) - 1] + 1)
            pool.memset(a1["fqT"][MN:MN + 2, :, :], 1.0).then_inc(pool_seq, 1)
            pool.memset(a1["fkT"][MN:MN + 2, :, :], 1.0).then_inc(pool_seq, 1)
            pool.wait_ge(pv_done, last_v[1, len(plan[1]) - 1] + 1)
            pool.memset(a2["tbl"][32:33, :], NEG).then_inc(pool_seq, 1)

        @block.vector
        def _(dve):
            seen = Ticks()

            def link(ins):
                n = seen.next("dve_seq")
                ins.then_inc(dve_seq, 1)
                dve.wait_ge(dve_seq, n)

            def give(ins, s, value):
                ins.then_inc(s, 1)
                dve.wait_ge(s, value)

            def release(ins, name):
                p = prn[name]
                give(ins, pr_free[p % 2], p // 2 + 1)

            def hear(s, key):
                dve.wait_ge(s, seen.next(key))

            def say(ins, s, key):
                give(ins, s, seen.next(key))

            def tt(dst, a, b, op):
                return dve.tensor_tensor(dst, a, b, op)

            def ts(dst, a, s1, op0, s2=None, op1=None):
                if op1 is None:
                    return dve.tensor_scalar(dst, a, s1, None, op0)
                return dve.tensor_scalar(dst, a, s1, s2, op0, op1)

            def stt(dst, a, s, b, op0, op1):
                return dve.scalar_tensor_tensor(out=dst, in0=a, scalar=s, in1=b, op0=op0, op1=op1)

            def rsqrt(src, n, width, eps):
                say(ts(rv[:, 0:n], src, 1.0 / width, ALU.mult, eps, ALU.add), rs_v, "rs_v")
                hear(rs_e, "rs_e")
                link(tt(rt[:, 0:n], rr[:, 0:n], rr[:, 0:n], ALU.mult))
                link(tt(rt[:, 0:n], rt[:, 0:n], rv[:, 0:n], ALU.mult))
                link(ts(rt[:, 0:n], rt[:, 0:n], -0.5, ALU.mult, 1.5, ALU.add))
                link(tt(rr[:, 0:n], rr[:, 0:n], rt[:, 0:n], ALU.mult))

            def square_sum(i):
                link(dve.tensor_tensor_reduce(out=tok[:, i, :], in0=x[:, i, :], in1=x[:, i, :], scale=1.0,
                                              scalar=0.0, op0=ALU.mult, op1=ALU.add,
                                              accum_out=lam_ss[:, i:i + 1]))

            def normalise(L):
                rsqrt(lam_ss[:, 0:T], T, D, EPS)
                for i in range(T):
                    say(ts(tok[:, i, :], x[:, i, :], rr[:, i:i + 1], ALU.mult), xn_s, "xn_s")

            def ada(L):
                for c in range(4):
                    b = take(dve, ("adac", L, c))
                    if c == 0 and L:
                        drained(dve, ("hT", L - 1, KT - 1))
                    release(tt(modc[:, 4 * c:4 * c + 4], b[:, 0:4], bcol[:, L, 4 * c:4 * c + 4], ALU.add),
                            ("adac", L, c))
                say(stt(acol[:, :], modc[:, 8:16], 1.0, gpre[:, L, :], ALU.add, ALU.mult), mod_s, "mod_s")
                for c in range(2):
                    b = take(dve, ("adag", L, c))
                    if c == 0:
                        dve.wait_ge(row_in, 32 * (L + 1))
                    w = slice(512 * c, 512 * c + 512)
                    link(tt(d1[:, :], b[:, :], bgate[:, w], ALU.add))
                    release(tt(grow[:, w], d1[:, :], gpost[:, w], ALU.mult), ("adag", L, c))

            def hT_odd(L):
                for k in range(1, KT, 2):
                    b = take(dve, ("hT", L, k))
                    if L < 2:
                        ins = ts(hT[:, k, :], b[:, :], acol[:, k:k + 1], ALU.mult, modc[:, k:k + 1], ALU.add)
                    else:
                        ins = dve.tensor_copy(hT[:, k, :], b[:, :])
                    release(ins, ("hT", L, k))

            def rope(dst, src, nh, w, cos, sin):
                h = w // 2
                a = d1[:, 0:nh * w].rearrange("p (n w) -> p n w", n=nh)
                b = d2[:, 0:nh * w].rearrange("p (n w) -> p n w", n=nh)
                link(tt(a, src, spread(cos, nh), ALU.mult))
                link(tt(b[:, :, 0:h], src[:, :, h:w], spread(sin[:, 0:h], nh), ALU.mult))
                link(tt(b[:, :, h:w], src[:, :, 0:h], spread(sin[:, h:w], nh), ALU.mult))
                return a, b

            def norm_tile(name, i, width, dst):
                b = take(dve, name)
                hear(sq_s, "sq_s")
                rsqrt(ss[:, 0:1], 1, width, EPS)
                return b, ts(dst, b[:, 0:width], rr[:, 0:1], ALU.mult)

            gates_seen = []

            def exp_gate(name, c0, n):
                b = take(dve, name)
                t = (t1, t2)[len(gates_seen) % 2]
                gates_seen.append(name)
                say(ts(t[:, 0:n], b[:, c0:c0 + n], -CLAMP, ALU.max), sil_c, "sil_c")
                hear(sil_s, "sil_s")
                return b, t

            def silu(name, c0, n, dst):
                b, t = exp_gate(name, c0, n)
                link(ts(t[:, 0:n], t[:, 0:n], 1.0, ALU.add))
                link(dve.reciprocal(t[:, 0:n], t[:, 0:n]))
                release(tt(dst, b[:, c0:c0 + n], t[:, 0:n], ALU.mult), name)

            def finish_group(L, g):
                kind, i, vus = plan[L][g]
                no = g_no[L, g]
                dve.wait_ge(pv_done, last_v[L, g] + 1)
                ob, row = OB[no % 2], no % 16
                if kind in ("mla", "swa", "fox"):
                    den = rsum[:, row, :]
                    if kind == "swa":
                        link(tt(fr[:, 0:NH], den, esink[:, row, :], ALU.add))
                        den = fr[:, 0:NH]
                    link(dve.reciprocal(fr[:, 0:NH], den))
                    o = d1[:, :].rearrange("p (h d) -> p h d", h=NH)
                    link(tt(o, ob[:, :].rearrange("p (h d) -> p h d", h=NH), widen(fr[:, 0:NH], MN), ALU.mult))
                    dst = tok[:, i, 0:512] if kind == "mla" else tok[:, i, 512:1024]
                    give(tt(dst, dst, d1[:, :], ALU.mult), ob_free, no + 1)
                elif kind == "dif":
                    link(dve.reciprocal(fr[:, 0:DH], rsum[:, row, 0:NH:2]))
                    o = d1[:, :].rearrange("p (h d) -> p h d", h=DH)
                    q = d2[:, :].rearrange("p (h d) -> p h d", h=DH)
                    link(tt(o, ob[:, :].rearrange("p (h d) -> p h d", h=DH), widen(fr[:, 0:DH], 2 * MN), ALU.mult))
                    link(tt(d2[:, :], d1[:, :], d1[:, :], ALU.mult))
                    link(dve.tensor_reduce(fr[:, 4:8], q, AX.X, ALU.add))
                    rsqrt(fr[:, 4:8], DH, 2 * MN, EPS)
                    link(tt(o, o, widen(rr[:, 0:DH], 2 * MN), ALU.mult))
                    link(tt(o, o, spread(subln[:, :], DH), ALU.mult))
                    dst = tok[:, i, 0:512]
                    give(tt(dst, dst, d1[:, :], ALU.mult), ob_free, no + 1)
                elif kind == "sb":
                    dst = tok[:, i, 384:640]
                    give(tt(dst, dst, ob[:, 0:256], ALU.mult), ob_free, no + 1)
                else:
                    br = ("cmp", "sel", "win").index(kind)
                    link(dve.reciprocal(fr[:, 0:NSH], rsum[:, row, 0:NSH]))
                    gate = a2["gates"][:, i, br:18:3]
                    link(tt(fr[:, 0:NSH], fr[:, 0:NSH], gate, ALU.mult))
                    o3 = ob[:, 0:384].rearrange("p (h d) -> p h d", h=NSH)
                    if br == 0:
                        acc = d3[:, 0:384].rearrange("p (h d) -> p h d", h=NSH)
                        give(tt(acc, o3, widen(fr[:, 0:NSH], MN), ALU.mult), ob_free, no + 1)
                    else:
                        o = d2[:, 0:384].rearrange("p (h d) -> p h d", h=NSH)
                        link(tt(o, o3, widen(fr[:, 0:NSH], MN), ALU.mult))
                        if br == 1:
                            give(tt(d3[:, 0:384], d3[:, 0:384], d2[:, 0:384], ALU.add), ob_free, no + 1)
                        else:
                            link(tt(d3[:, 0:384], d3[:, 0:384], d2[:, 0:384], ALU.add))
                            dst = tok[:, i, 0:384]
                            give(tt(dst, dst, d3[:, 0:384], ALU.mult), ob_free, no + 1)

            def attention(L):
                pending = []

                def stick_tail():
                    if pending:
                        s = pending.pop()
                        n = score_operands(s_units[s][2])[4]
                        z, l = zm[:, s % 2, 0:n], (t1, t2)[s % 2][:, 0:n]
                        hear(sb_l, "sb_l")
                        link(stt(d1[:, 0:n], z, 0.0, l, ALU.max, ALU.add))
                        link(dve.tensor_tensor_scan(d2[:, 0:n][:, ::-1], d1[:, 0:n][:, ::-1],
                                                    d1[:, 0:n][:, ::-1], 0.0, ALU.add, ALU.bypass))
                        say(stt(z, d2[:, 0:n], -1.0, z, ALU.mult, ALU.add), sb_a, "sb_a")

                for v, (_, g, j, sus), new in steps(L):
                    for s in new:
                        _, sg, su, _ = s_units[s]
                        _, _, mask, scale, n = score_operands(su)
                        row, c = g_no[L, sg] % 16, su[1]
                        if su[0] != "sb":
                            stick_tail()
                        dve.wait_ge(s_done, s + 1)
                        if s >= 2:
                            dve.wait_ge(p_done, s - 1)
                        z = zm[:, s % 2, 0:n]
                        if su[0] == "sb":
                            t = (t1, t2)[s % 2][:, 0:n]
                            link(tt(z, SC[s % 2][:, 0:n], mask, ALU.add))
                            give(stt(t, z, -1.0, z, ALU.mult, ALU.min), masked, s + 1)
                            stick_tail()
                            pending.append(s)
                            continue
                        start = sink[:, 1, c:c + 1] if su[0] == "swa" else 3.0e38
                        give(dve.tensor_tensor_reduce(out=z, in0=SC[s % 2][:, 0:n], in1=mask, scale=-scale,
                                                      scalar=start, op0=ALU.add, op1=ALU.min,
                                                      accum_out=nmax[:, row, c:c + 1]), masked, s + 1)
                    if s_units[-1][0] == L and s_no[sus[-1]] + LOOK >= len(s_units) - 1:
                        stick_tail()
                    s = s_no[sus[-1]]
                    n = score_operands(sus[-1])[4]
                    row = g_no[L, g] % 16
                    if sus[-1][0] == "dif":
                        c = sus[0][1]
                        dve.wait_ge(p_done, s + 1)
                        link(dve.reciprocal(fr[:, 8:9], rsum[:, row, c + 1:c + 2]))
                        link(stt(fr[:, 8:9], fr[:, 8:9], rsum[:, row, c:c + 1], lam[:, 5:6], ALU.mult, ALU.mult))
                        give(stt(pb[:, s % NP, 0:n], pb[:, s % NP, 0:n], fr[:, 8:9], pb[:, (s - 1) % NP, 0:n],
                                 ALU.mult, ALU.add), post, post_no[v] + 1)
                    if sus[-1][0] == "cmp":
                        dve.wait_ge(p_done, s + 1)
                        give(tt(pb[:, s % NP, 0:n], pb[:, s % NP, 0:n], a2["cmpok"][:, plan[L][g][1], :], ALU.mult),
                             post, post_no[v] + 1)
                    if v % 2 == 1:
                        dve.wait_ge(pt_done, v + 1)
                        if v >= 2:
                            dve.wait_ge(pv_done, v - 1)
                        r, w = transposed_shape(sus[-1])
                        give(dve.tensor_copy(pts[0:r, 1, 0:w], PT[1][0:r, 0:w]), pt_ev[1], v // 2 + 1)
                    if v >= 1 and v_units[v - 1][0] == L and last_v[L, v_units[v - 1][1]] == v - 1:
                        finish_group(L, v_units[v - 1][1])
                finish_group(L, len(plan[L]) - 1)

            def out_proj(L):
                for i in range(T):
                    b = take(dve, ("mT", L, i, 1))
                    release(dve.tensor_copy(hT[:, 4:8, i * P:i * P + P], b[:, :].rearrange("p (j t) -> p j t", j=4)),
                            ("mT", L, i, 1))
                for i in range(T):
                    yb = ybuf[:, i % 2, :]
                    for h in range(2):
                        b = take(dve, ("y", L, i, h))
                        w = slice(512 * h, 512 * h + 512)
                        if L == 2:
                            ins = stt(yb[:, w], x[:, i, w], ALPHA, b[:, :], ALU.mult, ALU.add)
                        else:
                            ins = dve.tensor_copy(yb[:, w], b[:, :])
                        release(ins, ("y", L, i, h))
                    hear(sq_s, "sq_s")
                    if L == 2:
                        say(ts(lam[:, 7:8], ss[:, 0:1], -1.0 / D, ALU.mult), mean_s, "mean_s")
                        hear(sq_s, "sq_s")
                        rsqrt(ss[:, 0:1], 1, D, LN_EPS)
                        if i == 0:
                            dve.wait_ge(ln_in, 32)
                        link(ts(yb, yb, lam[:, 7:8], ALU.add, rr[:, 0:1], ALU.mult))
                        link(tt(yb, yb, lng, ALU.mult))
                        say(tt(x[:, i, :], yb, lnb, ALU.add), x_s, "x_s")
                    else:
                        rsqrt(ss[:, 0:1], 1, D, EPS)
                        link(stt(yb, yb, rr[:, 0:1], grow[:, :], ALU.mult, ALU.mult))
                        say(tt(x[:, i, :], x[:, i, :], yb, ALU.add), x_s, "x_s")
                        if L == 0:
                            square_sum(i)

            dve.wait_ge(x_in, 32)
            say(ts(cond[:, :], cT[:, :], -CLAMP, ALU.max), exp_b, "exp_b")
            for i in range(T):
                square_sum(i)
            hear(exp_c, "exp_c")
            link(ts(cond[:, :], cond[:, :], 1.0, ALU.add))
            link(dve.reciprocal(cond[:, :], cond[:, :]))
            say(tt(cond[:, :], cT[:, :], cond[:, :], ALU.mult), cond_s, "cond_s")
            normalise(0)
            dve.wait_ge(c_in, 16 * N_C)
            link(ts(sink[:, 1, :], sink[:, 0, :], -1.0, ALU.mult))
            for n in range(2):
                ins = dve.tensor_tensor_reduce(out=lamr[:, 2 * n, :], in0=lamr[:, 2 * n, :], in1=lamr[:, 2 * n + 1, :],
                                               scale=1.0, scalar=0.0, op0=ALU.mult, op1=ALU.add,
                                               accum_out=lam[:, n:n + 1])
                if n == 0:
                    link(ins)
                else:
                    say(ins, lam_a, "lam_a")
            link(ts(subln[:, :], subln[:, :], 1.0 - LAM_INIT, ALU.mult))
            ada(0)
            hT_odd(0)
            for i in range(T):
                _, ins = norm_tile(("cq", i), i, QL, cqn[:, i, :])
                release(ins, ("cq", i))
            for i in range(T):
                b, ins = norm_tile(("ckv", i), i, KVL, ckvn[:, i, :])
                link(ins)
                kr = b[:, KVL:KVL + RD].rearrange("p (n w) -> p n w", n=1)
                u, w = rope(None, kr, 1, RD, cosl[:, i, :], sinl[:, i, :])
                release(tt(a0["krr"][:, i:i + 1, :], u, w, ALU.add), ("ckv", i))
            for i in range(T):
                if i >= 2:
                    used(dve, ("mqT", i - 2, 1))
                for g in range(2):
                    b = take(dve, ("uq", i, g))[:, 0:384].rearrange("p (h w) -> p h w", h=4)
                    qt = qtok[:, i % 2, 384 * g:384 * g + 384].rearrange("p (h w) -> p h w", h=4)
                    link(dve.tensor_copy(qt[:, :, 0:MN], b[:, :, 0:MN]))
                    u, w = rope(None, b[:, :, MN:MQ], 4, RD, cosl[:, i, :], sinl[:, i, :])
                    release(tt(qt[:, :, MN:MQ], u, w, ALU.add), ("uq", i, g))
            for i in range(T):
                for g in range(2):
                    b = take(dve, ("mkT", i, g))
                    release(dve.tensor_copy(a0["mkT"][:, 4 * g:4 * g + 4, i * P:i * P + P],
                                            b[0:MQ, :].rearrange("p (j t) -> p j t", j=4)), ("mkT", i, g))
            for i in range(T):
                if i >= 2:
                    used(dve, ("sqT", i - 2))
                b = take(dve, ("sq", i))[:, :].rearrange("p (n w) -> p n w", n=NH)
                u, w = rope(None, b, NH, MN, cosh_[:, i, :], sinh_[:, i, :])
                dst = rtok[:, i % 2, :].rearrange("p (j v d) -> p v j d", j=4, v=2)
                four = lambda z: z.rearrange("p (v j) d -> p v j d", v=2)
                for kv in range(2):
                    ins = tt(dst[:, kv, :, :], four(u)[:, kv, :, :], four(w)[:, kv, :, :], ALU.add)
                    if kv == 0:
                        link(ins)
                release(ins, ("sq", i))
            for i in range(T):
                if i >= 2:
                    used(dve, ("skT", i - 2))
                b = take(dve, ("skv", i))
                link(dve.tensor_copy(a0["sV"][:, i, :], b[:, P:2 * P]))
                u, w = rope(None, b[:, 0:P].rearrange("p (n w) -> p n w", n=2), 2, MN, cosh_[:, i, :], sinh_[:, i, :])
                release(tt(rktok[:, i % 2, :].rearrange("p (n w) -> p n w", n=2), u, w, ALU.add), ("skv", i))
            for g in range(2):
                for i in range(T):
                    silu(("gate0", g, i), 0, 512, tok[:, i, 512 * g:512 * g + 512])
            attention(0)
            out_proj(0)
            normalise(1)
            ada(1)
            hT_odd(1)
            for n in ("dq", "dk"):
                for i in range(T):
                    if i >= 2:
                        used(dve, (n + "T", i - 2))
                    b = take(dve, (n, i))[:, :].rearrange("p (n w) -> p n w", n=NH)
                    if n == "dk" and i < 2:
                        used(dve, ("dqT", i + 2))
                    u, w = rope(None, b, NH, MN, cosh_[:, i, :], sinh_[:, i, :])
                    release(tt(rtok[:, i % 2, :].rearrange("p (n w) -> p n w", n=NH), u, w, ALU.add), (n, i))
            hear(lam_b, "lam_b")
            link(tt(lam[:, 4:5], lam[:, 3:4], lam[:, 2:3], ALU.subtract))
            link(ts(lam[:, 5:6], lam[:, 4:5], -LAM_INIT, ALU.add))
            b = take(dve, ("ff",))
            link(ts(d1[0:NH, :], b[0:NH, :], fbias[:, 0:1], ALU.add))
            say(stt(d2[0:NH, :], d1[0:NH, :], -1.0, d1[0:NH, :], ALU.mult, ALU.min), ff_b, "ff_b")
            hear(ff_a, "ff_a")
            link(stt(d3[0:NH, :], d1[0:NH, :], 0.0, d2[0:NH, :], ALU.min, ALU.subtract))
            release(dve.tensor_tensor_scan(frow, d3[0:NH, :], d3[0:NH, :], 0.0, ALU.add, ALU.bypass), ("ff",))
            say(ts(nfrow, frow, -1.0, ALU.mult), frow_s, "frow_s")
            for m in range(4):
                b = take(dve, ("fk", m))
                link(dve.tensor_copy(a1["fkT"][0:MN, 2 * m, :], b[0:MN, :]))
                release(dve.tensor_copy(a1["fkT"][0:MN, 2 * m + 1, :], b[MN:P, :]), ("fk", m))
            for i in range(T):
                b = take(dve, ("fv", i))
                release(dve.tensor_copy(a1["fV"][:, i, :], b[:, :]), ("fv", i))
            for g in range(2):
                for i in range(T):
                    silu(("gate1", g, i), 0, 512, tok[:, i, 512 * g:512 * g + 512])
            attention(1)
            out_proj(1)
            hT_odd(2)
            for r in range(2):
                b = take(dve, ("relrow", r))
                release(dve.tensor_copy(relrow[:, 320 * r:320 * r + 320], b[0:NSH, 0:320]), ("relrow", r))
            for r in range(2):
                b = take(dve, ("relcmp", r))[:, 0:2 * NC * NSH].rearrange("p (i n h) -> p i n h", i=2, n=NC)
                for i in range(2):
                    ins = dve.tensor_copy(a2["Bc"][:, 2 * r + i, :, :].rearrange("p h n -> p n h"), b[:, i, :, :])
                    if i == 0:
                        link(ins)
                release(ins, ("relcmp", r))
            dve.wait_ge(l2_in, 16 * N_L2)
            say(ts(rt[:, 0:1], rt[:, 0:1], 1.0, ALU.mult), relr_s, "relr_s")

            def blocks(n):
                for g in range(NG):
                    src = kvC[n][:, g, 0:S]
                    src = bass.AP(src.tensor, src.offset, [list(src.ap[0]), [2, 16], [CS, NC]])
                    ins = tt(blk[n][:, :, g * NC:g * NC + NC], src, widen(a2["pos2"], NC), ALU.add)
                    if g == 0:
                        link(ins)
                say(ins, blk_s, "blk_s")

            drained(dve, ("vc",))
            blocks("k")
            blocks("v")
            for i in range(T):
                b, t = exp_gate(("vwg", i), P, 18)
                link(ts(t[:, 0:18], t[:, 0:18], 1.0, ALU.add))
                link(dve.reciprocal(a2["gates"][:, i, :], t[:, 0:18]))
                release(dve.tensor_copy(a2["vw"][:, i, :], b[:, 0:P]), ("vwg", i))
            n = NG * NC
            for name, dst in (("ckh", a2["hk"]), ("cvh", a2["hv"])):
                b = take(dve, (name,))
                link(dve.tensor_copy(d1[:, 0:n], b[:, 0:n]))
                link(tt(d2[:, 0:n], d1[:, 0:n], d1[:, 0:n], ALU.mult))
                link(ts(d2[:, 0:n], d2[:, 0:n], 0.044715, ALU.mult, 1.0, ALU.add))
                link(tt(d2[:, 0:n], d2[:, 0:n], d1[:, 0:n], ALU.mult))
                say(ts(d2[:, 0:n], d2[:, 0:n], -CLAMP / 2, ALU.max), ge_b, "ge_b")
                hear(ge_a, "ge_a")
                link(ts(d2[:, 0:n], d2[:, 0:n], 1.0, ALU.add))
                link(dve.reciprocal(d2[:, 0:n], d2[:, 0:n]))
                release(tt(dst, d1[:, 0:n], d2[:, 0:n], ALU.mult), (name,))
            b = take(dve, ("kcT",))
            link(dve.tensor_copy(a2["kcT"][0:MN, :], b[0:MN, 0:NC]))
            release(dve.tensor_copy(a2["kcT"][MN:P, :], b[0:MN, NC:2 * NC]), ("kcT",))
            for g in range(NG):
                b = take(dve, ("vcT", g))
                release(dve.tensor_copy(a2["vc"][:, g, :], b[0:NC, 0:MN]), ("vcT", g))
            for i in range(T):
                silu(("nz", i), 0, 384, tok[:, i, 0:384])
            for i in range(T):
                b = take(dve, ("sbvz", i))
                link(dve.tensor_copy(a2["sbv"][:, i, :], b[:, 0:256]))
                silu(("sbvz", i), 256, 256, tok[:, i, 384:640])
            for m in range(3):
                take(dve, ("hf", m))
                hear(hg_a, "hg_a")
                link(ts(t2[:, :], t1[:, :], CLAMP, ALU.min))
                say(stt(d1[:, :], t1[:, :], -1.0, t1[:, :], ALU.mult, ALU.min), hg_b, "hg_b")
                hear(hg_a, "hg_a")
                link(ts(t2[:, :], t2[:, :], 1.0, ALU.add))
                link(dve.reciprocal(a2["key"][:, m, :], t2[:, :]))
                link(stt(d2[:, :], t1[:, :], 0.0, d1[:, :], ALU.min, ALU.subtract))
                link(ts(d3[:, :], d2[:, :], -1.0, ALU.mult, LOG_FLOOR, ALU.add))
                say(stt(d1[:, :], d2[:, :], LOG_FLOOR, d3[:, :], ALU.subtract, ALU.min), hg_b, "hg_b")
                hear(hg_a, "hg_a")
                link(stt(d3[:, :], d2[:, :], LOG_FLOOR, d1[:, :], ALU.max, ALU.add))
                for c in range(T):
                    t = slice(c * P, c * P + P)
                    ins = dve.tensor_tensor_scan(a2["b"][:, m, t], d3[:, t], d3[:, t], 0.0, ALU.add, ALU.bypass)
                    if c < T - 1:
                        link(ins)
                release(ins, ("hf", m))
            for i in range(T):
                b = take(dve, ("hi", i))
                release(dve.tensor_copy(a2["hi"][:, i, :], b[:, 0:384]), ("hi", i))
            for i in range(T):
                silu(("hz", i), 0, 384, tok[:, i, 640:1024])
            attention(2)

            def halves(v, l, off, ref=False):
                h = 1 << l
                dims = [list(d) for d in v.ap]
                return bass.AP(v.tensor, v.offset + off, [dims[0], dims[1], [2 * h, P // (2 * h)], [0 if ref else 1, h]])

            def differences(c):
                t = slice(c * P, c * P + P)
                bc = a2["b"][:, :, t]
                if c >= 2:
                    dve.wait_ge(g_done, HGH * (c - 1))
                    dve.wait_ge(ho_done, HGH * (c - 1))
                for l in range(NLEV):
                    h = 1 << l
                    yl = Y[c % 2][:, l, :, :]
                    ref = halves(bc, l, h - 1, True)
                    link(tt(halves(yl, l, 0), ref, halves(bc, l, 0), ALU.subtract))
                    link(tt(halves(yl, l, h), halves(bc, l, h), ref, ALU.subtract))
                last = a2["b"][:, :, c * P + P - 1]
                give(tt(kb[c % 2], widen(last, P), bc, ALU.subtract), y_s, c + 1)

            def operands(c):
                t = slice(c * P, c * P + P)
                dve.wait_ge(ye_s, c + 1)
                for l in range(NLEV):
                    h = 1 << l
                    yl = Y[c % 2][:, l, :, :]
                    link(tt(halves(yl, l, 0), halves(yl, l, 0), halves(a2["key"][:, :, t], l, 0), ALU.mult))
                    link(tt(halves(yl, l, h), halves(yl, l, h), halves(a2["hq"][:, :, t], l, h), ALU.mult))
                link(tt(kb[c % 2], kb[c % 2], a2["key"][:, :, t], ALU.mult))
                give(tt(qb[c % 2], qb[c % 2], a2["hq"][:, :, t], ALU.mult), yr_s, c + 1)

            GB = [SC, PT]
            dve.wait_ge(hg_in, 32)
            link(dve.memset(state, 0.0))
            differences(0)
            operands(0)
            for c in range(T):
                if c < T - 1:
                    differences(c + 1)
                for h in range(HGH):
                    n = c * HGH + h
                    dve.wait_ge(g_done, n + 1)
                    if n >= 2:
                        dve.wait_ge(ho_done, n - 1)
                    for r in range(2):
                        ins = tt(gm[n % 2][:, 4 * r:4 * r + 4, :],
                                 GB[n % 2][r][:, :].rearrange("p (l t) -> p l t", l=4),
                                 levels[:, 4 * r:4 * r + 4, :], ALU.mult)
                        if r == 0:
                            link(ins)
                    give(ins, gm_s, n + 1)
                    if h == 2 and c < T - 1:
                        operands(c + 1)
                dve.wait_ge(ho_done, HGH * (c + 1))
                ob = OB[c % 2]
                link(dve.tensor_copy(d1[:, 0:384], ob[:, 0:384]))
                link(tt(d2[:, 0:384], d1[:, 0:384], d1[:, 0:384], ALU.mult))
                link(dve.tensor_reduce(fr[:, 0:HGH], d2[:, 0:384].rearrange("p (h d) -> p h d", h=HGH), AX.X, ALU.add))
                rsqrt(fr[:, 0:HGH], HGH, MN, EPS)
                o = d1[:, 0:384].rearrange("p (h d) -> p h d", h=HGH)
                link(tt(o, o, widen(rr[:, 0:HGH], MN), ALU.mult))
                link(tt(d1[:, 0:384], d1[:, 0:384], hgnorm, ALU.mult))
                dst = tok[:, c, 640:1024]
                give(tt(dst, dst, d1[:, 0:384], ALU.mult), hof, c + 1)
                if c < T - 1:
                    b = take(dve, ("st", c))
                    for m in range(3):
                        for r in range(2):
                            q = slice(MN * r, MN * r + MN)
                            src = b[q, m * P + MN * r:m * P + MN * r + MN]
                            dst = state[q, m, MN * r:MN * r + MN]
                            if c == 0:
                                ins = dve.tensor_copy(dst, src)
                            else:
                                ins = stt(dst, dst, dec[c % 2][q, m:m + 1], src,
                                          ALU.mult, ALU.add)
                            if (m, r) != (2, 1):
                                link(ins)
                    release(ins, ("st", c))
            out_proj(2)


class Ticks:

    def __init__(self):
        self.n = {}

    def next(self, key):
        self.n[key] = self.n.get(key, 0) + 1
        return self.n[key]


def spread(v, n):
    dims = [list(d) for d in v.ap]
    return bass.AP(v.tensor, v.offset, [dims[0], [0, n]] + dims[1:])


def widen(v, n):
    return bass.AP(v.tensor, v.offset, [list(d) for d in v.ap] + [[0, n]])


def transposed_shape(su):
    kind, _, i = su
    if kind == "cmp":
        return NC, P
    if kind == "swa":
        return P, P * (2 if i else 1)
    return P, P * (i + 1)


N_C = 1 + 4 + 4 + 2 + 2 + 1 + 1 + 1 + 1
N_L2 = 9


def kernel(**inputs):
    import concourse.bacc as bacc
    from concourse.bass_utils import run_bass_kernel_spmd

    nc = bacc.Bacc("TRN2", target_bir_lowering=False, num_devices=1)
    arrays, A, C = {}, {}, {}
    for name, a in inputs.items():
        a = np.ascontiguousarray(a)
        arrays[f"in_{name}"] = a
        A[name] = nc.dram_tensor(f"in_{name}", a.shape, mybir.dt.from_np(a.dtype), kind="ExternalInput").ap()
    for name, a in constants().items():
        arrays[f"const_{name}"] = a
        C[name] = nc.dram_tensor(f"const_{name}", a.shape, F32, kind="ExternalInput").ap()
    out = nc.dram_tensor("out_0", (1, S, D), F32, kind="ExternalOutput").ap()
    two_block_kernel(nc, A, C, out)
    r = run_bass_kernel_spmd(nc, [arrays], core_ids=[0])
    return r.results[0]["out_0"]
```

```python
from contextlib import ExitStack
import math

import numpy as np
import concourse.bass as bass
from concourse import mybir

F32 = mybir.dt.float32
ALU = mybir.AluOpType
ACT = mybir.ActivationFunctionType
AX = mybir.AxisListType

P = 128
D = 1024
S = 512
T = S // P
KT = D // P
NEG = -1e30

QL, KVL, RD = 384, 256, 32
NH = 8
MN = 64
MQ = MN + RD
DH = 4
LAM_INIT = 0.8 - 0.6 * math.exp(-0.3 * 1)
EPS = 1e-6
NG, HPG, NSH = 2, 3, 6
CB, CS = 32, 16
NC = (S - CB) // CS + 1
SBH, HGH = 4, 6
ALPHA = 2 ** 0.25
LN_EPS = 1e-5
LOG_FLOOR = float(np.log(np.float32(1e-30)))
CLAMP = 80.0
NLEV = 7

ADA = 3 * D


def bucket_onehots():
    dist = np.arange(-511, 513)
    n = np.maximum(dist, 0)
    large = 16 + (np.log(np.maximum(n, 1).astype(np.float32) / np.float32(16))
                  / np.float32(math.log(128 / 16)) * np.float32(16)).astype(np.int32)
    b = np.where(n < 16, n, np.clip(large, 0, 31))
    b = np.where(dist < 0, 32, b)
    fwd = (np.arange(33)[:, None] == b[None, :]).astype(np.float32)
    return np.ascontiguousarray(fwd[:, 1022:382:-1])


def constants():
    c = {}
    for name, dim in (("head", 64), ("lat", RD)):
        inv = 1.0 / (np.float32(10000.0) ** (np.arange(0, dim, 2, dtype=np.float32) / np.float32(dim)))
        ang = np.arange(S, dtype=np.float32)[:, None] * inv[None, :].astype(np.float32)
        cos, sin = np.cos(ang).astype(np.float32), np.sin(ang).astype(np.float32)
        c[f"cos_{name}"] = np.concatenate([cos, cos], 1)
        c[f"sin_{name}"] = np.concatenate([-sin, sin], 1)
    q, k = np.arange(P)[:, None], np.arange(P)[None, :]
    zero = np.zeros((P, S - P), np.float32)
    c["causal"] = np.concatenate([zero, np.where(k <= q, 0, NEG).astype(np.float32)], 1)
    c["strict"] = np.concatenate([zero, np.where(k < q, 0, NEG).astype(np.float32)], 1)
    c["window"] = np.concatenate([np.where(k > q, 0, NEG), np.where(k <= q, 0, NEG)], 1).astype(np.float32)
    c["ident"] = np.eye(P, dtype=np.float32)
    lev = []
    s, t = np.arange(P)[:, None], np.arange(P)[None, :]
    for l in range(NLEV):
        h = 1 << l
        lev.append((s // (2 * h) == t // (2 * h)) & (s % (2 * h) < h) & (t % (2 * h) >= h))
    lev.append(s == t)
    c["levels"] = np.concatenate(lev, 1).astype(np.float32)
    end = np.arange(NC) * CS + CB - 1
    ok = (np.arange(S)[:, None] >= end[None, :]).astype(np.float32)
    c["cmp_ok"] = ok
    c["onehot_r"] = bucket_onehots()
    return c


FILLERS = [
    [(("w", "gate0", 0), [("gate0", 0, i) for i in range(1, T)]),
     (("w", "gate0", 1), [("gate0", 1, i) for i in range(T)])]
    + [(("ada", *chunk_), [(("adag", chunk_[0], chunk_[1] - 4) if chunk_[1] >= 4 else ("adac", *chunk_))])
       for chunk_ in ((0, 4), (1, 0), (0, 5), (1, 1), (1, 4), (1, 2), (1, 5), (1, 3))],
    [(("w", "gate1", 0), [("gate1", 0, i) for i in range(2, T)]),
     (("w", "ff"), [("ff",)]),
     (("w", "fq"), [("fq", m) for m in range(4)]),
     (("w", "fk"), [("fk", m) for m in range(4)]),
     (("w", "fv"), [("fv", i) for i in range(T)]),
     (("w", "gate1", 1), [("gate1", 1, i) for i in range(T)])],
    [(("w", "nz"), [("nz", i) for i in range(1, T)]),
     (("w", "sbqk"), [("sbq", 0), ("sbq", 1), ("sbk", 0), ("sbk", 1)]),
     (("w", "sbvz"), [("sbvz", i) for i in range(T)]),
     (("w", "hf"), [("hf", m) for m in range(3)]),
     (("w", "hz"), [("hz", i) for i in range(T)]),
     (("w", "hq"), [("hq", m) for m in range(3)]),
     (("w", "hi"), [("hi", i) for i in range(T)])],
]
POOL_ADA = [(1, c) for c in range(4)]
SPREAD = [[(7, 24), (8, 40)], [(15, 15), (4, 31)], [(21, 68), (4, 14)]]
UNITS = {"adac": 4}


def filler_schedule(L):
    names = [t for _, tiles in FILLERS[L] for t in tiles]
    counts, done = [], []
    for n, steps in SPREAD[L]:
        mine, names = names[:n], names[n:]
        ends, total = [], 0
        for t in mine:
            total += UNITS.get(t[0], KT)
            ends.append((total, t))
        at = 0
        for k in range(1, steps + 1):
            upto = total * k // steps
            counts.append(upto - at)
            done.append([t for e, t in ends if at < e <= upto])
            at = upto
    assert not names
    return counts, done


def pr_plan():
    jobs, chunks = [], []

    def chunk(name, names):
        chunks.append(name)
        jobs.extend(names)
        chunk_end[name] = len(jobs)

    chunk_end = {}

    def transposes(name):
        jobs.extend((name, i) for i in range(T))

    def out_proj(L):
        for k in range(T):
            jobs.extend([("mT", L, k, 0), ("mT", L, k, 1)])
        chunks.append(("wo", L, 0))
        chunks.append(("wo", L, 1))
        for i in range(T):
            for h in range(2):
                jobs.append(("y", L, i, h))
        chunk_end[("wo", L, 0)] = chunk_end[("wo", L, 1)] = len(jobs)

    def fillers(L):
        for name, tiles in FILLERS[L]:
            chunk(name, tiles)

    jobs.append(("cols",))
    for c in range(4):
        chunk(("ada", 0, c), [("adac", 0, c)])
    jobs.extend(("hT", 0, k) for k in range(KT))
    chunk(("w", "cq"), [("cq", i) for i in range(T)])
    chunk(("w", "ckv"), [("ckv", i) for i in range(T)])
    transposes("cqT")
    transposes("ckvT")
    for w, t in (("uq", "mqT"), ("ukv", "mkT")):
        u = []
        for i in range(T + 1):
            if i < T:
                u += [(w, i, 0), (w, i, 1)]
            if i >= 1:
                u += [(t, i - 1, 0), (t, i - 1, 1)]
        chunk(("w", w), u)

    def with_transposes(a, b):
        u = []
        for i in range(T):
            u.append((a, i))
            if i >= 1:
                u.append((b, i - 1))
        return u + [(b, T - 1)]

    chunk(("w", "sq"), with_transposes("sq", "sqT"))
    chunk(("w", "skv"), with_transposes("skv", "skT"))
    jobs.append(("gate0", 0, 0))
    fillers(0)
    out_proj(0)
    jobs.extend(("hT", 1, k) for k in range(KT))
    chunk(("w", "dq"), with_transposes("dq", "dqT"))
    chunk(("w", "dk"), with_transposes("dk", "dkT"))
    chunk(("w", "dv"), [("dv", i) for i in range(T)])
    jobs.extend([("gate1", 0, 0), ("gate1", 0, 1)])
    fillers(1)
    out_proj(1)
    jobs.extend(("hT", 2, k) for k in range(KT))
    jobs.append(("relrow", 0))
    jobs.append(("relrow", 1))
    chunk(("w", "kvc"), [("kc",), ("vc",), ("ks",)] + [("vs", i) for i in range(T)])
    chunk(("w", "kw"), [("kw",)] + [("vwg", i) for i in range(T)])
    chunk(("w", "nq"), [("nq", m) for m in range(3)])
    chunk(("w", "ck1"), [("ckh",)])
    chunk(("w", "cv1"), [("cvh",)])
    jobs.extend([("kcT",), ("vcT", 0), ("vcT", 1), ("nz", 0)])
    fillers(2)
    chunks.extend([("wo", 2, 0), ("wo", 2, 1)])
    for c in range(T + 1):
        if c < T - 1:
            jobs.append(("kbT", c))
        if c:
            jobs.extend([("mT", 2, c - 1, 0), ("mT", 2, c - 1, 1), ("y", 2, c - 1, 0), ("y", 2, c - 1, 1)])
        if c < T - 1:
            jobs.append(("st", c))
    chunk_end[("wo", 2, 0)] = chunk_end[("wo", 2, 1)] = len(jobs)
    return jobs, chunks, chunk_end


def attention_plan(L):
    groups = []
    if L == 0:
        for kind in ("mla", "swa"):
            groups += [(kind, i, [[(kind, h, i)] for h in range(NH)]) for i in range(T)]
    elif L == 1:
        groups += [("dif", i, [[("dif", 2 * h, i), ("dif", 2 * h + 1, i)] for h in range(DH)]) for i in range(T)]
        groups += [("fox", i, [[("fox", h, i)] for h in range(NH)]) for i in range(T)]
    else:
        for i in range(T):
            groups += [(kind, i, [[(kind, h, i)] for h in range(NSH)]) for kind in ("cmp", "sel", "win")]
        groups += [("sb", i, [[("sb", h, i)] for h in range(SBH)]) for i in range(T)]
    return groups


OUT_SPREAD = [0, 0, 8, 4, 4, 4, 4]
RING = 3
WCOLS = KT * 512
SIG_CLAMP = 44.0
NP = 4
HG_EARLY = (78, 84)
LOOK = 2

_CONSTS = ["cos_head", "sin_head", "cos_lat", "sin_lat", "causal", "strict", "window", "ident",
           "levels", "cmp_ok", "onehot_r"]


def two_block_kernel(nc, A, C, out):
    jobs, chunks, chunk_end = pr_plan()
    prn = {name: n for n, name in enumerate(jobs)}
    beside = {t for L in range(3) for _, tiles in FILLERS[L] for t in tiles}
    beside |= {("gate0", 0, 0), ("gate1", 0, 0), ("gate1", 0, 1), ("nz", 0)}
    bank_of, nth, per_bank, turn = [], [], [0] * 8, [0, 0]
    for name in jobs:
        few = name in beside or name[0] in ("kbT", "st") or name[:2] in (("mT", 2), ("y", 2))
        b = turn[few] % (2 if few else 8)
        turn[few] += 1
        per_bank[b] += 1
        bank_of.append(b)
        nth.append(per_bank[b])

    with ExitStack() as ctx:
        def sb(name, shape):
            return ctx.enter_context(nc.sbuf_tensor(name, shape, F32))

        def bank(name):
            return ctx.enter_context(nc.psum_tensor(name, [P, 512], F32))

        def sem(name):
            return ctx.enter_context(nc.semaphore(name))

        PR = [bank(f"PR{i}") for i in range(2)]
        SC = [bank(f"SC{i}") for i in range(2)]
        PT = [bank(f"PT{i}") for i in range(2)]
        OB = [bank(f"OB{i}") for i in range(2)]
        JB = PR + SC + PT + OB

        ring = sb("ring", [P, RING, WCOLS])
        x = sb("x", [P, T, D])
        hT = sb("hT", [P, KT, S])
        tok = sb("tok", [P, T, D])
        stage = sb("stage", [P, 3072])
        pts = sb("pts", [P, 2, 512])
        t1 = sb("t1", [P, 512])
        t2 = sb("t2", [P, 512])
        d1 = sb("d1", [P, 512])
        d2 = sb("d2", [P, 512])
        d3 = sb("d3", [P, 512])
        trig = sb("trig", [P, 2 * T * 64])
        cosh_ = trig[:, 0:256].rearrange("p (i d) -> p i d", i=T)
        sinh_ = trig[:, 256:512].rearrange("p (i d) -> p i d", i=T)
        acc = trig[:, 0:384]
        cosl = sb("cosl", [P, T, RD])
        sinl = sb("sinl", [P, T, RD])
        causal = sb("causal", [P, 512])
        window = sb("window", [P, 256])
        ident = sb("ident", [P, P])
        grow = sb("grow", [P, 1024])
        vrows = sb("vrows", [77, P])
        cols = sb("cols", [P, 77])
        cT = cols[:, 0:8]
        bcol = cols[:, 8:40].rearrange("p (l k) -> p l k", l=2)
        gpre = cols[:, 40:56].rearrange("p (l k) -> p l k", l=2)
        qn, kvn, pos2 = cols[:, 56:59], cols[:, 59:61], cols[:, 61:77]
        ones = sb("ones", [P, 1])
        cond = sb("cond", [P, KT])
        modc = sb("modc", [P, 16])
        acol = sb("acol", [P, KT])
        sink = sb("sink", [P, 2, NH])
        ss = sb("ss", [P, 8])
        rv = sb("rv", [P, 8])
        rr = sb("rr", [P, 8])
        rt = sb("rt", [P, 8])
        lamr = sb("lamr", [P, 4, 64])
        lam = sb("lam", [P, 8])
        subln = sb("subln", [P, 2 * MN])
        rsum = sb("rsum", [P, 16, NH])
        nmax = sb("nmax", [P, 16, NH])
        esink = sb("esink", [P, 16, NH])
        fbias = sb("fbias", [NH, 1])
        fr = sb("fr", [P, 16])
        lam_ss = sb("lam_ss", [P, T])

        arena = sb("arena", [P, 17984])

        def carve(sizes):
            at, got = 0, {}
            for name, shape, rows in sizes:
                n = int(np.prod(shape))
                v = arena[0:rows, at:at + n]
                if len(shape) == 2:
                    v = v.rearrange("p (a b) -> p a b", a=shape[0])
                if len(shape) == 3:
                    v = v.rearrange("p (a b c) -> p a b c", a=shape[0], b=shape[1])
                got[name] = v
                at += n
            assert at <= 17600, at
            return got

        a0 = carve([("mqT", (NH, S), MQ), ("mkT", (NH, S), MQ), ("mV", (T, NH * MN), P),
                    ("sqT", (4, S), P), ("skT", (S,), P), ("sV", (T, P), P), ("krr", (T, RD), P),
                    ("cqT", (3, S), P), ("ckvT", (2, S), P)])
        a1 = carve([("dqT", (DH, S), P), ("dkT", (DH, S), P), ("dV", (T, 512), P),
                    ("fqT", (NH, S), MN + 2), ("fkT", (NH, S), MN + 2), ("fV", (T, 512), P)])
        a2 = carve([("nqT", (3, S), P), ("ksT", (S,), P), ("kwT", (S,), P), ("vs", (T, P), P),
                    ("vw", (T, P), P), ("B", (NSH, S), P), ("sbq", (2, S), P), ("sbk", (2, S), P),
                    ("sbv", (T, 256), P), ("hgt", (T * NSH * NC,), P), ("hq", (3, S), P),
                    ("key", (3, S), P), ("b", (3, S), P), ("hi", (T, 384), P),
                    ("gates", (T, 18), P), ("kcT", (NC,), P), ("vc", (NG, MN), NC),
                    ("cmpok", (T, NC), P), ("hk", (NG * NC,), P), ("hv", (NG * NC,), P),
                    ("ck2", (MN,), P), ("cv2", (MN,), P), ("tbl", (NSH,), 33)])
        kvC = {n: arena[:, o:o + 1024].rearrange("p (g t) -> p g t", g=NG)
               for n, o in (("k", 6656), ("v", 7680))}
        onehot_r = arena[0:33, 10472 + 1024:10472 + 1664]
        relrow = arena[0:NSH, 10472 + 1664:10472 + 2304]
        blk = {"k": stage[:, 0:992].rearrange("p (c n) -> p c n", c=16),
               "v": stage[:, 1024:1024 + 992].rearrange("p (c n) -> p c n", c=16)}
        Y = [arena[:, o:o + NLEV * 384].rearrange("p (l m t) -> p l m t", l=NLEV, m=3)
             for o in (0, 2688)]
        spare = ring[:, chunks.index(("w", "hi")) % RING, :]
        qb = [v.rearrange("p (m t) -> p m t", m=3) for v in (arena[:, 5376:5760], spare[:, 2048:2432])]
        kb = [v.rearrange("p (m t) -> p m t", m=3) for v in (arena[:, 5760:6144], spare[:, 2432:2816])]
        gsum = [spare[:, 2816 + P * r:2816 + P * r + P] for r in range(2)]
        ybuf2 = spare[:, 0:2048].rearrange("p (b n) -> p b n", b=2)
        kbT = arena[:, 6144:6528]
        dec = [arena[:, 6528 + 4 * r:6531 + 4 * r] for r in range(2)]
        state = arena[:, 6656:7040].rearrange("p (m e) -> p m e", m=3)
        hgnorm = arena[:, 17600:17984]
        gm = [stage[:, 1024 * r:1024 * r + 1024].rearrange("p (l t) -> p l t", l=8) for r in range(2)]
        levels = grow[:, :].rearrange("p (l t) -> p l t", l=8)
        lng = arena[:, 7680:8704]
        lnb = arena[:, 8704:9728]

        cqn = stage[:, 0:1536].rearrange("p (i n) -> p i n", i=T)
        ckvn = stage[:, 1536:2560].rearrange("p (i n) -> p i n", i=T)
        qtok = stage[:, 0:1536].rearrange("p (b n) -> p b n", b=2)
        ktok = stage[:, 1536:3072].rearrange("p (b n) -> p b n", b=2)
        rtok = stage[:, 0:1024].rearrange("p (b n) -> p b n", b=2)
        rktok = stage[:, 1024:1280].rearrange("p (b n) -> p b n", b=2)
        bgate = arena[:, 13440:14464]
        gpost = arena[:, 14464:15488]
        pool_sums = [arena[:, 15488:16000], arena[:, 17408:17920]]
        grows = [arena[:, 16384:17408], grow]
        zm = stage[:, 0:1024].rearrange("p (b n) -> p b n", b=2)
        pb = stage[:, 1024:3072].rearrange("p (b n) -> p b n", b=NP)
        ybuf = stage[:, 0:2048].rearrange("p (b n) -> p b n", b=2)
        frow = arena[0:NH, 16384:16896]
        nfrow = arena[0:NH, 16896:17408]

        pr_done = sem("pr_done")
        pr_free = [sem(f"pr_free{i}") for i in range(8)]
        w_in = [sem(f"w_in{i}") for i in range(RING)]
        v_in = sem("v_in")
        x_in = sem("x_in")
        c_in = sem("c_in")
        row_in = sem("row_in")
        l1_in = sem("l1_in")
        l2_in = sem("l2_in")
        hg_in = sem("hg_in")
        ln_in = sem("ln_in")
        frow_in = sem("frow_in")
        rel_out = sem("rel_out")
        rel_in = sem("rel_in")
        y_out = sem("y_out")
        act_seq = sem("act_seq")
        dve_seq = sem("dve_seq")
        pool_own = sem("pool_own")
        pool_seq = sem("pool_seq")
        rs_v = sem("rs_v")
        rs_e = sem("rs_e")
        sq_s = sem("sq_s")
        exp_b = sem("exp_b")
        exp_c = sem("exp_c")
        cond_s = sem("cond_s")
        acp_s = sem("acp_s")
        acc_s = sem("acc_s")
        xn_s = sem("xn_s")
        x_s = sem("x_s")
        mod_s = sem("mod_s")
        sil_c = sem("sil_c")
        sil_s = sem("sil_s")
        lam_a = sem("lam_a")
        lam_b = sem("lam_b")
        ff_a = sem("ff_a")
        ff_b = sem("ff_b")
        frow_s = sem("frow_s")
        ybuf_s = sem("ybuf_s")
        mean_s = sem("mean_s")
        relr_s = sem("relr_s")
        blk_s = sem("blk_s")
        ge_a = sem("ge_a")
        ge_b = sem("ge_b")
        hg_a = sem("hg_a")
        hg_b = sem("hg_b")
        hgf = sem("hgf")
        s_done = sem("s_done")
        masked = sem("masked")
        p_done = sem("p_done")
        post = sem("post")
        sb_l = sem("sb_l")
        sb_a = sem("sb_a")
        pt_done = sem("pt_done")
        pt_ev = [sem(f"pt_ev{i}") for i in range(2)]
        pv_done = sem("pv_done")
        ob_free = sem("ob_free")
        y_s = sem("y_s")
        ye_s = sem("ye_s")
        yr_s = sem("yr_s")
        g_done = sem("g_done")
        gm_s = sem("gm_s")
        gs_s = sem("gs_s")
        ho_done = sem("ho_done")
        hof = sem("hof")
        st_s = sem("st_s")
        ln_s = sem("ln_s")

        plan = [attention_plan(L) for L in range(3)]
        s_no, v_no, g_no, last_v = {}, {}, {}, {}
        s_units, v_units = [], []
        for L in range(3):
            for g, (kind, i, vus) in enumerate(plan[L]):
                for j, sus in enumerate(vus):
                    v_no[L, g, j] = len(v_units)
                    for su in sus:
                        s_no[su] = len(s_units)
                        s_units.append((L, g, su, len(v_units)))
                    v_units.append((L, g, j, sus))
                g_no[L, g] = len(g_no)
                last_v[L, g] = len(v_units) - 1

        post_no = {}
        for v, e in enumerate(v_units):
            if e[3][0][0] in ("dif", "cmp"):
                post_no[v] = len(post_no)

        def steps(L):
            mine = [v for v, e in enumerate(v_units) if e[0] == L]
            s_all = [s for s, e in enumerate(s_units) if e[0] == L]
            nxt = s_all[0]
            for v in mine:
                need = s_no[v_units[v][3][-1]]
                upto = min(need + LOOK, s_all[-1])
                new = list(range(nxt, upto + 1))
                nxt = max(nxt, upto + 1)
                yield v, v_units[v], new

        def score_operands(su):
            kind, h, i = su
            q = slice(i * P, i * P + P)
            nk = (i + 1) * P
            tail = slice(S - nk, S)
            if kind == "mla":
                return a0["mqT"][:, h, q], a0["mkT"][:, h, 0:nk], causal[:, tail], MQ ** -0.5, nk
            if kind == "swa":
                r, j = 64 * (h // 4), h % 4
                k0 = max(i - 1, 0) * P
                return (a0["sqT"][r:r + 64, j, q], a0["skT"][r:r + 64, k0:nk],
                        window[:, 256 - (nk - k0):256], MN ** -0.5, nk - k0)
            if kind == "dif":
                r = 64 * (h % 2)
                return (a1["dqT"][r:r + 64, h // 2, q], a1["dkT"][r:r + 64, h // 2, 0:nk],
                        causal[:, tail], MN ** -0.5, nk)
            if kind == "fox":
                return a1["fqT"][:, h, q], a1["fkT"][:, h, 0:nk], causal[:, tail], 1.0, nk
            r, m = 64 * (h // HPG), h % HPG
            if kind == "cmp":
                return a2["nqT"][r:r + 64, m, q], a2["kcT"][r:r + 64, 0:blocks_seen(i)], a2["B"][:, h, S - nk + CB - 1::CS], 1.0, blocks_seen(i)
            if kind in ("sel", "win"):
                k = a2["ksT" if kind == "sel" else "kwT"]
                return a2["nqT"][r:r + 64, m, q], k[r:r + 64, 0:nk], a2["B"][:, h, tail], 1.0, nk
            r = 64 * (h % 2)
            return a2["sbq"][r:r + 64, h // 2, q], a2["sbk"][r:r + 64, h // 2, 0:nk], causal[:, tail], 1.0, nk

        def value_blocks(su):
            kind, h, i = su
            if kind == "mla":
                return [a0["mV"][:, k, h * 64:h * 64 + 64] for k in range(i + 1)]
            if kind == "swa":
                r = 64 * (h // 4)
                return [a0["sV"][:, k, r:r + 64] for k in range(max(i - 1, 0), i + 1)]
            if kind == "dif":
                return [a1["dV"][:, k, (h // 2) * P:(h // 2) * P + P] for k in range(i + 1)]
            if kind == "fox":
                return [a1["fV"][:, k, h * 64:h * 64 + 64] for k in range(i + 1)]
            if kind == "cmp":
                return [a2["vc"][0:blocks_seen(i), h // HPG, :]]
            if kind in ("sel", "win"):
                v, r = a2["vs" if kind == "sel" else "vw"], 64 * (h // HPG)
                return [v[:, k, r:r + 64] for k in range(i + 1)]
            return [a2["sbv"][:, k, h * 64:h * 64 + 64] for k in range(i + 1)]

        def take(eng, name):
            p = prn[name]
            eng.wait_ge(pr_done, p + 1)
            return JB[bank_of[p]]

        def drained(eng, name):
            p = prn[name]
            for b in range(8):
                got = [q for q in range(max(0, p - 15), p + 1) if bank_of[q] == b]
                if got:
                    eng.wait_ge(pr_free[b], nth[got[-1]])

        def banks_back(eng, name):
            for b in range(2, 8):
                last = [q for q in range(prn[name] + 1) if bank_of[q] == b][-1]
                eng.wait_ge(pr_free[b], nth[last])

        def used(eng, name):
            eng.wait_ge(pr_done, prn[name] + 1)

        OFF1 = {n: o for n, o in zip(("dq", "dk", "dv", "fq", "fk", "fv", "ff", "gate"),
                                     (0, 512, 1024, 1536, 2048, 2560, 3072, 3080))}

        def wsrc(w, c0, n):
            return w[:, c0:c0 + n].rearrange("(k p) n -> p k n", p=P)

        def chunk_parts(name):
            kind = name[0]
            if kind == "ada":
                return KT, 512, [(slice(0, 512), wsrc(A["w_ada"][name[1]], 512 * name[2], 512))]
            if kind == "wo":
                w = {0: A["ev_w_out"][0], 1: A["od_w_out"][0], 2: A["w_out_2"][0]}[name[1]]
                return KT, 512, [(slice(0, 512), wsrc(w, 512 * name[2], 512))]
            n = name[1]
            ev, od, w2 = A["ev_w_in"][0], A["od_w_in"][0], A["w_in_2"][0]
            if n in ("uq", "ukv"):
                w = A["ev_w_uq"][0] if n == "uq" else A["ev_w_ukv"][0]
                return w.shape[0] // P, w.shape[1], [(slice(0, w.shape[1]), wsrc(w, 0, w.shape[1]))]
            if n in ("ck1", "cv1"):
                w = A["w_ck1_2" if n == "ck1" else "w_cv1_2"][0]
                return 16, P, [(slice(0, P), wsrc(w, 0, P))]
            if n == "nq":
                w = w2[:, 0:384].rearrange("(k p) (g m d) -> m p k g d", p=P, g=NG, m=3)
                return KT, 384, [((m, g), w[m][:, :, g, :]) for m in range(3) for g in range(NG)]
            at = {"cq": (ev, 0, 384), "ckv": (ev, 384, 288), "sq": (ev, 672, 512), "skv": (ev, 1184, 256),
                  "kvc": (w2, 384, 512), "kw": (w2, 896, 274), "nz": (w2, 1170, 384),
                  "sbqk": (w2, 1554, 512), "sbvz": (w2, 2066, 512), "hq": (w2, 2578, 384),
                  "hf": (w2, 2962, 384), "hi": (w2, 3346, 384), "hz": (w2, 3730, 384)}
            if n in at:
                w, c0, n_ = at[n]
            elif n == "gate0":
                w, c0, n_ = ev, 1440 + 512 * name[2], 512
            elif n == "gate1":
                w, c0, n_ = od, OFF1["gate"] + 512 * name[2], 512
            else:
                w, c0, n_ = od, OFF1[n], 8 if n == "ff" else 512
            return KT, n_, [(slice(0, n_), wsrc(w, c0, n_))]

        schedule = [filler_schedule(L) for L in range(3)]
        chunk_of = {t: c for L in range(3) for c, tiles in FILLERS[L] for t in tiles}
        for name in (("gate0", 0, 0), ("gate1", 0, 0), ("gate1", 0, 1), ("nz", 0)):
            chunk_of[name] = ("w",) + name[:-1]
        chunk_no = {c: n for n, c in enumerate(chunks)}
        w_val, w_view, filled = {}, {}, [0] * RING
        for n, c in enumerate(chunks):
            K, width, parts = chunk_parts(c)
            filled[n % RING] += 16 * len(parts)
            w_val[c] = filled[n % RING]
            w_view[c] = ring[:, n % RING, 0:K * width].rearrange("p (k n) -> p k n", k=K)

        def rows(ap, n, at=0):
            return bass.AP(ap.tensor, ap.offset + at, [[0, P], [1, n]])

        scr = nc.dram_tensor("rel_rows", [NSH, P, 640], F32, kind="Internal").ap()
        block = ctx.enter_context(nc.Block())

        @block.sync
        def _(sp):
            sp.wait_ge(v_in, 16 * N_V)
            for n, c in enumerate(chunks):
                if n >= RING:
                    sp.wait_ge(pr_done, chunk_end[chunks[n - RING]])
                if c == ("w", "gate0", 0):
                    used(sp, ("ukv", T - 1, 1))
                    sp.dma_start(bgate, rows(A["b_ada"], D, 2 * D)).then_inc(row_in, 16)
                    sp.dma_start(gpost, rows(A["g_post"], D)).then_inc(row_in, 16)
                if c == ("ada", 1, 4):
                    drained(sp, ("adag", 0, 1))
                    sp.dma_start(bgate, rows(A["b_ada"], D, ADA + 2 * D)).then_inc(row_in, 16)
                    sp.dma_start(gpost, rows(A["g_post"], D, D)).then_inc(row_in, 16)
                for where, src in chunk_parts(c)[2]:
                    if isinstance(where, tuple):
                        dst = w_view[c][:, :, where[0] * P + where[1] * MN:where[0] * P + where[1] * MN + MN]
                    else:
                        dst = w_view[c][:, :, where]
                    sp.dma_start(dst, src).then_inc(w_in[n % RING], 16)
                if c == ("w", "cv1"):
                    sp.wait_ge(relr_s, 1)
                    sp.dma_start(scr, spread(relrow, P)).then_inc(rel_out, 16)
                    sp.wait_ge(rel_out, 16)
                    sp.dma_start(a2["B"], bass.AP(scr.tensor, scr.offset + P - 1,
                                                  [[639, P], [640 * P, NSH], [1, S]])).then_inc(rel_in, 16)
            for i in range(T):
                sp.wait_ge(x_s, 2 * T + i + 1)
                sp.dma_start(out[0, i * P:i * P + P, :], x[:, i, :]).then_inc(y_out, 16)
            sp.wait_ge(y_out, 16 * T)

        @block.tensor
        def _(pe):
            count = [0]

            def begin(name):
                p = prn[name]
                assert p == count[0], (name, p, count[0])
                count[0] += 1
                if nth[p] > 1:
                    pe.wait_ge(pr_free[bank_of[p]], nth[p] - 1)
                return JB[bank_of[p]]

            def weights(c):
                pe.wait_ge(w_in[chunk_no[c] % RING], w_val[c])
                return w_view[c]

            def contract(dst, lhs, rhs, K):
                for k in range(K):
                    mm = pe.matmul(dst, lhs(k), rhs(k), start=(k == 0), stop=(k == K - 1))
                return mm

            def token_major(name, W, i, c0, n, src=hT, K=KT):
                b = begin(name)
                contract(b[:, 0:n], lambda k: src[:, k, i * P:i * P + P], lambda k: W[:, k, c0:c0 + n],
                         K).then_inc(pr_done, 1)

            def feature_major(name, W, c0, m=P):
                b = begin(name)
                contract(b[0:m, :], lambda k: W[:, k, c0:c0 + m], lambda k: hT[:, k, :], KT).then_inc(pr_done, 1)

            def transposes(name, srcs, m=P):
                b = begin(name)
                for j, s in enumerate(srcs):
                    tr = pe.transpose(b[0:m, j * P:j * P + P], s, ident[:, :])
                tr.then_inc(pr_done, 1)

            FEATURE = {"fq": P, "fk": P, "ff": NH, "sbq": P, "sbk": P, "hf": P, "hq": P}
            WIDTH = {"nz": 384, "hi": 384, "hz": 384}

            def tile_matmuls(name):
                kind = name[0]
                W = None if kind == "adac" else weights(chunk_of[name])
                b = begin(name)
                if kind == "adac":
                    n = POOL_ADA.index(name[1:])
                    pe.wait_ge(acp_s, n + 1)
                    for m in range(4):
                        mm = pe.matmul(b[:, m:m + 1], pool_sums[n % 2][:, m * P:m * P + P], ones[:, :],
                                       start=True, stop=True)
                        if m == 3:
                            mm.then_inc(pr_done, 1)
                        yield
                    return
                for k in range(KT):
                    w = W[:, k, :]
                    if kind == "adag":
                        dst, l, r = b[:, :], cond[:, k:k + 1].to_broadcast([P, P]), w
                    elif kind in FEATURE:
                        m = name[1] if len(name) > 1 else 0
                        c0 = (m + 2 * (kind == "sbk")) * P
                        dst, l, r = b[0:FEATURE[kind], :], w[:, c0:c0 + FEATURE[kind]], hT[:, k, :]
                    else:
                        n, i = WIDTH.get(kind, 512), name[-1]
                        dst, l, r = b[:, 0:n], hT[:, k, i * P:i * P + P], w[:, 0:n]
                    mm = pe.matmul(dst, l, r, start=(k == 0), stop=(k == KT - 1))
                    if k == KT - 1:
                        mm.then_inc(pr_done, 1)
                    yield

            def whole_tile(name):
                for _ in tile_matmuls(name):
                    pass

            def make_hT(L):
                src = x if L == 2 else tok
                for k in range(KT):
                    if k == 0:
                        if L == 2:
                            pe.wait_ge(x_s, 2 * T)
                        else:
                            pe.wait_ge(xn_s, T * (L + 1))
                    transposes(("hT", L, k), [src[:, i, k * P:k * P + P] for i in range(T)])
                drained(pe, ("hT", L, KT - 1))

            def attention(L):
                def values(v):
                    L_, g, j, sus = v_units[v]
                    su = sus[-1]
                    ob = OB[g_no[L, g] % 2]
                    if j == 0 and g_no[L, g] >= 2:
                        pe.wait_ge(ob_free, g_no[L, g] - 1)
                    pe.wait_ge(pt_ev[v % 2], v // 2 + 1)
                    blocks = value_blocks(su)
                    w = 128 if su[0] == "dif" else 64
                    h = su[1] // 2 if su[0] == "dif" else su[1]
                    for n, vb in enumerate(blocks):
                        rows_ = blocks_seen(su[2]) if su[0] == "cmp" else P
                        mm = pe.matmul(ob[:, h * w:h * w + w], pts[0:rows_, v % 2, n * P:n * P + P], vb,
                                       start=(n == 0), stop=(n == len(blocks) - 1))
                    mm.then_inc(pv_done, 1)

                first = True
                counts, _ = schedule[L]
                fill = (None for _, tiles in FILLERS[L] for t in tiles for _ in tile_matmuls(t))

                def filler(n):
                    for _ in range(n):
                        next(fill)

                for r, (v, (_, g, j, sus), new) in enumerate(steps(L)):
                    for s in new:
                        if s_units[s][2] == ("fox", 0, 0):
                            drained(pe, ("fv", T - 1))
                            pe.wait_ge(frow_in, 32 * NH)
                        if s_units[s][2] == ("sb", 0, 0):
                            drained(pe, ("sbvz", T - 1))
                        if s >= 2:
                            pe.wait_ge(masked, s - 1)
                        q, k, _, _, n = score_operands(s_units[s][2])
                        pe.matmul(SC[s % 2][:, 0:n], q, k, start=True, stop=True).then_inc(s_done, 1)
                    more = counts[r] if r < len(counts) else 0
                    filler(more // 2)
                    su = sus[-1]
                    s = s_no[su]
                    if su[0] in ("dif", "cmp"):
                        pe.wait_ge(post, post_no[v] + 1)
                    else:
                        pe.wait_ge(p_done, s + 1)
                    if v >= 2:
                        pe.wait_ge(pt_ev[v % 2], v // 2)
                    n = score_operands(su)[4]
                    nb = -(-n // P)
                    for b in range(nb):
                        w = min(P, n - b * P)
                        tr = pe.transpose(PT[v % 2][0:w, b * P:b * P + P], pb[:, s % NP, b * P:b * P + w],
                                          ident[:, :])
                    tr.then_inc(pt_done, 1)
                    filler(more - more // 2)
                    if not first:
                        values(v - 1)
                    first = False
                values(v)

            def output_tile(i):
                for g in range(2):
                    b = begin(("mT", 2, i, g))
                    for j in range(4):
                        if (g, j) == (0, 0):
                            pe.wait_ge(hof, i + 1)
                        tr = pe.transpose(b[:, j * P:j * P + P], tok[:, i, (4 * g + j) * P:(4 * g + j + 1) * P],
                                          ident[:, :])
                        if j == 3:
                            tr.then_inc(pr_done, 1)
                        yield
                drained(pe, ("mT", 2, i, 1))
                for h in range(2):
                    W = weights(("wo", 2, h))
                    b = begin(("y", 2, i, h))
                    for k in range(KT):
                        mm = pe.matmul(b[:, :], hT[:, k, i * P:i * P + P], W[:, k, :], start=(k == 0), stop=(k == KT - 1))
                        if k == KT - 1:
                            mm.then_inc(pr_done, 1)
                        yield

            def out_proj(L):
                pe.wait_ge(ob_free, g_no[L, len(plan[L]) - 1] + 1)
                pe.wait_ge(masked, sum(e[0] <= L for e in s_units))
                for r in range(2):
                    pe.wait_ge(pt_ev[r], (sum(e[0] <= L for e in v_units) + 1 - r) // 2)
                for i in range(T):
                    for g in range(2):
                        transposes(("mT", L, i, g), [tok[:, i, (4 * g + j) * P:(4 * g + j + 1) * P] for j in range(4)])
                drained(pe, ("mT", L, T - 1, 1))
                W = [weights(("wo", L, h)) for h in range(2)]
                for i in range(T):
                    for h in range(2):
                        token_major(("y", L, i, h), W[h], i, 0, 512)

            pe.wait_ge(v_in, 16 * N_V)
            b = begin(("cols",))
            pe.transpose(b[:, 0:77], vrows[:, :], ident[0:77, 0:77]).then_inc(pr_done, 1)
            pe.wait_ge(pool_seq, 1)
            for c in range(4):
                pe.wait_ge(acc_s, c + 1)
                b = begin(("adac", 0, c))
                for m in range(4):
                    mm = pe.matmul(b[:, m:m + 1], (d1, d2)[c % 2][:, m * P:m * P + P], ones[:, :],
                                   start=True, stop=True)
                mm.then_inc(pr_done, 1)
            make_hT(0)
            W = weights(("w", "cq"))
            for i in range(T):
                token_major(("cq", i), W, i, 0, 384)
            W = weights(("w", "ckv"))
            for i in range(T):
                token_major(("ckv", i), W, i, 0, 288)
            for i in range(T):
                if i == 0:
                    drained(pe, ("ckv", T - 1))
                transposes(("cqT", i), [cqn[:, i, k * P:k * P + P] for k in range(3)])
            for i in range(T):
                transposes(("ckvT", i), [ckvn[:, i, k * P:k * P + P] for k in range(2)])
            drained(pe, ("ckvT", T - 1))
            for w, src, K, n, tr_name, tile in (("uq", a0["cqT"], 3, 384, "mqT", qtok),
                                                ("ukv", a0["ckvT"], 2, 512, "mkT", ktok)):
                W = weights(("w", w))
                for i in range(T + 1):
                    if i < T:
                        for g in range(2):
                            token_major((w, i, g), W, i, n * g, n, src, K)
                    if i >= 1:
                        drained(pe, (w, i - 1, 1))
                        for g in range(2):
                            transposes((tr_name, i - 1, g),
                                       [tile[:, (i - 1) % 2, (4 * g + j) * MQ:(4 * g + j + 1) * MQ] for j in range(4)], MQ)

            def roped(name, n, nt, tile):
                W = weights(("w", name[0]))
                for i in range(T + 1):
                    if i < T:
                        token_major((name[0], i), W, i, 0, n)
                    if i >= 1:
                        drained(pe, (name[0], i - 1))
                        transposes((name[1], i - 1), [tile[:, (i - 1) % 2, k * P:k * P + P] for k in range(nt)])

            roped(("sq", "sqT"), 512, 4, rtok)
            roped(("skv", "skT"), 256, 1, rktok)
            whole_tile(("gate0", 0, 0))
            banks_back(pe, ("gate0", 0, 0))
            attention(0)
            out_proj(0)
            make_hT(1)
            roped(("dq", "dqT"), 512, 4, rtok)
            roped(("dk", "dkT"), 512, 4, rtok)
            W = weights(("w", "dv"))
            for i in range(T):
                token_major(("dv", i), W, i, 0, 512)
            whole_tile(("gate1", 0, 0))
            whole_tile(("gate1", 0, 1))
            banks_back(pe, ("gate1", 0, 1))
            attention(1)
            out_proj(1)
            make_hT(2)
            pe.wait_ge(l2_in, 16 * N_L2)
            pe.wait_ge(pool_seq, 4)
            for r in range(2):
                b = begin(("relrow", r))
                pe.matmul(b[0:NSH, 0:320], a2["tbl"][:, 0:NSH], onehot_r[:, 320 * r:320 * r + 320],
                          start=True, stop=True).then_inc(pr_done, 1)
            W = weights(("w", "kvc"))
            for n, name in enumerate((("kc",), ("vc",), ("ks",))):
                feature_major(name, W, n * P)
            for i in range(T):
                token_major(("vs", i), W, i, 384, P)
            W = weights(("w", "kw"))
            feature_major(("kw",), W, 0)
            for i in range(T):
                token_major(("vwg", i), W, i, P, 146)
            W = weights(("w", "nq"))
            for m in range(3):
                feature_major(("nq", m), W, m * P)
            for n, name in (("k", "ckh"), ("v", "cvh")):
                W = weights(("w", f"c{n}1"))
                pe.wait_ge(blk_s, 1 if n == "k" else 2)
                b = begin((name,))
                contract(b[:, 0:NG * NC], lambda k: W[:, k, :], lambda k: blk[n][:, k, :], 16).then_inc(pr_done, 1)
            drained(pe, ("cvh",))
            b = begin(("kcT",))
            pe.matmul(b[0:MN, 0:NG * NC], a2["ck2"], a2["hk"], start=True, stop=True).then_inc(pr_done, 1)
            for g in range(NG):
                b = begin(("vcT", g))
                pe.matmul(b[0:NC, 0:MN], a2["hv"][:, g * NC:g * NC + NC], a2["cv2"],
                          start=True, stop=True).then_inc(pr_done, 1)
            whole_tile(("nz", 0))
            pe.wait_ge(rel_in, 16)
            banks_back(pe, ("nz", 0))
            attention(2)

            drained(pe, ("hi", T - 1))
            pe.wait_ge(ob_free, len(g_no))
            pe.wait_ge(masked, len(s_units))
            for r in range(2):
                pe.wait_ge(pt_ev[r], (len(v_units) + 1 - r) // 2)
            GB = [SC, PT]
            for c in range(T):
                t = slice(c * P, c * P + P)
                pe.wait_ge(yr_s, c + 1)
                if c < T - 1:
                    transposes(("kbT", c), [kb[c % 2][:, m, :] for m in range(3)])

                def level_products(h):
                    n = c * HGH + h
                    m, r = h // 2, 64 * (h % 2)
                    if n >= 2:
                        pe.wait_ge(gm_s, n - 1)
                    for l in range(8):
                        dst = GB[n % 2][l // 4][:, (l % 4) * P:(l % 4 + 1) * P]
                        if l < NLEV:
                            a = b_ = Y[c % 2][r:r + 64, l, m, :]
                        else:
                            a, b_ = a2["key"][r:r + 64, m, t], a2["hq"][r:r + 64, m, t]
                        mm = pe.matmul(dst, a, b_, start=True, stop=True)
                    mm.then_inc(g_done, 1)

                def outputs(h):
                    n = c * HGH + h
                    m, r = h // 2, 64 * (h % 2)
                    ob = OB[c % 2][:, h * MN:h * MN + MN]
                    if h == 0:
                        if c >= 2:
                            pe.wait_ge(hof, c - 1)
                        if c > 0:
                            drained(pe, ("st", c - 1))
                    if c > 0 and h % 2 == 0:
                        pe.matmul(OB[c % 2][:, m * P:m * P + P], qb[c % 2][:, m, :], state[:, m, :],
                                  start=True, stop=False)
                    pe.wait_ge(gs_s, n + 1)
                    pe.matmul(ob, gsum[n % 2], a2["hi"][:, c, h * MN:h * MN + MN],
                              start=(c == 0), stop=(c == 0 or h % 2 == 1)).then_inc(ho_done, 1)

                beside_it = output_tile(c - 1) if c else iter(())
                for h in range(HGH + 1):
                    if h < HGH:
                        level_products(h)
                    for _ in range(OUT_SPREAD[h]):
                        next(beside_it, None)
                    if h >= 1:
                        outputs(h - 1)
                for _ in beside_it:
                    pass
                if c < T - 1:
                    drained(pe, ("kbT", c))
                    b = begin(("st", c))
                    for m in range(3):
                        mm = pe.matmul(b[:, m * P:m * P + P], kbT[:, m * P:m * P + P],
                                       a2["hi"][:, c, m * P:m * P + P], start=True, stop=True)
                    mm.then_inc(pr_done, 1)
            for _ in output_tile(T - 1):
                pass

        @block.scalar
        def _(act):
            seen = Ticks()

            def link(ins):
                n = seen.next("act_seq")
                ins.then_inc(act_seq, 1)
                act.wait_ge(act_seq, n)

            def give(ins, s, value):
                ins.then_inc(s, 1)
                act.wait_ge(s, value)

            def release(ins, name):
                p = prn[name]
                give(ins, pr_free[bank_of[p]], nth[p])

            def hear(s, key):
                act.wait_ge(s, seen.next(key))

            def say(ins, s, key):
                give(ins, s, seen.next(key))

            def copy(dst, src, scale=1.0):
                return act.activation(dst, src, ACT.Copy, scale=scale)

            def rsqrt(n=1):
                hear(rs_v, "rs_v")
                link(act.activation(rr[:, 0:n], rv[:, 0:n], ACT.Ln))
                say(act.activation(rr[:, 0:n], rr[:, 0:n], ACT.Exp, scale=-0.5), rs_e, "rs_e")

            def token_square(name, n):
                b = take(act, name)
                say(act.activation(t1[:, 0:n], b[:, 0:n], ACT.Square, accum_out=ss[:, 0:1]), sq_s, "sq_s")
                rsqrt()

            gates_seen = []

            def exp_neg(name, n):
                t = (t1, t2)[len(gates_seen) % 2][:, 0:n]
                gates_seen.append(name)
                hear(sil_c, "sil_c")
                link(act.activation(t, t, ACT.Exp, scale=-1.0))
                link(act.activation(t, t, ACT.Ln, bias=1.0))
                say(act.activation(t, t, ACT.Exp, scale=-1.0), sil_s, "sil_s")

            def heads(v, j=4):
                return v.rearrange("p (j t) -> p j t", j=j)

            def hT_even(L):
                if L < 2:
                    act.wait_ge(mod_s, L + 1)
                for k in range(0, KT, 2):
                    b = take(act, ("hT", L, k))
                    if L < 2:
                        ins = act.activation(hT[:, k, :], b[:, :], ACT.Identity, scale=acol[:, k:k + 1],
                                             bias=modc[:, k:k + 1])
                    else:
                        ins = copy(hT[:, k, :], b[:, :])
                    release(ins, ("hT", L, k))

            def tile_done(name):
                kind = name[0]
                if kind in ("gate0", "gate1"):
                    exp_neg(name, 512)
                elif kind in ("nz", "hz"):
                    exp_neg(name, 384)
                elif kind == "sbvz":
                    exp_neg(name, 256)
                elif kind == "ff":
                    act.wait_ge(ff_b, 1)
                    link(act.activation(d2[0:NH, :], d2[0:NH, :], ACT.Exp))
                    say(act.activation(d2[0:NH, :], d2[0:NH, :], ACT.Ln, bias=1.0), ff_a, "ff_a")
                    act.wait_ge(frow_s, 1)
                    act.wait_ge(pool_seq, 3)
                    for h in range(NH):
                        act.dma_start(a1["fqT"][MN + 1:MN + 2, h, :], frow[h:h + 1, :]).then_inc(frow_in, 16)
                        act.dma_start(a1["fkT"][MN:MN + 1, h, :], nfrow[h:h + 1, :]).then_inc(frow_in, 16)
                elif kind == "fq":
                    m = name[1]
                    b = take(act, name)
                    link(copy(a1["fqT"][0:MN, 2 * m, :], b[0:MN, :], MN ** -0.5))
                    release(copy(a1["fqT"][0:MN, 2 * m + 1, :], b[MN:P, :], MN ** -0.5), name)
                elif kind in ("sbq", "sbk"):
                    b = take(act, name)
                    release(copy(a2[kind][:, name[1], :], b[:, :], MN ** -0.5 if kind == "sbq" else 1.0), name)
                elif kind == "hq":
                    b = take(act, name)
                    release(copy(a2["hq"][:, name[1], :], b[:, :]), name)
                elif kind == "hf":
                    forget.append(forget_tile(name[1]))

            forget = []

            def forget_tile(m):
                key, u = a2["key"][:, m, :], a2["b"][:, m, :]
                b = take(act, ("hf", m))
                release(copy(a2["hq"][:, m, :], b[:, :]), ("hf", m))
                yield
                for n in range(2):
                    hear(hg_b, "hg_b")
                    if n == 0:
                        link(act.activation(key, key, ACT.Exp))
                    link(act.activation(u, u, ACT.Exp))
                    say(act.activation(u, u, ACT.Ln, bias=1.0), hg_a, "hg_a")
                    yield

            def attention(L):
                pending = []

                def stick_tail():
                    if pending:
                        s = pending.pop()
                        n = score_operands(s_units[s][2])[4]
                        hear(sb_a, "sb_a")
                        give(act.activation(pb[:, s % NP, 0:n], zm[:, s % 2, 0:n], ACT.Exp), p_done, s + 1)

                for r_, (v, (_, g, j, sus), new) in enumerate(steps(L)):
                    for s in new:
                        _, sg, su, _ = s_units[s]
                        n = score_operands(su)[4]
                        c = su[1]
                        row = g_no[L, sg] % 16
                        if su[0] != "sb":
                            stick_tail()
                        act.wait_ge(masked, s + 1)
                        if s >= NP:
                            act.wait_ge(pt_done, s_units[s - NP][3] + 1)
                        if su[0] == "sb":
                            t = (t1, t2)[s % 2][:, 0:n]
                            link(act.activation(t, zm[:, s % 2, 0:n], ACT.Abs))
                            link(act.activation(t, t, ACT.Exp, scale=-1.0))
                            say(act.activation(t, t, ACT.Ln, bias=1.0), sb_l, "sb_l")
                            stick_tail()
                            pending.append(s)
                            continue
                        give(act.activation(pb[:, s % NP, 0:n], zm[:, s % 2, 0:n], ACT.Exp,
                                            bias=nmax[:, row, c:c + 1], scale=-1.0,
                                            accum_out=rsum[:, row, c:c + 1]), p_done, s + 1)
                        if su[0] == "swa":
                            link(act.activation(esink[:, row, c:c + 1], sink[:, 0, c:c + 1], ACT.Exp,
                                                bias=nmax[:, row, c:c + 1]))
                    if s_units[-1][0] == L and s_no[sus[-1]] + LOOK >= len(s_units) - 1:
                        stick_tail()
                    act.wait_ge(pt_done, v + 1)
                    if v >= 2:
                        act.wait_ge(pv_done, v - 1)
                    r, w = transposed_shape(sus[-1])
                    give(copy(pts[0:r, v % 2, 0:w], PT[v % 2][0:r, 0:w]), pt_ev[v % 2], v // 2 + 1)
                    if v >= 1 and v_units[v - 1][0] == L and last_v[L, v_units[v - 1][1]] == v - 1 \
                            and v_units[v - 1][3][0][0] == "dif":
                        rsqrt(DH)
                    for tile in forget:
                        next(tile, None)
                    if r_ < len(schedule[L][1]):
                        for name in schedule[L][1][r_]:
                            tile_done(name)
                            if name[0] == "hf":
                                next(forget[-1])
                    if L == 2 and r_ in HG_EARLY:
                        exponentials(HG_EARLY.index(r_))

            def exponentials(c):
                t = slice(c * P, c * P + P)
                act.wait_ge(y_s, c + 1)
                link(act.activation(Y[c % 2], Y[c % 2], ACT.Exp))
                link(act.activation(kb[c % 2], kb[c % 2], ACT.Exp))
                link(act.activation(qb[c % 2], a2["b"][:, :, t], ACT.Exp))
                if c >= 2:
                    act.wait_ge(pr_free[bank_of[prn["st", c - 2]]], nth[prn["st", c - 2]])
                give(act.activation(dec[c % 2], a2["b"][:, :, c * P + P - 1:c * P + P], ACT.Exp), ye_s, c + 1)

            def output_tile(i):
                drained(act, ("y", 2, i, 1))
                yb = ybuf2[:, i % 2, :]
                say(act.activation(tok[:, i, :], yb, ACT.Copy, accum_out=ss[:, 0:1]), sq_s, "sq_s")
                hear(mean_s, "mean_s")
                say(act.activation(tok[:, i, :], yb, ACT.Square, bias=lam[:, 7:8], accum_out=ss[:, 0:1]), sq_s, "sq_s")
                rsqrt()

            def out_proj(L):
                for i in range(T):
                    b = take(act, ("mT", L, i, 0))
                    release(copy(hT[:, 0:4, i * P:i * P + P], heads(b[:, :])), ("mT", L, i, 0))
                for i in range(T):
                    drained(act, ("y", L, i, 1))
                    say(act.activation(tok[:, i, :], ybuf[:, i % 2, :], ACT.Square,
                                       accum_out=ss[:, 0:1]), sq_s, "sq_s")
                    rsqrt()
                    if L == 0:
                        rsqrt()

            nc.scalar.preload_act_table_set("natural_log_exp_and_others")
            act.dma_start(ident[:, :], C["ident"]).then_inc(v_in, 16)
            at = 0
            for src in (A["c"], A["b_ada"][0:1, 0:2 * D], A["b_ada"][1:2, 0:2 * D], A["g_pre"],
                        A["ev_q_norm"], A["ev_kv_norm"], A["cmp_pos_2"][0]):
                n = int(np.prod(src.shape)) // P
                act.dma_start(vrows[at:at + n, :], bass.AP(src.tensor, src.offset, [[P, n], [1, P]])).then_inc(v_in, 16)
                at += n
            act.dma_start(x[:, :, :], A["x"][0].rearrange("(i p) d -> p i d", p=P)).then_inc(x_in, 16)
            for dst, name in ((cosh_, "cos_head"), (sinh_, "sin_head"), (cosl, "cos_lat"), (sinl, "sin_lat")):
                act.dma_start(dst[:, :, :], C[name].rearrange("(i p) d -> p i d", p=P)).then_inc(c_in, 16)
            act.dma_start(causal[:, :], C["causal"]).then_inc(c_in, 16)
            act.dma_start(window[:, :], C["window"]).then_inc(c_in, 16)
            act.dma_start(sink[:, 0, :], rows(A["ev_sinks"], NH)).then_inc(c_in, 16)
            act.dma_start(lamr[:, :, :], bass.AP(A["od_lambda"].tensor, 0, [[0, P], [64, 4], [1, 64]])).then_inc(c_in, 16)
            act.dma_start(subln[:, :], rows(A["od_subln"], 2 * MN)).then_inc(c_in, 16)
            act.dma_start(fbias[:, :], A["od_forget_bias"].rearrange("o h -> h o"),
                          allow_slow_non_contiguous=True).then_inc(c_in, 16)

            act.wait_ge(exp_b, 1)
            say(act.activation(cond[:, :], cond[:, :], ACT.Exp, scale=-1.0), exp_c, "exp_c")
            rsqrt(T)
            hT_even(0)
            for i in range(T):
                token_square(("cq", i), QL)
            for i in range(T):
                token_square(("ckv", i), KVL)
            for name, nk, dst, g in (("cqT", 3, a0["cqT"], qn), ("ckvT", 2, a0["ckvT"], kvn)):
                for i in range(T):
                    b = take(act, (name, i))
                    for k in range(nk):
                        ins = act.activation(dst[:, k, i * P:i * P + P], b[:, k * P:k * P + P], ACT.Copy,
                                             scale=g[:, k:k + 1])
                        if k < nk - 1:
                            link(ins)
                    release(ins, (name, i))
            for i in range(T):
                for g in range(2):
                    b = take(act, ("mqT", i, g))
                    release(copy(a0["mqT"][:, 4 * g:4 * g + 4, i * P:i * P + P], heads(b[0:MQ, :])), ("mqT", i, g))
            for i in range(T):
                if i >= 2:
                    used(act, ("mkT", i - 2, 1))
                for g in range(2):
                    b = take(act, ("ukv", i, g))[:, :].rearrange("p (h d) -> p h d", h=4)
                    kt = ktok[:, i % 2, 384 * g:384 * g + 384].rearrange("p (h d) -> p h d", h=4)
                    link(copy(kt[:, :, 0:MN], b[:, :, 0:MN]))
                    link(copy(kt[:, :, MN:MQ], spread(a0["krr"][:, i, :], 4)))
                    mv = a0["mV"][:, i, 256 * g:256 * g + 256].rearrange("p (h d) -> p h d", h=4)
                    release(copy(mv, b[:, :, MN:2 * MN]), ("ukv", i, g))
            for i in range(T):
                b = take(act, ("sqT", i))
                release(copy(a0["sqT"][:, :, i * P:i * P + P], heads(b[:, :])), ("sqT", i))
            for i in range(T):
                b = take(act, ("skT", i))
                release(copy(a0["skT"][:, i * P:i * P + P], b[:, 0:P]), ("skT", i))
            tile_done(("gate0", 0, 0))
            attention(0)
            out_proj(0)

            hT_even(1)
            for n in ("dq", "dk"):
                for i in range(T):
                    b = take(act, (n + "T", i))
                    release(copy(a1[n + "T"][:, :, i * P:i * P + P], heads(b[:, :])), (n + "T", i))
            for i in range(T):
                b = take(act, ("dv", i))
                release(copy(a1["dV"][:, i, :], b[:, :]), ("dv", i))
            act.wait_ge(lam_a, 1)
            say(act.activation(lam[:, 2:4], lam[:, 0:2], ACT.Exp), lam_b, "lam_b")
            tile_done(("gate1", 0, 0))
            tile_done(("gate1", 0, 1))
            attention(1)
            act.wait_ge(ob_free, g_no[1, len(plan[1]) - 1] + 1)
            act.dma_start(onehot_r, C["onehot_r"]).then_inc(l2_in, 16)
            act.dma_start(a2["tbl"][0:32, :], A["rel_bias_2"]).then_inc(l2_in, 16)
            act.dma_start(a2["ck2"], A["w_ck2_2"][0]).then_inc(l2_in, 16)
            act.dma_start(a2["cv2"], A["w_cv2_2"][0]).then_inc(l2_in, 16)
            act.dma_start(a2["cmpok"], C["cmp_ok"].rearrange("(i p) n -> p i n", p=P)).then_inc(l2_in, 16)
            act.dma_start(causal[:, :], C["strict"]).then_inc(l2_in, 16)
            out_proj(1)

            act.wait_ge(x_s, 2 * T)
            act.dma_start(grow[:, :], C["levels"]).then_inc(hg_in, 16)
            act.dma_start(hgnorm, rows(A["hg_norm_w_2"], 384)).then_inc(hg_in, 16)
            hT_even(2)
            for n, dst in (("k", kvC["k"]), ("v", kvC["v"])):
                b = take(act, (n + "c",))
                for g in range(NG):
                    link(copy(dst[0:MN, g, :], b[MN * g:MN * g + MN, :]))
                    ins = copy(dst[MN:P, g, 0:S - 1], b[MN * g:MN * g + MN, 1:S])
                    if g == 0:
                        link(ins)
                release(ins, (n + "c",))
            b = take(act, ("ks",))
            release(copy(a2["ksT"], b[:, :]), ("ks",))
            for i in range(T):
                b = take(act, ("vs", i))
                release(copy(a2["vs"][:, i, :], b[:, 0:P]), ("vs", i))
            b = take(act, ("kw",))
            release(copy(a2["kwT"], b[:, :]), ("kw",))
            for i in range(T):
                exp_neg(("vwg", i), 18)
            for m in range(3):
                b = take(act, ("nq", m))
                release(copy(a2["nqT"][:, m, :], b[:, :], MN ** -0.5), ("nq", m))
            for _ in range(2):
                hear(ge_b, "ge_b")
                say(act.activation(d2[:, 0:NG * NC], d2[:, 0:NG * NC], ACT.Exp,
                                   scale=-2.0 * math.sqrt(2.0 / math.pi)), ge_a, "ge_a")
            tile_done(("nz", 0))
            attention(2)
            act.wait_ge(ob_free, g_no[2, len(plan[2]) - 1] + 1)
            act.dma_start(lng, rows(A["ln_g_2"], D)).then_inc(ln_in, 16)
            act.dma_start(lnb, rows(A["ln_b_2"], D)).then_inc(ln_in, 16)

            for c in range(T + 1):
                if c < T - 1:
                    b = take(act, ("kbT", c))
                    if c:
                        used(act, ("st", c - 1))
                    release(copy(kbT, b[:, 0:384]), ("kbT", c))
                if 1 <= c < T - 1:
                    exponentials(c + 1)
                if c >= 2:
                    output_tile(c - 2)
                if c:
                    b = take(act, ("mT", 2, c - 1, 0))
                    release(copy(hT[:, 0:4, (c - 1) * P:c * P], heads(b[:, :])), ("mT", 2, c - 1, 0))
                if c < T:
                    rsqrt(HGH)
            output_tile(T - 1)

        @block.gpsimd
        def _(pool):
            seen = Ticks()

            def own(ins):
                n = seen.next("pool_own")
                ins.then_inc(pool_own, 1)
                pool.wait_ge(pool_own, n)

            pool.memset(ones[:, :], 1.0).then_inc(pool_seq, 1)
            drained(pool, ("ckvT", T - 1))
            for n, (L, c) in enumerate(POOL_ADA):
                W = w_view["ada", L, c]
                pool.wait_ge(w_in[chunk_no["ada", L, c] % RING], w_val["ada", L, c])
                if n == 0:
                    used(pool, ("ukv", T - 1, 1))
                if n >= 2:
                    used(pool, ("adac",) + POOL_ADA[n - 2])
                own(pool.tensor_tensor(W, W, widen(cond[:, :], 512), ALU.mult))
                for k in (4, 2):
                    own(pool.tensor_tensor(W[:, 0:k, :], W[:, 0:k, :], W[:, k:2 * k, :], ALU.add))
                pool.tensor_tensor(pool_sums[n % 2], W[:, 0, :], W[:, 1, :], ALU.add).then_inc(acp_s, 1)
                pool.wait_ge(acp_s, n + 1)
            pool.wait_ge(pv_done, last_v[0, len(plan[0]) - 1] + 1)
            drained(pool, ("adac", 1, 3))
            pool.memset(a1["fqT"][MN:MN + 2, :, :], 1.0).then_inc(pool_seq, 1)
            pool.memset(a1["fkT"][MN:MN + 2, :, :], 1.0).then_inc(pool_seq, 1)
            pool.wait_ge(pv_done, last_v[1, len(plan[1]) - 1] + 1)
            pool.memset(a2["tbl"][32:33, :], NEG).then_inc(pool_seq, 1)

            def tt(dst, a, b, op):
                return pool.tensor_tensor(dst, a, b, op)

            def halves(v, l, off, ref=False):
                h = 1 << l
                dims = [list(d) for d in v.ap]
                return bass.AP(v.tensor, v.offset + off, [dims[0], dims[1], [2 * h, P // (2 * h)], [0 if ref else 1, h]])

            def differences(c):
                bc = a2["b"][:, :, c * P:c * P + P]
                if c >= 2:
                    pool.wait_ge(g_done, HGH * (c - 1))
                    pool.wait_ge(ho_done, HGH * (c - 1))
                for l in range(NLEV):
                    h = 1 << l
                    yl = Y[c % 2][:, l, :, :]
                    ref = halves(bc, l, h - 1, True)
                    own(tt(halves(yl, l, 0), ref, halves(bc, l, 0), ALU.subtract))
                    own(tt(halves(yl, l, h), halves(bc, l, h), ref, ALU.subtract))
                last = a2["b"][:, :, c * P + P - 1]
                tt(kb[c % 2], widen(last, P), bc, ALU.subtract).then_inc(y_s, 1)
                pool.wait_ge(y_s, c + 1)

            def operands(c):
                t = slice(c * P, c * P + P)
                pool.wait_ge(ye_s, c + 1)
                for l in range(NLEV):
                    h = 1 << l
                    yl = Y[c % 2][:, l, :, :]
                    own(tt(halves(yl, l, 0), halves(yl, l, 0), halves(a2["key"][:, :, t], l, 0), ALU.mult))
                    own(tt(halves(yl, l, h), halves(yl, l, h), halves(a2["hq"][:, :, t], l, h), ALU.mult))
                own(tt(kb[c % 2], kb[c % 2], a2["key"][:, :, t], ALU.mult))
                tt(qb[c % 2], qb[c % 2], a2["hq"][:, :, t], ALU.mult).then_inc(yr_s, 1)
                pool.wait_ge(yr_s, c + 1)

            def output_tile(i):
                pool.wait_ge(ln_s, i + 1)
                if i == 0:
                    pool.wait_ge(ln_in, 32)
                yb = ybuf2[:, i % 2, :]
                own(tt(yb, yb, lng, ALU.mult))
                tt(x[:, i, :], yb, lnb, ALU.add).then_inc(x_s, 1)
                pool.wait_ge(x_s, 2 * T + i + 1)

            nsa = [g for g, e in enumerate(plan[2]) if e[0] != "sb"][-1]
            pool.wait_ge(hgf, 3)
            pool.wait_ge(pv_done, last_v[2, nsa] + 1)
            pool.wait_ge(masked, s_no["sb", 0, 0])
            differences(0)
            drained(pool, ("hq", 2))
            operands(0)
            used(pool, ("hi", T - 1))
            differences(1)
            operands(1)
            for c in range(T + 1):
                if c + 2 < T:
                    differences(c + 2)
                if c + 2 < T:
                    operands(c + 2)
                if c >= 1:
                    output_tile(c - 1)

        @block.vector
        def _(dve):
            seen = Ticks()

            def link(ins):
                n = seen.next("dve_seq")
                ins.then_inc(dve_seq, 1)
                dve.wait_ge(dve_seq, n)

            def give(ins, s, value):
                ins.then_inc(s, 1)
                dve.wait_ge(s, value)

            def release(ins, name):
                p = prn[name]
                give(ins, pr_free[bank_of[p]], nth[p])

            def hear(s, key):
                dve.wait_ge(s, seen.next(key))

            def say(ins, s, key):
                give(ins, s, seen.next(key))

            def tt(dst, a, b, op):
                return dve.tensor_tensor(dst, a, b, op)

            def ts(dst, a, s1, op0, s2=None, op1=None):
                if op1 is None:
                    return dve.tensor_scalar(dst, a, s1, None, op0)
                return dve.tensor_scalar(dst, a, s1, s2, op0, op1)

            def stt(dst, a, s, b, op0, op1):
                return dve.scalar_tensor_tensor(out=dst, in0=a, scalar=s, in1=b, op0=op0, op1=op1)

            def rsqrt(src, n, width, eps):
                say(ts(rv[:, 0:n], src, 1.0 / width, ALU.mult, eps, ALU.add), rs_v, "rs_v")
                newton(n)

            def newton(n):
                hear(rs_e, "rs_e")
                link(tt(rt[:, 0:n], rr[:, 0:n], rr[:, 0:n], ALU.mult))
                link(tt(rt[:, 0:n], rt[:, 0:n], rv[:, 0:n], ALU.mult))
                link(ts(rt[:, 0:n], rt[:, 0:n], -0.5, ALU.mult, 1.5, ALU.add))
                link(tt(rr[:, 0:n], rr[:, 0:n], rt[:, 0:n], ALU.mult))

            def square_sum(i):
                link(dve.tensor_tensor_reduce(out=tok[:, i, :], in0=x[:, i, :], in1=x[:, i, :], scale=1.0,
                                              scalar=0.0, op0=ALU.mult, op1=ALU.add,
                                              accum_out=lam_ss[:, i:i + 1]))

            def normalise(L):
                rsqrt(lam_ss[:, 0:T], T, D, EPS)
                for i in range(T):
                    say(ts(tok[:, i, :], x[:, i, :], rr[:, i:i + 1], ALU.mult), xn_s, "xn_s")

            def normalise_tile(i):
                rsqrt(lam_ss[:, i:i + 1], 1, D, EPS)
                say(ts(tok[:, i, :], x[:, i, :], rr[:, 0:1], ALU.mult), xn_s, "xn_s")

            def modulation(L, c):
                b = take(dve, ("adac", L, c))
                if c == 0 and L:
                    drained(dve, ("hT", L - 1, KT - 1))
                release(tt(modc[:, 4 * c:4 * c + 4], b[:, 0:4], bcol[:, L, 4 * c:4 * c + 4], ALU.add),
                        ("adac", L, c))
                if c == 3:
                    say(stt(acol[:, :], modc[:, 8:16], 1.0, gpre[:, L, :], ALU.add, ALU.mult), mod_s, "mod_s")

            def hT_odd(L):
                for k in range(1, KT, 2):
                    b = take(dve, ("hT", L, k))
                    if L < 2:
                        ins = ts(hT[:, k, :], b[:, :], acol[:, k:k + 1], ALU.mult, modc[:, k:k + 1], ALU.add)
                    else:
                        ins = dve.tensor_copy(hT[:, k, :], b[:, :])
                    release(ins, ("hT", L, k))

            def rope(dst, src, nh, w, cos, sin):
                h = w // 2
                a = d1[:, 0:nh * w].rearrange("p (n w) -> p n w", n=nh)
                b = d2[:, 0:nh * w].rearrange("p (n w) -> p n w", n=nh)
                link(tt(a, src, spread(cos, nh), ALU.mult))
                link(tt(b[:, :, 0:h], src[:, :, h:w], spread(sin[:, 0:h], nh), ALU.mult))
                link(tt(b[:, :, h:w], src[:, :, 0:h], spread(sin[:, h:w], nh), ALU.mult))
                return a, b

            def norm_tile(name, i, width, dst):
                b = take(dve, name)
                hear(sq_s, "sq_s")
                rsqrt(ss[:, 0:1], 1, width, EPS)
                return b, ts(dst, b[:, 0:width], rr[:, 0:1], ALU.mult)

            gates_seen = []

            late = []
            forget = []

            def sigmoid(name, c0, n):
                b = take(dve, name)
                t = (t1, t2)[len(gates_seen) % 2]
                gates_seen.append(name)
                say(ts(t[:, 0:n], b[:, c0:c0 + n], -SIG_CLAMP, ALU.max), sil_c, "sil_c")
                return b, t

            def silu(name, c0, n, dst):
                b, t = sigmoid(name, c0, n)
                late.append((name, dst, b[:, c0:c0 + n], t[:, 0:n]))

            def finish_gates():
                for name, dst, z, t in late:
                    hear(sil_s, "sil_s")
                    release(tt(dst, z, t, ALU.mult), name)
                late.clear()

            def tile_done(name):
                kind, i = name[0], name[-1]
                if kind in ("gate0", "gate1"):
                    silu(name, 0, 512, tok[:, i, 512 * name[1]:512 * name[1] + 512])
                elif kind == "adac":
                    modulation(name[1], name[2])
                elif kind == "adag":
                    L, c = name[1:]
                    b = take(dve, name)
                    if c == 0:
                        dve.wait_ge(row_in, 32 * (L + 1))
                    w = slice(512 * c, 512 * c + 512)
                    link(tt(d1[:, :], b[:, :], bgate[:, w], ALU.add))
                    release(tt(grows[L][:, w], d1[:, :], gpost[:, w], ALU.mult), name)
                elif kind == "ff":
                    b = take(dve, name)
                    link(ts(d1[0:NH, :], b[0:NH, :], fbias[:, 0:1], ALU.add))
                    say(stt(d2[0:NH, :], d1[0:NH, :], -1.0, d1[0:NH, :], ALU.mult, ALU.min), ff_b, "ff_b")
                    hear(ff_a, "ff_a")
                    link(stt(d3[0:NH, :], d1[0:NH, :], 0.0, d2[0:NH, :], ALU.min, ALU.subtract))
                    release(dve.tensor_tensor_scan(frow, d3[0:NH, :], d3[0:NH, :], 0.0, ALU.add, ALU.bypass), name)
                    say(ts(nfrow, frow, -1.0, ALU.mult), frow_s, "frow_s")
                elif kind == "fk":
                    b = take(dve, name)
                    link(dve.tensor_copy(a1["fkT"][0:MN, 2 * i, :], b[0:MN, :]))
                    release(dve.tensor_copy(a1["fkT"][0:MN, 2 * i + 1, :], b[MN:P, :]), name)
                elif kind == "fv":
                    b = take(dve, name)
                    release(dve.tensor_copy(a1["fV"][:, i, :], b[:, :]), name)
                elif kind == "nz":
                    silu(name, 0, 384, tok[:, i, 0:384])
                elif kind == "sbvz":
                    b = take(dve, name)
                    link(dve.tensor_copy(a2["sbv"][:, i, :], b[:, 0:256]))
                    silu(name, 256, 256, tok[:, i, 384:640])
                elif kind == "hi":
                    b = take(dve, name)
                    release(dve.tensor_copy(a2["hi"][:, i, :], b[:, 0:384]), name)
                elif kind == "hz":
                    silu(name, 0, 384, tok[:, i, 640:1024])
                elif kind == "hf":
                    forget.append(forget_tile(i))
                    next(forget[-1])

            def forget_tile(m):
                f, key, u, v = a2["hq"][:, m, :], a2["key"][:, m, :], a2["b"][:, m, :], a2["hgt"][:, 0:S]
                yield
                drained(dve, ("hf", m))
                link(ts(key, f, CLAMP, ALU.min))
                say(stt(u, f, -1.0, f, ALU.mult, ALU.min), hg_b, "hg_b")
                yield
                hear(hg_a, "hg_a")
                link(ts(key, key, 1.0, ALU.add))
                link(dve.reciprocal(key, key))
                link(stt(v, f, 0.0, u, ALU.min, ALU.subtract))
                link(ts(d3[:, :], v, -1.0, ALU.mult, LOG_FLOOR, ALU.add))
                say(stt(u, v, LOG_FLOOR, d3[:, :], ALU.subtract, ALU.min), hg_b, "hg_b")
                yield
                hear(hg_a, "hg_a")
                link(stt(d3[:, :], v, LOG_FLOOR, u, ALU.max, ALU.add))
                for c in range(T):
                    t = slice(c * P, c * P + P)
                    ins = dve.tensor_tensor_scan(a2["b"][:, m, t], d3[:, t], d3[:, t], 0.0, ALU.add, ALU.bypass)
                    if c < T - 1:
                        link(ins)
                give(ins, hgf, m + 1)

            late_group = []

            def finish_group(L, g, part=0):
                kind, i, vus = plan[L][g]
                no = g_no[L, g]
                dve.wait_ge(pv_done, last_v[L, g] + 1)
                ob, row = OB[no % 2], no % 16
                if kind in ("mla", "swa", "fox"):
                    den = rsum[:, row, :]
                    if kind == "swa":
                        link(tt(fr[:, 0:NH], den, esink[:, row, :], ALU.add))
                        den = fr[:, 0:NH]
                    link(dve.reciprocal(fr[:, 0:NH], den))
                    o = d1[:, :].rearrange("p (h d) -> p h d", h=NH)
                    link(tt(o, ob[:, :].rearrange("p (h d) -> p h d", h=NH), widen(fr[:, 0:NH], MN), ALU.mult))
                    dst = tok[:, i, 0:512] if kind == "mla" else tok[:, i, 512:1024]
                    give(tt(dst, dst, d1[:, :], ALU.mult), ob_free, no + 1)
                elif kind == "dif" and part == 0:
                    link(dve.reciprocal(fr[:, 0:DH], rsum[:, row, 0:NH:2]))
                    o = d1[:, :].rearrange("p (h d) -> p h d", h=DH)
                    q = d2[:, :].rearrange("p (h d) -> p h d", h=DH)
                    link(tt(o, ob[:, :].rearrange("p (h d) -> p h d", h=DH), widen(fr[:, 0:DH], 2 * MN), ALU.mult))
                    link(tt(d2[:, :], d1[:, :], d1[:, :], ALU.mult))
                    link(dve.tensor_reduce(fr[:, 4:8], q, AX.X, ALU.add))
                    say(ts(rv[:, 0:DH], fr[:, 4:8], 1.0 / (2 * MN), ALU.mult, EPS, ALU.add), rs_v, "rs_v")
                    late_group.append((L, g))
                elif kind == "dif":
                    newton(DH)
                    o = d1[:, :].rearrange("p (h d) -> p h d", h=DH)
                    link(tt(o, o, widen(rr[:, 0:DH], 2 * MN), ALU.mult))
                    link(tt(o, o, spread(subln[:, :], DH), ALU.mult))
                    dst = tok[:, i, 0:512]
                    give(tt(dst, dst, d1[:, :], ALU.mult), ob_free, no + 1)
                elif kind == "sb":
                    dst = tok[:, i, 384:640]
                    give(tt(dst, dst, ob[:, 0:256], ALU.mult), ob_free, no + 1)
                else:
                    br = ("cmp", "sel", "win").index(kind)
                    link(dve.reciprocal(fr[:, 0:NSH], rsum[:, row, 0:NSH]))
                    gate = a2["gates"][:, i, br:18:3]
                    link(tt(fr[:, 0:NSH], fr[:, 0:NSH], gate, ALU.mult))
                    o3 = ob[:, 0:384].rearrange("p (h d) -> p h d", h=NSH)
                    if br == 0:
                        give(tt(acc.rearrange("p (h d) -> p h d", h=NSH), o3, widen(fr[:, 0:NSH], MN), ALU.mult), ob_free, no + 1)
                    else:
                        o = d2[:, 0:384].rearrange("p (h d) -> p h d", h=NSH)
                        link(tt(o, o3, widen(fr[:, 0:NSH], MN), ALU.mult))
                        if br == 1:
                            give(tt(acc, acc, d2[:, 0:384], ALU.add), ob_free, no + 1)
                        else:
                            link(tt(acc, acc, d2[:, 0:384], ALU.add))
                            dst = tok[:, i, 0:384]
                            give(tt(dst, dst, acc, ALU.mult), ob_free, no + 1)

            def attention(L):
                pending = []

                def stick_tail():
                    if pending:
                        s = pending.pop()
                        n = score_operands(s_units[s][2])[4]
                        z, l = zm[:, s % 2, 0:n], (t1, t2)[s % 2][:, 0:n]
                        hear(sb_l, "sb_l")
                        link(stt(d1[:, 0:n], z, 0.0, l, ALU.max, ALU.add))
                        link(dve.tensor_tensor_scan(d2[:, 0:n][:, ::-1], d1[:, 0:n][:, ::-1],
                                                    d1[:, 0:n][:, ::-1], 0.0, ALU.add, ALU.bypass))
                        say(stt(z, d2[:, 0:n], -1.0, z, ALU.mult, ALU.add), sb_a, "sb_a")

                for r_, (v, (_, g, j, sus), new) in enumerate(steps(L)):
                    for s in new:
                        _, sg, su, _ = s_units[s]
                        _, _, mask, scale, n = score_operands(su)
                        row, c = g_no[L, sg] % 16, su[1]
                        if su[0] != "sb":
                            stick_tail()
                        dve.wait_ge(s_done, s + 1)
                        if s >= 2:
                            dve.wait_ge(p_done, s - 1)
                        z = zm[:, s % 2, 0:n]
                        if su[0] == "sb":
                            give(tt(z, SC[s % 2][:, 0:n], mask, ALU.add), masked, s + 1)
                            stick_tail()
                            pending.append(s)
                            continue
                        start = sink[:, 1, c:c + 1] if su[0] == "swa" else 3.0e38
                        give(dve.tensor_tensor_reduce(out=z, in0=SC[s % 2][:, 0:n], in1=mask, scale=-scale,
                                                      scalar=start, op0=ALU.add, op1=ALU.min,
                                                      accum_out=nmax[:, row, c:c + 1]), masked, s + 1)
                    if s_units[-1][0] == L and s_no[sus[-1]] + LOOK >= len(s_units) - 1:
                        stick_tail()
                    s = s_no[sus[-1]]
                    n = score_operands(sus[-1])[4]
                    row = g_no[L, g] % 16
                    if sus[-1][0] == "dif":
                        c = sus[0][1]
                        dve.wait_ge(p_done, s + 1)
                        link(dve.reciprocal(fr[:, 8:9], rsum[:, row, c + 1:c + 2]))
                        link(stt(fr[:, 8:9], fr[:, 8:9], rsum[:, row, c:c + 1], lam[:, 5:6], ALU.mult, ALU.mult))
                        give(stt(pb[:, s % NP, 0:n], pb[:, s % NP, 0:n], fr[:, 8:9], pb[:, (s - 1) % NP, 0:n],
                                 ALU.mult, ALU.add), post, post_no[v] + 1)
                    if sus[-1][0] == "cmp":
                        dve.wait_ge(p_done, s + 1)
                        give(tt(pb[:, s % NP, 0:n], pb[:, s % NP, 0:n], a2["cmpok"][:, plan[L][g][1], 0:n], ALU.mult),
                             post, post_no[v] + 1)
                    if late_group:
                        finish_group(*late_group.pop(), part=1)
                    if v >= 1 and v_units[v - 1][0] == L and last_v[L, v_units[v - 1][1]] == v - 1:
                        finish_group(L, v_units[v - 1][1])
                    for tile in forget:
                        next(tile, None)
                    finish_gates()
                    if r_ < len(schedule[L][1]):
                        for name in schedule[L][1][r_]:
                            tile_done(name)
                finish_group(L, len(plan[L]) - 1)

            def out_proj(L):
                for i in range(T):
                    b = take(dve, ("mT", L, i, 1))
                    release(dve.tensor_copy(hT[:, 4:8, i * P:i * P + P], b[:, :].rearrange("p (j t) -> p j t", j=4)),
                            ("mT", L, i, 1))
                for i in range(T):
                    yb = ybuf[:, i % 2, :]
                    for h in range(2):
                        b = take(dve, ("y", L, i, h))
                        w = slice(512 * h, 512 * h + 512)
                        ins = dve.tensor_copy(yb[:, w], b[:, :])
                        release(ins, ("y", L, i, h))
                    hear(sq_s, "sq_s")
                    rsqrt(ss[:, 0:1], 1, D, EPS)
                    link(stt(yb, yb, rr[:, 0:1], grows[L][:, :], ALU.mult, ALU.mult))
                    say(tt(x[:, i, :], x[:, i, :], yb, ALU.add), x_s, "x_s")
                    if L == 0:
                        square_sum(i)
                        normalise_tile(i)

            b = take(dve, ("cols",))
            release(dve.tensor_copy(cols[:, :], b[:, 0:77]), ("cols",))
            say(ts(cond[:, :], cT[:, :], -CLAMP, ALU.max), exp_b, "exp_b")
            hear(exp_c, "exp_c")
            link(ts(cond[:, :], cond[:, :], 1.0, ALU.add))
            link(dve.reciprocal(cond[:, :], cond[:, :]))
            say(tt(cond[:, :], cT[:, :], cond[:, :], ALU.mult), cond_s, "cond_s")
            for c in range(5):
                if c < 4:
                    W = w_view["ada", 0, c]
                    dve.wait_ge(w_in[chunk_no["ada", 0, c] % RING], w_val["ada", 0, c])
                    t = (d1, d2)[c % 2][:, :]
                    link(ts(t, W[:, 0, :], cond[:, 0:1], ALU.mult))
                    for k in range(1, KT):
                        ins = stt(t, W[:, k, :], cond[:, k:k + 1], t, ALU.mult, ALU.add)
                        if k < KT - 1:
                            link(ins)
                    say(ins, acc_s, "acc_s")
                if c >= 1:
                    modulation(0, c - 1)
                if c == 2:
                    dve.wait_ge(x_in, 16)
                if c in (2, 3):
                    square_sum(2 * c - 4)
                    square_sum(2 * c - 3)
                if c == 3:
                    normalise(0)
            dve.wait_ge(c_in, 16 * N_C)
            link(ts(sink[:, 1, :], sink[:, 0, :], -1.0, ALU.mult))
            for n in range(2):
                ins = dve.tensor_tensor_reduce(out=lamr[:, 2 * n, :], in0=lamr[:, 2 * n, :], in1=lamr[:, 2 * n + 1, :],
                                               scale=1.0, scalar=0.0, op0=ALU.mult, op1=ALU.add,
                                               accum_out=lam[:, n:n + 1])
                if n == 0:
                    link(ins)
                else:
                    say(ins, lam_a, "lam_a")
            link(ts(subln[:, :], subln[:, :], 1.0 - LAM_INIT, ALU.mult))
            hT_odd(0)
            for i in range(T):
                _, ins = norm_tile(("cq", i), i, QL, cqn[:, i, :])
                release(ins, ("cq", i))
            for i in range(T):
                b, ins = norm_tile(("ckv", i), i, KVL, ckvn[:, i, :])
                link(ins)
                kr = b[:, KVL:KVL + RD].rearrange("p (n w) -> p n w", n=1)
                u, w = rope(None, kr, 1, RD, cosl[:, i, :], sinl[:, i, :])
                release(tt(a0["krr"][:, i:i + 1, :], u, w, ALU.add), ("ckv", i))
            for i in range(T):
                if i >= 2:
                    used(dve, ("mqT", i - 2, 1))
                for g in range(2):
                    b = take(dve, ("uq", i, g))[:, 0:384].rearrange("p (h w) -> p h w", h=4)
                    qt = qtok[:, i % 2, 384 * g:384 * g + 384].rearrange("p (h w) -> p h w", h=4)
                    link(dve.tensor_copy(qt[:, :, 0:MN], b[:, :, 0:MN]))
                    u, w = rope(None, b[:, :, MN:MQ], 4, RD, cosl[:, i, :], sinl[:, i, :])
                    release(tt(qt[:, :, MN:MQ], u, w, ALU.add), ("uq", i, g))
            for i in range(T):
                for g in range(2):
                    b = take(dve, ("mkT", i, g))
                    release(dve.tensor_copy(a0["mkT"][:, 4 * g:4 * g + 4, i * P:i * P + P],
                                            b[0:MQ, :].rearrange("p (j t) -> p j t", j=4)), ("mkT", i, g))
            for i in range(T):
                if i >= 2:
                    used(dve, ("sqT", i - 2))
                b = take(dve, ("sq", i))[:, :].rearrange("p (n w) -> p n w", n=NH)
                u, w = rope(None, b, NH, MN, cosh_[:, i, :], sinh_[:, i, :])
                dst = rtok[:, i % 2, :].rearrange("p (j v d) -> p v j d", j=4, v=2)
                four = lambda z: z.rearrange("p (v j) d -> p v j d", v=2)
                for kv in range(2):
                    ins = tt(dst[:, kv, :, :], four(u)[:, kv, :, :], four(w)[:, kv, :, :], ALU.add)
                    if kv == 0:
                        link(ins)
                release(ins, ("sq", i))
            for i in range(T):
                if i >= 2:
                    used(dve, ("skT", i - 2))
                b = take(dve, ("skv", i))
                link(dve.tensor_copy(a0["sV"][:, i, :], b[:, P:2 * P]))
                u, w = rope(None, b[:, 0:P].rearrange("p (n w) -> p n w", n=2), 2, MN, cosh_[:, i, :], sinh_[:, i, :])
                release(tt(rktok[:, i % 2, :].rearrange("p (n w) -> p n w", n=2), u, w, ALU.add), ("skv", i))
            tile_done(("gate0", 0, 0))
            finish_gates()
            attention(0)
            out_proj(0)
            hT_odd(1)
            for n in ("dq", "dk"):
                for i in range(T):
                    if i >= 2:
                        used(dve, (n + "T", i - 2))
                    b = take(dve, (n, i))[:, :].rearrange("p (n w) -> p n w", n=NH)
                    if n == "dk" and i < 2:
                        used(dve, ("dqT", i + 2))
                    u, w = rope(None, b, NH, MN, cosh_[:, i, :], sinh_[:, i, :])
                    release(tt(rtok[:, i % 2, :].rearrange("p (n w) -> p n w", n=NH), u, w, ALU.add), (n, i))
            hear(lam_b, "lam_b")
            link(tt(lam[:, 4:5], lam[:, 3:4], lam[:, 2:3], ALU.subtract))
            link(ts(lam[:, 5:6], lam[:, 4:5], -LAM_INIT, ALU.add))
            tile_done(("gate1", 0, 0))
            finish_gates()
            tile_done(("gate1", 0, 1))
            finish_gates()
            attention(1)
            out_proj(1)
            hT_odd(2)
            for r in range(2):
                b = take(dve, ("relrow", r))
                release(dve.tensor_copy(relrow[:, 320 * r:320 * r + 320], b[0:NSH, 0:320]), ("relrow", r))
            dve.wait_ge(l2_in, 16 * N_L2)
            say(ts(rt[:, 0:1], rt[:, 0:1], 1.0, ALU.mult), relr_s, "relr_s")

            def blocks(n):
                for g in range(NG):
                    src = kvC[n][:, g, 0:S]
                    src = bass.AP(src.tensor, src.offset, [list(src.ap[0]), [2, 16], [CS, NC]])
                    ins = tt(blk[n][:, :, g * NC:g * NC + NC], src, widen(pos2, NC), ALU.add)
                    if g == 0:
                        link(ins)
                say(ins, blk_s, "blk_s")

            drained(dve, ("vc",))
            blocks("k")
            blocks("v")
            for i in range(T):
                b, t = sigmoid(("vwg", i), P, 18)
                hear(sil_s, "sil_s")
                link(dve.tensor_copy(a2["gates"][:, i, :], t[:, 0:18]))
                release(dve.tensor_copy(a2["vw"][:, i, :], b[:, 0:P]), ("vwg", i))
            n = NG * NC
            for name, dst in (("ckh", a2["hk"]), ("cvh", a2["hv"])):
                b = take(dve, (name,))
                link(dve.tensor_copy(d1[:, 0:n], b[:, 0:n]))
                link(tt(d2[:, 0:n], d1[:, 0:n], d1[:, 0:n], ALU.mult))
                link(ts(d2[:, 0:n], d2[:, 0:n], 0.044715, ALU.mult, 1.0, ALU.add))
                link(tt(d2[:, 0:n], d2[:, 0:n], d1[:, 0:n], ALU.mult))
                say(ts(d2[:, 0:n], d2[:, 0:n], -CLAMP / 2, ALU.max), ge_b, "ge_b")
                hear(ge_a, "ge_a")
                link(ts(d2[:, 0:n], d2[:, 0:n], 1.0, ALU.add))
                link(dve.reciprocal(d2[:, 0:n], d2[:, 0:n]))
                release(tt(dst, d1[:, 0:n], d2[:, 0:n], ALU.mult), (name,))
            b = take(dve, ("kcT",))
            link(dve.tensor_copy(a2["kcT"][0:MN, :], b[0:MN, 0:NC]))
            release(dve.tensor_copy(a2["kcT"][MN:P, :], b[0:MN, NC:2 * NC]), ("kcT",))
            for g in range(NG):
                b = take(dve, ("vcT", g))
                release(dve.tensor_copy(a2["vc"][:, g, :], b[0:NC, 0:MN]), ("vcT", g))
            tile_done(("nz", 0))
            finish_gates()
            attention(2)

            GB = [SC, PT]
            dve.wait_ge(hg_in, 32)
            link(dve.memset(state, 0.0))

            def output_tile(i):
                yb = ybuf2[:, i % 2, :]
                hear(sq_s, "sq_s")
                say(ts(lam[:, 7:8], ss[:, 0:1], -1.0 / D, ALU.mult), mean_s, "mean_s")
                hear(sq_s, "sq_s")
                rsqrt(ss[:, 0:1], 1, D, LN_EPS)
                give(ts(yb, yb, lam[:, 7:8], ALU.add, rr[:, 0:1], ALU.mult), ln_s, i + 1)

            def mixed_half(i):
                b = take(dve, ("mT", 2, i, 1))
                release(dve.tensor_copy(hT[:, 4:8, i * P:i * P + P], b[:, :].rearrange("p (j t) -> p j t", j=4)),
                        ("mT", 2, i, 1))

            def residual_half(i, h):
                w = slice(512 * h, 512 * h + 512)
                if i >= 2 and h == 0:
                    dve.wait_ge(x_s, 2 * T + i - 1)
                b = take(dve, ("y", 2, i, h))
                release(stt(ybuf2[:, i % 2, w], x[:, i, w], ALPHA, b[:, :], ALU.mult, ALU.add), ("y", 2, i, h))

            for c in range(T):
                for h in range(HGH):
                    n = c * HGH + h
                    dve.wait_ge(g_done, n + 1)
                    for r in range(2):
                        ins = tt(gm[0][:, 4 * r:4 * r + 4, :],
                                 GB[n % 2][r][:, :].rearrange("p (l t) -> p l t", l=4),
                                 levels[:, 4 * r:4 * r + 4, :], ALU.mult)
                        if r == 0:
                            link(ins)
                    give(ins, gm_s, n + 1)
                    if n >= 2:
                        dve.wait_ge(ho_done, n - 1)
                    give(dve.tensor_reduce(gsum[n % 2], gm[0].rearrange("p l t -> p t l"), AX.X, ALU.add), gs_s, n + 1)
                    if c >= 2 and h == 1:
                        output_tile(c - 2)
                    if c and h == 2:
                        mixed_half(c - 1)
                    if c and h == 4:
                        residual_half(c - 1, 0)
                dve.wait_ge(ho_done, HGH * (c + 1))
                ob = OB[c % 2]
                link(dve.tensor_copy(d1[:, 0:384], ob[:, 0:384]))
                link(tt(d2[:, 0:384], d1[:, 0:384], d1[:, 0:384], ALU.mult))
                link(dve.tensor_reduce(fr[:, 0:HGH], d2[:, 0:384].rearrange("p (h d) -> p h d", h=HGH), AX.X, ALU.add))
                rsqrt(fr[:, 0:HGH], HGH, MN, EPS)
                o = d1[:, 0:384].rearrange("p (h d) -> p h d", h=HGH)
                link(tt(o, o, widen(rr[:, 0:HGH], MN), ALU.mult))
                link(tt(d1[:, 0:384], d1[:, 0:384], hgnorm, ALU.mult))
                dst = tok[:, c, 640:1024]
                give(tt(dst, dst, d1[:, 0:384], ALU.mult), hof, c + 1)
                if c:
                    residual_half(c - 1, 1)
                if c < T - 1:
                    b = take(dve, ("st", c))
                    for m in range(3):
                        for r in range(2):
                            q = slice(MN * r, MN * r + MN)
                            src = b[q, m * P + MN * r:m * P + MN * r + MN]
                            dst = state[q, m, MN * r:MN * r + MN]
                            if c == 0:
                                ins = dve.tensor_copy(dst, src)
                            else:
                                ins = stt(dst, dst, dec[c % 2][q, m:m + 1], src,
                                          ALU.mult, ALU.add)
                            if (m, r) != (2, 1):
                                link(ins)
                    release(ins, ("st", c))
            output_tile(T - 2)
            mixed_half(T - 1)
            residual_half(T - 1, 0)
            residual_half(T - 1, 1)
            output_tile(T - 1)


class Ticks:

    def __init__(self):
        self.n = {}

    def next(self, key):
        self.n[key] = self.n.get(key, 0) + 1
        return self.n[key]


def spread(v, n):
    dims = [list(d) for d in v.ap]
    return bass.AP(v.tensor, v.offset, [dims[0], [0, n]] + dims[1:])


def widen(v, n):
    return bass.AP(v.tensor, v.offset, [list(d) for d in v.ap] + [[0, n]])


def blocks_seen(i):
    return ((i + 1) * P - CB) // CS + 1


def transposed_shape(su):
    kind, _, i = su
    if kind == "cmp":
        return blocks_seen(i), P
    if kind == "swa":
        return P, P * (2 if i else 1)
    return P, P * (i + 1)


N_V = 8
N_C = 10
N_L2 = 6


def kernel(**inputs):
    import concourse.bacc as bacc
    from concourse.bass_utils import run_bass_kernel_spmd

    nc = bacc.Bacc("TRN2", target_bir_lowering=False, num_devices=1)
    arrays, A, C = {}, {}, {}
    for name, a in inputs.items():
        a = np.ascontiguousarray(a)
        arrays[f"in_{name}"] = a
        A[name] = nc.dram_tensor(f"in_{name}", a.shape, mybir.dt.from_np(a.dtype), kind="ExternalInput").ap()
    for name, a in constants().items():
        arrays[f"const_{name}"] = a
        C[name] = nc.dram_tensor(f"const_{name}", a.shape, F32, kind="ExternalInput").ap()
    out = nc.dram_tensor("out_0", (1, S, D), F32, kind="ExternalOutput").ap()
    two_block_kernel(nc, A, C, out)
    r = run_bass_kernel_spmd(nc, [arrays], core_ids=[0])
    return r.results[0]["out_0"]
```
